# Optimizing a Trainium2 kernel written in Bass

```python
import jax, jax.numpy as jnp
from jax import lax
import numpy as np

D_MODEL = 1024
BATCH = 1
SEQ = 256
DEPTH = 1

D_MIX = D_MODEL
D_ATTN = D_MIX // 2
HEAD_DIM_ATTN = 64
N_HEADS_ATTN = D_ATTN // HEAD_DIM_ATTN
D_MLSTM = D_MIX - D_ATTN
HEAD_DIM_MLSTM = 128
N_HEADS_MLSTM = D_MLSTM // HEAD_DIM_MLSTM
IN_SPLITS = (D_ATTN, 2 * D_ATTN, 3 * D_ATTN, 3 * D_ATTN + D_MLSTM, 3 * D_ATTN + 2 * D_MLSTM,
             3 * D_ATTN + 3 * D_MLSTM, 3 * D_ATTN + 3 * D_MLSTM + N_HEADS_MLSTM)
D_IN = 3 * D_ATTN + 3 * D_MLSTM + 2 * N_HEADS_MLSTM
DILATED_BRANCHES = ((128, 1), (512, 4), (2048, 16))
MAX_WINDOW = 2048
Q_BLOCK = 128
CONV_K = 4
MLSTM_CHUNK = 64
N_EXPERTS = 32
TOP_K = 4
D_FF = D_MODEL
SWIGLU_LIMIT = 7.0
SWIGLU_ALPHA = 1.702
EXPERT_BLOCK = 128
EPS = 1e-6

kernel_name = 'hybrid_dilated_attn_mlstm_moe'

def rmsnorm(x, g):
    xf = x.astype(jnp.float32)
    y = xf * lax.rsqrt(jnp.mean(xf * xf, axis=-1, keepdims=True) + EPS)
    return (y * g.astype(jnp.float32)).astype(x.dtype)

def alibi_slopes(n):
    return jnp.exp2(-8.0 * jnp.arange(1, n + 1, dtype=jnp.float32) / n)

def dilated_sliding_attention(q, k, v, slopes):
    B, H, S, Dh = q.shape
    pad = ((0, 0), (0, 0), (MAX_WINDOW, 0), (0, 0))
    k_pad = jnp.pad(k, pad)
    v_pad = jnp.pad(v, pad)
    n_blocks = S // Q_BLOCK

    def query_block(blk):
        t0 = blk * Q_BLOCK
        qb = lax.dynamic_slice_in_dim(q, t0, Q_BLOCK, axis=2)
        pos = t0 + jnp.arange(Q_BLOCK)
        outs, lses = [], []
        for window, dil in DILATED_BRANCHES:
            dist = dil * jnp.arange(window // dil + 1)
            kpos = pos[:, None] - dist[None, :]
            idx = (kpos + MAX_WINDOW).reshape(-1)
            kg = jnp.take(k_pad, idx, axis=2).reshape(B, H, Q_BLOCK, -1, Dh)
            vg = jnp.take(v_pad, idx, axis=2).reshape(B, H, Q_BLOCK, -1, Dh)
            s = jnp.einsum('bhqd,bhqnd->bhqn', qb, kg).astype(jnp.float32)
            s = s - slopes[:, None, None] * dist.astype(jnp.float32)
            s = jnp.where(kpos >= 0, s, -jnp.inf)
            m = jnp.max(s, axis=-1, keepdims=True)
            p = jnp.exp(s - m)
            denom = jnp.sum(p, axis=-1)
            o = jnp.einsum('bhqn,bhqnd->bhqd', p, vg.astype(jnp.float32)) / denom[..., None]
            outs.append(o)
            lses.append(m[..., 0] + jnp.log(denom))
        w = jax.nn.softmax(jnp.stack(lses), axis=0)
        return jnp.einsum('rbhq,rbhqd->bhqd', w, jnp.stack(outs))

    o = lax.map(query_block, jnp.arange(n_blocks))
    return jnp.moveaxis(o, 0, 2).reshape(B, H, S, Dh).astype(q.dtype)

def mlstm_chunkwise(q, k, v, i_pre, f_pre):
    B, NH, S, DH = q.shape
    L = MLSTM_CHUNK
    nc = S // L

    def chunks(t):
        return jnp.moveaxis(t.astype(jnp.float32).reshape(B, NH, nc, L, *t.shape[3:]), 2, 0)

    log_f = jax.nn.log_sigmoid(f_pre.astype(jnp.float32))
    causal = jnp.tril(jnp.ones((L, L), dtype=bool))

    def step(carry, inp):
        C, n, m = carry
        qc, kc, vc, ic, lfc = inp
        b = jnp.cumsum(lfc, axis=-1)
        log_d = jnp.where(causal, b[..., :, None] - b[..., None, :] + ic[..., None, :], -jnp.inf)
        log_inter = b + m[..., None]
        m_t = jnp.maximum(log_inter, jnp.max(log_d, axis=-1))
        d = jnp.exp(log_d - m_t[..., None])
        inter = jnp.exp(log_inter - m_t)
        s = jnp.einsum('bhtd,bhsd->bhts', qc, kc) * d
        num = jnp.einsum('bhts,bhse->bhte', s, vc) + inter[..., None] * jnp.einsum('bhtd,bhde->bhte', qc, C)
        den = jnp.sum(s, axis=-1) + inter * jnp.einsum('bhtd,bhd->bht', qc, n)
        h = num / jnp.maximum(jnp.abs(den), jnp.exp(-m_t))[..., None]
        b_last = b[..., -1]
        log_w = b_last[..., None] - b + ic
        m_new = jnp.maximum(b_last + m, jnp.max(log_w, axis=-1))
        w = jnp.exp(log_w - m_new[..., None])
        decay = jnp.exp(b_last + m - m_new)
        C_new = decay[..., None, None] * C + jnp.einsum('bhs,bhsd,bhse->bhde', w, kc, vc)
        n_new = decay[..., None] * n + jnp.einsum('bhs,bhsd->bhd', w, kc)
        return (C_new, n_new, m_new), h

    init = (jnp.zeros((B, NH, DH, DH), jnp.float32), jnp.zeros((B, NH, DH), jnp.float32),
            jnp.zeros((B, NH), jnp.float32))
    _, hs = lax.scan(step, init, (chunks(q), chunks(k), chunks(v), chunks(i_pre), chunks(log_f)))
    return jnp.moveaxis(hs, 0, 2).reshape(B, NH, S, DH)

def moe_ffn(h, w_router, b_router, w_gate_up, b_gate_up, w_down, b_down):
    B, S, D = h.shape
    T = B * S
    A = T * TOP_K
    xf = h.reshape(T, D)
    logits = jnp.dot(xf, w_router).astype(jnp.float32) + b_router.astype(jnp.float32)
    top_v, top_e = lax.top_k(logits, TOP_K)
    gates = jax.nn.softmax(top_v, axis=-1)
    flat_e = top_e.reshape(A)
    order = jnp.argsort(flat_e).astype(jnp.int32)
    sizes = jnp.bincount(flat_e, length=N_EXPERTS)
    starts = jnp.cumsum(sizes) - sizes
    psizes = (sizes + EXPERT_BLOCK - 1) // EXPERT_BLOCK * EXPERT_BLOCK
    pends = jnp.cumsum(psizes)
    pstarts = pends - psizes
    e_sorted = flat_e[order]
    dest = pstarts[e_sorted] + (jnp.arange(A) - starts[e_sorted])
    n_blocks = -(-A // EXPERT_BLOCK) + N_EXPERTS
    n_slots = n_blocks * EXPERT_BLOCK
    slot_assign = jnp.full((n_slots,), A, jnp.int32).at[dest].set(order)
    slot_token = slot_assign // TOP_K
    slot_gate = jnp.concatenate([gates.reshape(A), jnp.zeros((1,), jnp.float32)])[slot_assign]
    block_expert = jnp.minimum(jnp.searchsorted(pends, jnp.arange(n_blocks) * EXPERT_BLOCK, side='right'),
                               N_EXPERTS - 1)
    x_ext = jnp.concatenate([xf, jnp.zeros((1, D), xf.dtype)], axis=0)

    def expert_block(args):
        tok, e = args
        xb = x_ext[tok]
        gu = jnp.dot(xb, w_gate_up[e]) + b_gate_up[e]
        gate = jnp.minimum(gu[:, :D_FF], SWIGLU_LIMIT)
        up = jnp.clip(gu[:, D_FF:], -SWIGLU_LIMIT, SWIGLU_LIMIT)
        act = gate * jax.nn.sigmoid(SWIGLU_ALPHA * gate) * (up + 1.0)
        return jnp.dot(act, w_down[e]) + b_down[e]

    ys = lax.map(expert_block, (slot_token.reshape(n_blocks, EXPERT_BLOCK), block_expert))
    ys = ys.reshape(n_slots, D) * slot_gate[:, None].astype(ys.dtype)
    out = jax.ops.segment_sum(ys, slot_token, num_segments=T + 1)[:T]
    return out.reshape(B, S, D)

def setup_inputs(seed: int = 0) -> dict:
    key = jax.random.key(seed)
    ks = jax.random.split(key, 20)

    def nrm(k, shape, scale):
        return scale * jax.random.normal(k, shape, jnp.float32)

    L = DEPTH
    return {
        'x': nrm(ks[0], (BATCH, SEQ, D_MODEL), 1.0),
        'norm1_g': 1.0 + nrm(ks[1], (L, D_MODEL), 0.1),
        'w_in': nrm(ks[2], (L, D_MODEL, D_IN), D_MODEL ** -0.5),
        'q_norm_g': 1.0 + nrm(ks[3], (L, HEAD_DIM_ATTN), 0.1),
        'k_norm_g': 1.0 + nrm(ks[4], (L, HEAD_DIM_ATTN), 0.1),
        'conv_w': nrm(ks[5], (L, CONV_K, D_MLSTM), CONV_K ** -0.5),
        'conv_b': nrm(ks[6], (L, D_MLSTM), 0.02),
        'w_mq': nrm(ks[7], (L, N_HEADS_MLSTM, HEAD_DIM_MLSTM, HEAD_DIM_MLSTM), HEAD_DIM_MLSTM ** -0.5),
        'w_mk': nrm(ks[8], (L, N_HEADS_MLSTM, HEAD_DIM_MLSTM, HEAD_DIM_MLSTM), HEAD_DIM_MLSTM ** -0.5),
        'b_igate': nrm(ks[9], (L, N_HEADS_MLSTM), 0.1),
        'b_fgate': jnp.linspace(3.0, 6.0, N_HEADS_MLSTM)[None, :] + nrm(ks[10], (L, N_HEADS_MLSTM), 0.1),
        'mh_norm_g': 1.0 + nrm(ks[11], (L, N_HEADS_MLSTM, HEAD_DIM_MLSTM), 0.1),
        'w_out': nrm(ks[12], (L, D_MIX, D_MODEL), D_MIX ** -0.5),
        'norm2_g': 1.0 + nrm(ks[13], (L, D_MODEL), 0.1),
        'w_router': nrm(ks[14], (L, D_MODEL, N_EXPERTS), D_MODEL ** -0.5),
        'b_router': nrm(ks[15], (L, N_EXPERTS), 0.01),
        'w_gate_up': nrm(ks[16], (L, N_EXPERTS, D_MODEL, 2 * D_FF), D_MODEL ** -0.5),
        'b_gate_up': nrm(ks[17], (L, N_EXPERTS, 2 * D_FF), 0.02),
        'w_down': nrm(ks[18], (L, N_EXPERTS, D_FF, D_MODEL), D_FF ** -0.5),
        'b_down': nrm(ks[19], (L, N_EXPERTS, D_MODEL), 0.02),
    }

def reference(x, norm1_g, w_in, q_norm_g, k_norm_g, conv_w, conv_b, w_mq, w_mk, b_igate, b_fgate,
              mh_norm_g, w_out, norm2_g, w_router, b_router, w_gate_up, b_gate_up, w_down, b_down):
    B, S, _ = x.shape
    slopes = alibi_slopes(N_HEADS_ATTN)

    def heads(t, nh, dh):
        return t.reshape(B, S, nh, dh).transpose(0, 2, 1, 3)

    for l in range(DEPTH):
        h = rmsnorm(x, norm1_g[l])
        z = jnp.einsum('bsd,de->bse', h, w_in[l])
        q_a, k_a, v_a, x_m, v_m, o_m, i_pre, f_pre = jnp.split(z, IN_SPLITS, axis=-1)

        qa = rmsnorm(heads(q_a, N_HEADS_ATTN, HEAD_DIM_ATTN), q_norm_g[l]) * (HEAD_DIM_ATTN ** -0.5)
        ka = rmsnorm(heads(k_a, N_HEADS_ATTN, HEAD_DIM_ATTN), k_norm_g[l])
        va = heads(v_a, N_HEADS_ATTN, HEAD_DIM_ATTN)
        attn = dilated_sliding_attention(qa, ka, va, slopes)
        attn = attn.transpose(0, 2, 1, 3).reshape(B, S, D_ATTN).astype(x.dtype)

        xp = jnp.pad(x_m, ((0, 0), (CONV_K - 1, 0), (0, 0)))
        xc = conv_b[l] + xp[:, 0:S, :] * conv_w[l, 0]
        for j in range(1, CONV_K):
            xc = xc + xp[:, j:j + S, :] * conv_w[l, j]
        xc = jax.nn.silu(xc).reshape(B, S, N_HEADS_MLSTM, HEAD_DIM_MLSTM)
        qm = jnp.einsum('bshd,hde->bhse', xc, w_mq[l])
        km = jnp.einsum('bshd,hde->bhse', xc, w_mk[l]) * (HEAD_DIM_MLSTM ** -0.5)
        vm = heads(v_m, N_HEADS_MLSTM, HEAD_DIM_MLSTM)
        ig = (i_pre + b_igate[l]).transpose(0, 2, 1)
        fg = (f_pre + b_fgate[l]).transpose(0, 2, 1)
        hm = mlstm_chunkwise(qm, km, vm, ig, fg)
        hm = rmsnorm(hm, mh_norm_g[l][:, None, :])
        hm = hm.transpose(0, 2, 1, 3).reshape(B, S, D_MLSTM).astype(x.dtype)
        mlstm_out = jax.nn.sigmoid(o_m) * hm

        mixed = jnp.concatenate([attn, mlstm_out], axis=-1)
        x = x + jnp.einsum('bse,ed->bsd', mixed, w_out[l])

        x = x + moe_ffn(rmsnorm(x, norm2_g[l]), w_router[l], b_router[l], w_gate_up[l], b_gate_up[l],
                        w_down[l], b_down[l])
    return x


_drawn_inputs = setup_inputs


def setup_inputs(seed=0):
    import zlib

    import numpy as np

    out = dict(_drawn_inputs(seed))
    spreads = {}
    factors = {'b_igate': 64.0, 'b_gate_up': 5.54, 'b_down': 6.461}
    for name, (base, spread) in spreads.items():
        noise = np.random.default_rng([zlib.crc32(name.encode()), seed]).standard_normal(out[name].shape)
        drawn = base * np.exp(spread * noise) if base else spread * noise
        out[name] = __import__('jax').numpy.asarray(drawn.astype(out[name].dtype))
    for name, factor in factors.items():
        out[name] = (out[name] * factor).astype(out[name].dtype)
    return out
```

```python
from contextlib import ExitStack

import numpy as np

import concourse.bass as bass
from concourse import mybir

F32 = mybir.dt.float32
I32 = mybir.dt.int32
U32 = mybir.dt.uint32
ALU = mybir.AluOpType
ACT = mybir.ActivationFunctionType
AX = mybir.AxisListType

P = 128
SEQ = 256
D = 1024
T = SEQ // P
KD = D // P
HALF = D // 2
BANK = 512
HA, DA = 8, 64
HM, DM = 4, 128
TAPS = 4
NE, TOPK = 32, 4
FF = D
CAP = 64
ROUNDS = SEQ // CAP
LIMIT, ALPHA = 7.0, 1.702
EPS = 1e-6
MASKED = -1e30
NOWHERE = -1000.0
SW = P + SEQ
WINS = 4
R_G1, R_G2, R_MH, R_CB, R_CW, R_QG, R_KG, ROWS = 0, 8, 16, 20, 24, 40, 41, 42


def attention_bias():
    p = np.arange(P)[:, None]
    dist = np.concatenate([p - np.arange(P)[None], p + P - np.arange(SEQ)[None]], 1)
    count = np.zeros(dist.shape)
    for window, dil in ((128, 1), (512, 4), (2048, 16)):
        count += (dist >= 0) & (dist <= window) & (dist % dil == 0)
    slopes = 2.0 ** (-8.0 * np.arange(1, HA + 1) / HA)
    bias = np.where(count > 0, np.log(np.maximum(count, 1)), MASKED)[:, None, :] - slopes[None, :, None] * dist[:, None, :]
    return np.where(count[:, None, :] > 0, bias, MASKED).astype(np.float32)


def layer_kernel(nc, x, norm1_g, w_in, q_norm_g, k_norm_g, conv_w, conv_b, w_mq, w_mk, b_igate, b_fgate,
                 mh_norm_g, w_out, norm2_g, w_router, b_router, w_gate_up, b_gate_up, w_down, b_down,
                 attn_bias, out):
    with ExitStack() as ctx:
        def sb(name, shape, dt=F32):
            return ctx.enter_context(nc.sbuf_tensor(name, shape, dt))

        def sem(name):
            return ctx.enter_context(nc.semaphore(name))

        gu_ring = sb("gu_ring", [P, 2 * KD * 2 * FF])
        d_ring = sb("d_ring", [P, KD * D])
        gu = gu_ring[:, :].rearrange("p (u k n) -> p u k n", u=2, k=KD)
        dn = d_ring[:, :].rearrange("p (k n) -> p k n", k=KD)
        win = gu_ring[:, 0:WINS * KD * HALF].rearrange("p (b k n) -> p b k n", b=WINS, k=KD)
        wout = dn
        half = KD * 2 * FF
        place = [half]

        def in_second_half(words):
            at = place[0]
            place[0] += words
            assert place[0] <= 2 * half
            return gu_ring[:, at:at + words]

        bias_a = in_second_half(HA * SW).rearrange("p (h n) -> p h n", h=HA)
        qk_n = in_second_half(2 * T * HALF).rearrange("p (s t n) -> p s t n", s=2, t=T)
        qk_t = in_second_half(2 * 4 * SEQ).rearrange("p (s j n) -> p s j n", s=2, j=4)
        v_a = in_second_half(T * HALF).rearrange("p (t n) -> p t n", t=T)
        assert place[0] == half + 4 * 2 * FF
        PADW = SEQ + TAPS - 1
        xm = in_second_half(HM * PADW).rearrange("p (h n) -> p h n", h=HM)
        conv = in_second_half(HM * SEQ).rearrange("p (h n) -> p h n", h=HM)
        xc = in_second_half(HM * SEQ).rearrange("p (h n) -> p h n", h=HM)
        vm = in_second_half(T * HM * (DM + 1)).rearrange("p (t h n) -> p t h n", t=T, h=HM)
        qm_t = in_second_half(HM * SEQ).rearrange("p (h n) -> p h n", h=HM)
        km_t = in_second_half(HM * SEQ).rearrange("p (h n) -> p h n", h=HM)
        wmq = in_second_half(HM * DM).rearrange("p (h n) -> p h n", h=HM)
        wmk = in_second_half(HM * DM).rearrange("p (h n) -> p h n", h=HM)
        sig_c = km_t

        xres = sb("xres", [P, T, D])
        hn = sb("hn", [P, T, D])
        hn_flat = hn[:, :, :].rearrange("p t n -> p (t n)")
        e_m = hn_flat[:, 0:2 * SW].rearrange("p (b n) -> p b n", b=2)
        g_m = hn_flat[:, 2 * SW:4 * SW].rearrange("p (b n) -> p b n", b=2)
        sel = hn_flat[0:HM, 4 * SW:4 * SW + HM * P].rearrange("p (h n) -> p h n", h=HM)
        ht = sb("ht", [P, KD, SEQ])
        ht_flat = ht[:, :, :].rearrange("p k n -> p (k n)")
        xe_t = ht_flat[:, 0:BANK].rearrange("p (k n) -> p k n", k=KD)
        act_t = ht_flat[:, BANK:2 * BANK]
        y_sb = ht_flat[:, 2 * BANK:3 * BANK]
        s_sb = ht_flat[:, 3 * BANK:3 * BANK + SEQ]
        mix_t = sb("mix_t", [P, KD, SEQ])
        mix_flat = mix_t[:, :, :].rearrange("p k n -> p (k n)")
        rows_i, rows_f, rows_l, rows_b, ones_r = (mix_flat[0:HM, i * SEQ:(i + 1) * SEQ] for i in range(5))
        gate_c, sig_g, up_c, act = (mix_flat[:, i * BANK:(i + 1) * BANK] for i in range(4))
        attn_tmp = sb("attn_tmp", [P, 4 * SW])
        p_a = attn_tmp[:, 0:2 * SW].rearrange("p (b n) -> p b n", b=2)
        pt_a = attn_tmp[:, 2 * SW:4 * SW].rearrange("p (b n) -> p b n", b=2)
        sq = attn_tmp[:, 0:2 * HALF].rearrange("p (b n) -> p b n", b=2)
        sq_x = attn_tmp[:, 0:D]
        brow = attn_tmp[:, 0:2 * BANK].rearrange("p (u n) -> p u n", u=2)
        om = sb("om", [P, T, HALF])
        bdn = om[0:NE, :, :].rearrange("p t n -> p (t n)")
        eps = sb("eps", [P, 1])
        qkg = sb("qkg", [P, 2])
        rows_a = sb("rows_a", [HM, SEQ])
        ident = sb("ident", [P, P])
        ones = sb("ones", [P, P])
        before = sb("before", [P, P])
        slot = sb("slot", [P, 2 * CAP])
        slot_i = sb("slot_i", [P, 2 * CAP], I32)
        expert_no = slot[:, 0:NE]
        vec_r = sb("vec_r", [ROWS, P])
        vec = sb("vec", [P, ROWS])
        bif = sb("bif", [HM, 2])
        wif = sb("wif", [P, KD, 2 * HM])
        wr = sb("wr", [P, KD, NE])
        br = sb("br", [P, NE])
        ss1 = sb("ss1", [P, T])
        rs1 = sb("rs1", [P, T])
        ssqk = sb("ssqk", [P, 2, T, HA])
        rsqk = sb("rsqk", [P, 2, T, HA])
        mx = sb("mx", [P, HA, T])
        nmx = sb("nmx", [P, HA, T])
        den = sb("den", [P, HA, T])
        rden = sb("rden", [P, HA, T])
        acol = sb("acol", [P, 2, T, HM])
        em = sb("em", [P, T, HM])
        dm = sb("dm", [P, T, HM])
        rm = sb("rm", [P, T, HM])
        ssm = sb("ssm", [P, T, HM])
        rsm = sb("rsm", [P, T, HM])
        ss2h = sb("ss2h", [P, T, 2])
        ss2 = sb("ss2", [P, T])
        rs2 = sb("rs2", [P, T])
        lg = sb("lg", [P, T, NE])
        top_v = sb("top_v", [P, T, 8])
        top_i = sb("top_i", [P, T, 8], U32)
        top_f = sb("top_f", [P, T, TOPK])
        nv0 = sb("nv0", [P, T])
        gate4 = sb("gate4", [P, T, TOPK])
        gsum = sb("gsum", [P, T])
        eq = sb("eq", [P, TOPK, NE])
        eqg = sb("eqg", [P, TOPK, NE])
        mask = sb("mask", [P, T, NE])
        gate = sb("gate", [P, T, NE])
        gate_t = sb("gate_t", [NE, SEQ])
        pos = sb("pos", [P, T, NE + 1])
        pmax = sb("pmax", [P, 1])
        pm1 = sb("pm1", [1, 1])
        flag = sb("flag", [1, 1], I32)
        pick = sb("pick", [P, T, CAP])
        pickg = sb("pickg", [P, T, 2 * CAP])

        bank = [ctx.enter_context(nc.psum_tensor(f"bank{i}", [P, BANK], F32)) for i in range(8)]

        ld_x = [sem(f"ld_x{t}") for t in range(T)]
        ld_vec = sem("ld_vec")
        ld_small = sem("ld_small")
        ld_wif = sem("ld_wif")
        ld_wr = sem("ld_wr")
        ld_win = [sem(f"ld_win{b}") for b in range(6)]
        ld_bias_a = sem("ld_bias_a")
        ld_wm = sem("ld_wm")
        ld_wout = sem("ld_wout")
        ld_bdn = sem("ld_bdn")
        ld_gu = [sem(f"ld_gu{i}") for i in range(2 * KD)]
        ld_d = [sem(f"ld_d{i}") for i in range(4)]
        ld_brow = [sem(f"ld_brow{i}") for i in range(2)]
        pool_step = sem("pool_step")
        consts = sem("consts")
        dve_step = sem("dve_step")
        act_step = sem("act_step")
        x_ms = sem("x_ms")
        x_rs = sem("x_rs")
        x_norm = sem("x_norm")
        x_turned = sem("x_turned")
        h_ready = sem("h_ready")
        vec_turned = sem("vec_turned")
        vec_ready = sem("vec_ready")
        win_used = sem("win_used")
        z_q = sem("z_q")
        z_xm = sem("z_xm")
        z_if = sem("z_if")
        z_v = sem("z_v")
        z_fill = sem("z_fill")
        fill_read = sem("fill_read")
        qk_sq = sem("qk_sq")
        qk_ms = sem("qk_ms")
        qk_rs = sem("qk_rs")
        qk_norm = sem("qk_norm")
        qk_turned = sem("qk_turned")
        qk_ready = sem("qk_ready")
        xm_read = sem("xm_read")
        conv_ready = sem("conv_ready")
        conv_sig = sem("conv_sig")
        xc_ready = sem("xc_ready")
        f_neg = sem("f_neg")
        f_log = sem("f_log")
        if_read = sem("if_read")
        rows_ready = sem("rows_ready")
        cols_turned = sem("cols_turned")
        cols_ready = sem("cols_ready")
        em_ready = sem("em_ready")
        v_read = sem("v_read")
        scores = sem("scores")
        s_max = sem("s_max")
        s_exp = sem("s_exp")
        p_ready = sem("p_ready")
        p_turned = sem("p_turned")
        pt_ready = sem("pt_ready")
        o_ready = sem("o_ready")
        mix_a = sem("mix_a")
        om_sig = sem("om_sig")
        qkm = sem("qkm")
        qkm_read = sem("qkm_read")
        m_scores = sem("m_scores")
        m_arg = sem("m_arg")
        m_exp = sem("m_exp")
        m_sel = sem("m_sel")
        m_g = sem("m_g")
        m_num = sem("m_num")
        m_ss = sem("m_ss")
        den_read = sem("den_read")
        m_ms = sem("m_ms")
        m_rs = sem("m_rs")
        m_out = sem("m_out")
        m_turned = sem("m_turned")
        mix_m = sem("mix_m")
        mixed = sem("mixed")
        x1_ready = sem("x1_ready")
        x1_ss = sem("x1_ss")
        x1_rs = sem("x1_rs")
        ss2_sum = sem("ss2_sum")
        h2_norm = sem("h2_norm")
        h2_turned = sem("h2_turned")
        h2_ready = sem("h2_ready")
        logits = sem("logits")
        top_ready = sem("top_ready")
        top_exp = sem("top_exp")
        mask_ready = sem("mask_ready")
        gates_ready = sem("gates_ready")
        ranks = sem("ranks")
        gate_turned = sem("gate_turned")
        bank6_read = sem("bank6_read")
        pmax_ready = sem("pmax_ready")
        pmax_turned = sem("pmax_turned")
        flag_ready = sem("flag_ready")
        picked = sem("picked")
        pickg_ready = sem("pickg_ready")
        gathered = sem("gathered")
        xe_ready = sem("xe_ready")
        gu_used = sem("gu_used")
        brow_used = sem("brow_used")
        gu_read = sem("gu_read")
        gate_cut = sem("gate_cut")
        sig_ready = sem("sig_ready")
        act_half = sem("act_half")
        moved = sem("moved")
        act_ready = sem("act_ready")
        slots_turned = sem("slots_turned")
        slots_ready = sem("slots_ready")
        act_turned = sem("act_turned")
        act_t_ready = sem("act_t_ready")
        d_used = sem("d_used")
        y_spread = sem("y_spread")
        acc_final = sem("acc_final")
        x_final = sem("x_final")
        stored = sem("stored")

        w_in0 = w_in[0].rearrange("(k p) n -> p k n", p=P)
        BLOCKS = [0, HALF, 3 * HALF, 2 * HALF, 4 * HALF, 5 * HALF]

        def overflow(eng):
            eng.wait_ge(flag_ready, 1)
            return eng.value_load(flag[0:1, 0:1], min_val=0, max_val=1)

        block = ctx.enter_context(nc.Block())

        @block.sync
        def _(sp):
            def load_gu(e, u, k):
                sp.dma_start(gu[:, u, k, :], w_gate_up[0, e, k * P:(k + 1) * P, :]).then_inc(ld_gu[u * KD + k], 16)

            def load_brow(e, u):
                sp.dma_start(brow[0:97:32, u, :], b_gate_up[0, e, :].rearrange("(i n) -> i n", n=BANK)).then_inc(ld_brow[u], 16)

            def load_d(e, j):
                sp.dma_start(dn[:, 2 * j:2 * j + 2, :],
                             w_down[0, e, 2 * j * P:2 * (j + 1) * P, :].rearrange("(c p) n -> p c n", p=P)).then_inc(ld_d[j], 16)

            def load_win(b):
                sp.dma_start(win[:, b % WINS, :, :], w_in0[:, :, BLOCKS[b]:BLOCKS[b] + HALF]).then_inc(ld_win[b], 16)

            for t in range(T):
                sp.dma_start(xres[:, t, :], x[0, t * P:(t + 1) * P, :]).then_inc(ld_x[t], 16)
            load_win(0)
            load_win(1)
            load_win(2)
            sp.dma_start(bias_a, attn_bias).then_inc(ld_bias_a, 16)
            load_win(3)
            sp.dma_start(wmq, w_mq[0].rearrange("h d e -> d h e")).then_inc(ld_wm, 16)
            sp.dma_start(wmk, w_mk[0].rearrange("h d e -> d h e")).then_inc(ld_wm, 16)
            for b in (4, 5):
                sp.wait_ge(win_used, b - WINS + 1)
                load_win(b)
            sp.dma_start(wout, w_out[0].rearrange("(k p) n -> p k n", p=P)).then_inc(ld_wout, 16)
            for b, used in ((2, 3), (3, 4), (0, 5), (1, 6)):
                sp.wait_ge(win_used, used)
                load_gu(0, 0, 2 * b)
                load_gu(0, 0, 2 * b + 1)
            sp.wait_ge(mix_a, 4)
            for k in range(4):
                load_gu(1, 1, k)
            load_brow(0, 0)
            load_brow(1, 1)
            sp.wait_ge(m_num, HM)
            for k in range(4, KD):
                load_gu(1, 1, k)
            sp.wait_ge(mix_m, HM)
            sp.dma_start(bdn, b_down[0]).then_inc(ld_bdn, 16)
            sp.wait_ge(mixed, 4)
            for j in range(4):
                load_d(0, j)

            def weights(base):
                def next_gu(n, e, u):
                    sp.wait_ge(brow_used, n - 1)
                    load_brow(e, u)
                    for k in range(KD):
                        sp.wait_ge(gu_used, KD * (n - 2) + k + 1)
                        load_gu(e, u, k)

                def next_d(n, e):
                    for j in range(4):
                        sp.wait_ge(d_used, 4 * (n - 1) + j + 1)
                        load_d(e, j)

                with sp.Fori(0, NE // 2 - 1) as i:
                    for u in range(2):
                        e = 2 * i + 2 + u
                        next_gu(base + e, e, u)
                        next_d(base + e - 1, e - 1)
                next_d(base + NE - 1, NE - 1)

            weights(0)
            more = overflow(sp)
            with sp.If(more > 0):
                with sp.Fori(1, ROUNDS) as r:
                    base = r * NE
                    for u in range(2):
                        sp.wait_ge(brow_used, base + u - 1)
                        load_brow(u, u)
                        for k in range(KD):
                            sp.wait_ge(gu_used, KD * (base + u - 2) + k + 1)
                            load_gu(u, u, k)
                    for j in range(4):
                        sp.wait_ge(d_used, 4 * (base - 1) + j + 1)
                        load_d(0, j)
                    weights(base)
            for t in range(T):
                for c in range(2):
                    sp.wait_ge(x_final, 2 * t + c + 1)
                    sp.dma_start(out[0, t * P:(t + 1) * P, c * BANK:(c + 1) * BANK],
                                 xres[:, t, c * BANK:(c + 1) * BANK]).then_inc(stored, 16)
            sp.wait_ge(stored, 16 * 2 * T)

        @block.gpsimd
        def _(pool):
            pool.memset(ident[:, :], 0.0).then_inc(pool_step, 1)
            pool.memset(ones[:, :], 1.0).then_inc(pool_step, 1)
            pool.iota(slot_i[:, :].rearrange("p (d n) -> p d n", d=2), pattern=[[0, 2], [1, CAP]], base=0,
                      channel_multiplier=0).then_inc(pool_step, 1)
            pool.wait_ge(pool_step, 3)
            pool.affine_select(out=ident[:, :], in_=ident[:, :], compare_op=ALU.not_equal, fill=1.0, base=0,
                               pattern=[[-1, P]], channel_multiplier=1).then_inc(consts, 1)
            pool.affine_select(out=before[:, :], in_=ones[:, :], compare_op=ALU.is_gt, fill=0.0, base=0,
                               pattern=[[1, P]], channel_multiplier=-1).then_inc(consts, 1)
            pool.tensor_copy(slot[:, :], slot_i[:, :]).then_inc(consts, 1)
            pool.memset(xm[:, :, 0:TAPS - 1], 0.0).then_inc(consts, 1)
            pool.memset(vm[:, :, :, DM:DM + 1], 1.0).then_inc(consts, 1)
            pool.memset(ones_r, 1.0).then_inc(consts, 1)
            pool.memset(pos[:, :, NE:NE + 1], NOWHERE).then_inc(consts, 1)
            pool.wait_ge(x_turned, 4)
            pool.memset(sel, 0.0).then_inc(pool_step, 1)
            pool.wait_ge(pool_step, 4)
            pool.affine_select(out=sel, in_=sel, compare_op=ALU.not_equal, fill=1.0, base=0,
                               pattern=[[-1, HM], [0, P]], channel_multiplier=1).then_inc(consts, 1)
            for h in range(HM):
                pool.wait_ge(m_exp, h + 1)
                diag = e_m[:, h % 2, :].rearrange("p (b n) -> p b n", b=3)[:, 0:3:2, :]
                pool.affine_select(out=diag, in_=diag, compare_op=ALU.is_ge, fill=0.0, base=0,
                                   pattern=[[0, 2], [1, P]], channel_multiplier=-1).then_inc(m_sel, 1)

        @block.scalar
        def _(act_e):
            act = act_e
            act.dma_start(vec_r[R_G1:R_G1 + KD, :], norm1_g[0].rearrange("(k n) -> k n", n=P)).then_inc(ld_vec, 16)
            act.dma_start(vec_r[R_G2:R_G2 + KD, :], norm2_g[0].rearrange("(k n) -> k n", n=P)).then_inc(ld_vec, 16)
            act.dma_start(vec_r[R_MH:R_MH + HM, :], mh_norm_g[0]).then_inc(ld_vec, 16)
            act.dma_start(vec_r[R_CB:R_CB + HM, :], conv_b[0].rearrange("(k n) -> k n", n=P)).then_inc(ld_vec, 16)
            act.dma_start(vec_r[R_CW:R_CW + TAPS * HM, :], conv_w[0].rearrange("j (k n) -> (j k) n", n=P)).then_inc(ld_vec, 16)
            for r, g in ((R_QG, q_norm_g), (R_KG, k_norm_g)):
                for i in range(2):
                    act.dma_start(vec_r[r:r + 1, i * DA:(i + 1) * DA], g).then_inc(ld_vec, 16)
            act.dma_start(bif[:, 0:1], b_igate[0].rearrange("(h o) -> h o", o=1)).then_inc(ld_small, 16)
            act.dma_start(bif[:, 1:2], b_fgate[0].rearrange("(h o) -> h o", o=1)).then_inc(ld_small, 16)
            act.dma_start(wif[:, :, :], w_in0[:, :, 6 * HALF:6 * HALF + 2 * HM]).then_inc(ld_wif, 16)
            act.dma_start(wr[:, :, :], w_router[0].rearrange("(k p) n -> p k n", p=P)).then_inc(ld_wr, 16)
            act.dma_start(br[:, :], b_router[0:1, :].broadcast_to([P, NE])).then_inc(ld_wr, 16)

            for t in range(T):
                act.wait_ge(ld_x[t], 16)
                if t:
                    act.wait_ge(x_ms, t)
                act.activation(sq_x, xres[:, t, :], ACT.Square, accum_out=ss1[:, t:t + 1]).then_inc(x_ms, 1)
                act.wait_ge(x_ms, t + 1)
            act.wait_ge(vec_ready, 1)
            act.activation(rs1[:, :], ss1[:, :], ACT.Ln, scale=1.0 / D, bias=eps[:, 0:1]).then_inc(act_step, 1)
            act.wait_ge(act_step, 1)
            act.activation(rs1[:, :], rs1[:, :], ACT.Exp, scale=-0.5).then_inc(x_rs, 1)
            for s in range(2):
                for t in range(T):
                    n = 2 * s + t
                    act.wait_ge(z_q, n + 1)
                    if n == 0:
                        act.wait_ge(x_ms, T)
                    if n >= 2:
                        act.wait_ge(qk_ms, n - 1)
                    act.activation(sq[:, t, :], bank[n][:, :], ACT.Square).then_inc(qk_sq, 1)
            for s in range(2):
                act.wait_ge(qk_ms, 2 * s + 2)
                act.activation(rsqk[:, s], ssqk[:, s], ACT.Ln, scale=1.0 / DA, bias=eps[:, 0:1]).then_inc(act_step, 1)
                act.wait_ge(act_step, 2 + s)
                act.activation(rsqk[:, s], rsqk[:, s], ACT.Exp, scale=-0.5).then_inc(qk_rs, 1)
            for i in range(2):
                act.wait_ge(z_xm, i + 1)
                if i == 0:
                    act.wait_ge(consts, 7)
                act.activation(xm[:, 2 * i:2 * i + 2, TAPS - 1:PADW], bank[6 + i][:, :].rearrange("p (h n) -> p h n", h=2),
                               ACT.Copy).then_inc(xm_read, 1)
            act.wait_ge(f_neg, 1)
            act.activation(rows_l, rows_l, ACT.Exp).then_inc(act_step, 1)
            act.wait_ge(act_step, 4)
            act.activation(rows_l, rows_l, ACT.Ln, bias=1.0).then_inc(f_log, 1)
            for n in range(4):
                act.wait_ge(qk_turned, n + 1)
                s, i = n // 2, n % 2
                act.activation(qk_t[:, s, 2 * i:2 * i + 2, :], bank[2 + n][:, :].rearrange("p (j n) -> p j n", j=2),
                               ACT.Copy, scale=qkg[:, s:s + 1]).then_inc(qk_ready, 1)
            act.wait_ge(z_v, 2)
            for t in range(T):
                act.activation(v_a[:, t, :], bank[t][:, :], ACT.Copy).then_inc(v_read, 1)
            act.wait_ge(cols_ready, 1)
            act.activation(em[:, :, :], acol[:, 1], ACT.Exp).then_inc(em_ready, 1)
            act.wait_ge(conv_ready, HM)
            act.activation(sig_c, conv, ACT.Sigmoid).then_inc(conv_sig, 1)

            def turned_p(h):
                act.wait_ge(p_turned, h + 1)
                if h >= 2:
                    act.wait_ge(o_ready, h - 1)
                act.activation(pt_a[:, h % 2, :], bank[6 + h % 2][:, 0:SW], ACT.Copy).then_inc(pt_ready, 1)

            def mixed_a(j):
                act.wait_ge(o_ready, 2 * j + 2)
                if j == 0:
                    act.wait_ge(cols_turned, 1)
                act.activation(mix_t[:, j, :], bank[2 + j % 2][:, (j // 2) * SEQ:(j // 2 + 1) * SEQ], ACT.Copy).then_inc(mix_a, 1)

            for h in range(HA + 2):
                if h < HA:
                    act.wait_ge(s_max, h + 1)
                    for t in range(T):
                        lo, hi = (0, P) if t == 0 else (P, SW)
                        act.activation(p_a[:, h % 2, lo:hi], p_a[:, h % 2, lo:hi], ACT.Exp, bias=nmx[:, h, t:t + 1],
                                       accum_out=den[:, h, t:t + 1]).then_inc(s_exp, 1)
                if 1 <= h <= HA:
                    turned_p(h - 1)
                if h in (3, 5, 7, 9):
                    mixed_a((h - 3) // 2)
                if h >= 2 and h % 2 == 0 and h <= 8:
                    n = h // 2 - 1
                    act.wait_ge(z_fill, n + 1)
                    if n < 2:
                        act.activation(vm[:, n, :, 0:DM], bank[n][:, :].rearrange("p (h n) -> p h n", h=HM),
                                       ACT.Copy).then_inc(fill_read, 1)
                    else:
                        act.activation(om[:, n - 2, :], bank[n - 2][:, :], ACT.Copy).then_inc(fill_read, 1)
            for i in range(2):
                act.wait_ge(qkm, i + 1)
                act.activation(qm_t[:, 2 * i:2 * i + 2, :], bank[4 + i][:, :].rearrange("p (h n) -> p h n", h=2),
                               ACT.Copy).then_inc(qkm_read, 1)
            for h in range(HM):
                act.wait_ge(m_arg, h + 1)
                act.activation(e_m[:, h % 2, :], e_m[:, h % 2, :], ACT.Exp, scale=-1.0).then_inc(m_exp, 1)
            for h in range(HM):
                act.wait_ge(den_read, T * HM)
                for t in range(T):
                    src = bank[2 * t + h // 2][:, (h % 2) * SEQ:(h % 2) * SEQ + DM]
                    if h + t:
                        act.wait_ge(m_ss, 2 * h + t)
                    act.activation(attn_tmp[:, 2 * BANK:2 * BANK + DM], src, ACT.Square, accum_out=ssm[:, t, h:h + 1]).then_inc(m_ss, 1)
            act.wait_ge(m_ms, 1)
            act.activation(rsm[:, :, :], ssm[:, :, :], ACT.Ln, scale=1.0 / DM, bias=eps[:, 0:1]).then_inc(act_step, 1)
            act.wait_ge(act_step, 5)
            act.activation(rsm[:, :, :], rsm[:, :, :], ACT.Exp, scale=-0.5).then_inc(m_rs, 1)
            act.wait_ge(fill_read, 4)
            act.activation(om[:, :, :], om[:, :, :], ACT.Sigmoid).then_inc(om_sig, 1)
            for h in range(HM):
                act.wait_ge(m_turned, h + 1)
                act.activation(mix_t[:, 4 + h, :], bank[4 + h][:, 0:SEQ], ACT.Copy,
                               scale=vec[:, R_MH + h:R_MH + h + 1]).then_inc(mix_m, 1)
            for t in range(T):
                for c in range(2):
                    act.wait_ge(x1_ready, 2 * t + c + 1)
                    if t + c == 0:
                        act.wait_ge(mix_m, HM)
                    if t:
                        act.wait_ge(x1_ss, c + 1)
                    act.activation(bank[6 + c][:, :], xres[:, t, c * BANK:(c + 1) * BANK], ACT.Square,
                                   accum_out=ss2h[:, t, c:c + 1]).then_inc(x1_ss, 1)
                act.wait_ge(ss2_sum, t + 1)
                act.activation(rs2[:, t:t + 1], ss2[:, t:t + 1], ACT.Ln, scale=1.0 / D, bias=eps[:, 0:1]).then_inc(act_step, 1)
                act.wait_ge(act_step, 6 + t)
                act.activation(rs2[:, t:t + 1], rs2[:, t:t + 1], ACT.Exp, scale=-0.5).then_inc(x1_rs, 1)
            for t in range(T):
                act.wait_ge(top_ready, t + 1)
                act.activation(gate4[:, t, :], top_v[:, t, 0:TOPK], ACT.Exp, bias=nv0[:, t:t + 1],
                               accum_out=gsum[:, t:t + 1]).then_inc(top_exp, 1)
            act.wait_ge(gate_turned, 1)
            act.activation(gate_t[:, :], bank[6][0:NE, 0:SEQ], ACT.Copy).then_inc(bank6_read, 1)

            def expert(n):
                act.wait_ge(slots_turned, n + 1)
                act.activation(s_sb, bank[6][:, 0:SEQ], ACT.Copy).then_inc(slots_ready, 1)
                act.wait_ge(gate_cut, n + 1)
                act.activation(sig_g, gate_c, ACT.Sigmoid, scale=ALPHA).then_inc(sig_ready, 1)
                act.wait_ge(act_turned, n + 1)
                act.activation(act_t, bank[6][:, :], ACT.Copy).then_inc(act_t_ready, 1)
                act.wait_ge(d_used, 4 * n + 4)
                act.activation(y_sb, bank[6][:, :], ACT.Copy).then_inc(bank6_read, 1)

            with act.Fori(0, NE) as e:
                expert(e)
            more = overflow(act)
            with act.If(more > 0):
                with act.Fori(NE, ROUNDS * NE) as e:
                    expert(e)

        @block.vector
        def _(dve):
            steps = [0]

            def step(ins):
                steps[0] += 1
                ins.then_inc(dve_step, 1)

            def settle():
                dve.wait_ge(dve_step, steps[0])

            dve.memset(eps[:, :], EPS).then_inc(dve_step, 1)
            steps[0] += 1
            settle()
            dve.wait_ge(vec_turned, 1)
            step(dve.tensor_copy(vec[:, :], bank[0][:, 0:ROWS]))
            settle()
            step(dve.tensor_scalar(qkg[:, 0:1], vec[:, R_QG:R_QG + 1], float(DA) ** -0.5, None, ALU.mult))
            dve.tensor_copy(qkg[:, 1:2], vec[:, R_KG:R_KG + 1]).then_inc(vec_ready, 1)
            dve.wait_ge(x_rs, 1)
            for t in range(T):
                dve.tensor_scalar(hn[:, t, :], xres[:, t, :], rs1[:, t:t + 1], None, ALU.mult).then_inc(x_norm, 1)
            for t in range(T):
                for i in range(2):
                    dve.wait_ge(x_turned, 2 * t + i + 1)
                    dve.tensor_tensor(ht[:, 4 * i:4 * i + 4, t * P:(t + 1) * P],
                                      bank[4 + 2 * t + i][:, :].rearrange("p (k n) -> p k n", k=4),
                                      vec[:, R_G1 + 4 * i:R_G1 + 4 * i + 4].unsqueeze(2).broadcast_to([P, 4, P]),
                                      ALU.mult).then_inc(h_ready, 1)
            for s in range(2):
                for t in range(T):
                    dve.wait_ge(qk_sq, 2 * s + t + 1)
                    dve.tensor_reduce(ssqk[:, s, t, :], sq[:, t, :].rearrange("p (h n) -> p h n", h=HA), AX.X,
                                      ALU.add).then_inc(qk_ms, 1)
                if s == 0:
                    continue
                for s2 in range(2):
                    dve.wait_ge(qk_rs, s2 + 1)
                    for t in range(T):
                        dve.tensor_tensor(qk_n[:, s2, t, :].rearrange("p (h n) -> p h n", h=HA),
                                          bank[2 * s2 + t][:, :].rearrange("p (h n) -> p h n", h=HA),
                                          rsqk[:, s2, t, :].unsqueeze(2).broadcast_to([P, HA, DA]),
                                          ALU.mult).then_inc(qk_norm, 1)
            dve.wait_ge(z_if, 1)
            dve.wait_ge(ld_small, 32)
            dve.wait_ge(consts, 7)
            step(dve.tensor_scalar(rows_f, bank[4][0:HM, SEQ:2 * SEQ], bif[:, 1:2], None, ALU.add))
            step(dve.tensor_scalar(rows_i, bank[4][0:HM, 0:SEQ], bif[:, 0:1], None, ALU.add))
            settle()
            dve.scalar_tensor_tensor(out=rows_l, in0=rows_f, scalar=-1.0, in1=rows_f, op0=ALU.mult, op1=ALU.min).then_inc(f_neg, 1)
            dve.wait_ge(xm_read, 2)
            for j in range(TAPS):
                for h in range(HM):
                    tap = vec[:, R_CW + j * HM + h:R_CW + j * HM + h + 1]
                    if j == 0:
                        step(dve.tensor_scalar(conv[:, h, :], xm[:, h, 0:SEQ], tap, vec[:, R_CB + h:R_CB + h + 1],
                                               ALU.mult, ALU.add))
                    else:
                        ins = dve.scalar_tensor_tensor(out=conv[:, h, :], in0=xm[:, h, j:j + SEQ], scalar=tap,
                                                       in1=conv[:, h, :], op0=ALU.mult, op1=ALU.add)
                        if j < TAPS - 1:
                            step(ins)
                        else:
                            ins.then_inc(conv_ready, 1)
                if j < TAPS - 1:
                    settle()
            dve.wait_ge(f_log, 1)
            step(dve.scalar_tensor_tensor(out=rows_f, in0=rows_f, scalar=0.0, in1=rows_l, op0=ALU.min, op1=ALU.subtract))
            settle()
            step(dve.tensor_tensor_scan(rows_b, ones_r, rows_f, 0.0, ALU.mult, ALU.add))
            settle()
            step(dve.tensor_tensor(rows_i, rows_i, rows_b, ALU.subtract))
            settle()
            step(dve.tensor_tensor_scan(rows_a[:, :], ones_r, rows_i, 0.0, ALU.mult, ALU.max))
            settle()
            dve.scalar_tensor_tensor(out=rows_l, in0=rows_b, scalar=-1.0, in1=rows_a[:, :], op0=ALU.mult,
                                     op1=ALU.subtract).then_inc(rows_ready, 1)

            def softmax(h):
                dve.wait_ge(scores, h + 1)
                if h == 0:
                    dve.wait_ge(ld_bias_a, 16)
                if h >= 2:
                    dve.wait_ge(p_turned, h - 1)
                for t in range(T):
                    lo, hi = (0, P) if t == 0 else (P, SW)
                    step(dve.tensor_tensor_reduce(out=p_a[:, h % 2, lo:hi], in0=bank[4 + h % 2][:, lo:hi],
                                                  in1=bias_a[:, h, lo:hi], scale=1.0, scalar=MASKED, op0=ALU.add,
                                                  op1=ALU.max, accum_out=mx[:, h, t:t + 1]))
                settle()
                dve.tensor_scalar(nmx[:, h, :], mx[:, h, :], -1.0, None, ALU.mult).then_inc(s_max, 1)

            def normalise(h):
                dve.wait_ge(s_exp, 2 * h + 2)
                step(dve.reciprocal(rden[:, h, :], den[:, h, :]))
                settle()
                for t in range(T):
                    lo, hi = (0, P) if t == 0 else (P, SW)
                    dve.tensor_scalar(p_a[:, h % 2, lo:hi], p_a[:, h % 2, lo:hi], rden[:, h, t:t + 1], None,
                                      ALU.mult).then_inc(p_ready, 1)

            for h in range(HA + 1):
                if h < HA:
                    softmax(h)
                if h == 1:
                    dve.wait_ge(cols_turned, 1)
                    dve.tensor_copy(acol[:, :, :, :], bank[2][:, 0:2 * T * HM].rearrange("p (s t h) -> p s t h", s=2, t=T)).then_inc(cols_ready, 1)
                    dve.wait_ge(conv_sig, 1)
                    dve.tensor_tensor(xc, conv, sig_c, ALU.mult).then_inc(xc_ready, 1)
                if h >= 1:
                    normalise(h - 1)
            for i in range(2):
                dve.wait_ge(qkm, 3 + i)
                dve.tensor_copy(km_t[:, 2 * i:2 * i + 2, :], bank[6 + i][:, :].rearrange("p (h n) -> p h n", h=2)).then_inc(qkm_read, 1)

            def decay(h):
                dve.wait_ge(m_scores, h + 1)
                if h >= 2:
                    dve.wait_ge(m_g, h - 1)
                a_bc = bank[6 + h % 2]
                step(dve.tensor_scalar(e_m[:, h % 2, 0:SEQ], a_bc[:, 0:SEQ], acol[:, 0, 0, h:h + 1], 0.0,
                                       ALU.subtract, ALU.max))
                step(dve.tensor_scalar(e_m[:, h % 2, SEQ:SW], a_bc[:, P:SEQ], acol[:, 0, 1, h:h + 1], 0.0,
                                       ALU.subtract, ALU.max))
                settle()
                dve.engine_nop().then_inc(m_arg, 1)

            def weighed(h):
                dve.wait_ge(m_sel, h + 1)
                if h >= 2:
                    dve.wait_ge(m_num, h - 1)
                dve.scalar_tensor_tensor(out=g_m[:, h % 2, :], in0=bank[4 + h % 2][:, 0:SW], scalar=float(DM) ** -0.5,
                                         in1=e_m[:, h % 2, :], op0=ALU.mult, op1=ALU.mult).then_inc(m_g, 1)

            for h in range(HM + 1):
                if h < HM:
                    decay(h)
                if h >= 1:
                    weighed(h - 1)
            for h in range(HM):
                dve.wait_ge(m_num, HM)
                for t in range(T):
                    at = (h % 2) * SEQ + DM
                    dve.tensor_copy(dm[:, t, h:h + 1], bank[2 * t + h // 2][:, at:at + 1]).then_inc(den_read, 1)
            dve.wait_ge(den_read, T * HM)
            step(dve.scalar_tensor_tensor(out=dm[:, :, :], in0=dm[:, :, :], scalar=-1.0, in1=dm[:, :, :], op0=ALU.mult, op1=ALU.max))
            settle()
            dve.wait_ge(em_ready, 1)
            step(dve.tensor_tensor(dm[:, :, :], dm[:, :, :], em[:, :, :], ALU.max))
            settle()
            step(dve.reciprocal(rm[:, :, :], dm[:, :, :]))
            settle()
            step(dve.tensor_tensor(dm[:, :, :], rm[:, :, :], rm[:, :, :], ALU.mult))
            settle()
            dve.wait_ge(m_ss, T * HM)
            dve.tensor_tensor(ssm[:, :, :], ssm[:, :, :], dm[:, :, :], ALU.mult).then_inc(m_ms, 1)
            dve.wait_ge(m_rs, 1)
            step(dve.tensor_tensor(rm[:, :, :], rm[:, :, :], rsm[:, :, :], ALU.mult))
            settle()
            dve.wait_ge(om_sig, 1)
            for h in range(HM):
                for t in range(T):
                    o = om[:, t, h * DM:(h + 1) * DM]
                    dve.scalar_tensor_tensor(out=o, in0=bank[2 * t + h // 2][:, (h % 2) * SEQ:(h % 2) * SEQ + DM],
                                             scalar=rm[:, t, h:h + 1], in1=o, op0=ALU.mult, op1=ALU.mult).then_inc(m_out, 1)
            for t in range(T):
                for c in range(2):
                    dve.wait_ge(mixed, 2 * t + c + 1)
                    xs = xres[:, t, c * BANK:(c + 1) * BANK]
                    dve.tensor_tensor(xs, bank[2 * t + c][:, :], xs, ALU.add).then_inc(x1_ready, 1)
                dve.wait_ge(x1_ss, 2 * t + 2)
                dve.tensor_tensor(ss2[:, t:t + 1], ss2h[:, t, 0:1], ss2h[:, t, 1:2], ALU.add).then_inc(ss2_sum, 1)
                dve.wait_ge(x1_rs, t + 1)
                dve.tensor_scalar(hn[:, t, :], xres[:, t, :], rs2[:, t:t + 1], None, ALU.mult).then_inc(h2_norm, 1)
            for t in range(T):
                for i in range(2):
                    dve.wait_ge(h2_turned, 2 * t + i + 1)
                    dve.tensor_tensor(ht[:, 4 * i:4 * i + 4, t * P:(t + 1) * P],
                                      bank[4 + 2 * t + i][:, :].rearrange("p (k n) -> p k n", k=4),
                                      vec[:, R_G2 + 4 * i:R_G2 + 4 * i + 4].unsqueeze(2).broadcast_to([P, 4, P]),
                                      ALU.mult).then_inc(h2_ready, 1)
            dve.wait_ge(ld_wr, 32)
            for t in range(T):
                dve.wait_ge(logits, T)
                step(dve.tensor_tensor(lg[:, t, :], bank[4][:, t * NE:(t + 1) * NE], br[:, :], ALU.add))
                settle()
                step(dve.max(top_v[:, t, :], lg[:, t, :]))
                settle()
                dve.tensor_scalar(nv0[:, t:t + 1], top_v[:, t, 0:1], -1.0, None, ALU.mult).then_inc(top_ready, 1)
                step(dve.max_index(top_i[:, t, :], top_v[:, t, :], lg[:, t, :]))
                settle()
                step(dve.tensor_copy(top_f[:, t, :], top_i[:, t, 0:TOPK]))
                settle()
                step(dve.tensor_tensor(eq[:, :, :], expert_no.unsqueeze(1).broadcast_to([P, TOPK, NE]),
                                       top_f[:, t, :].unsqueeze(2).broadcast_to([P, TOPK, NE]), ALU.is_equal))
                settle()
                dve.tensor_reduce(mask[:, t, :], eq[:, :, :].rearrange("p j e -> p e j"), AX.X, ALU.add).then_inc(mask_ready, 1)
                dve.wait_ge(top_exp, t + 1)
                step(dve.reciprocal(gsum[:, t:t + 1], gsum[:, t:t + 1]))
                settle()
                step(dve.tensor_scalar(gate4[:, t, :], gate4[:, t, :], gsum[:, t:t + 1], None, ALU.mult))
                settle()
                step(dve.tensor_tensor(eqg[:, :, :], eq[:, :, :], gate4[:, t, :].unsqueeze(2).broadcast_to([P, TOPK, NE]), ALU.mult))
                settle()
                dve.tensor_reduce(gate[:, t, :], eqg[:, :, :].rearrange("p j e -> p e j"), AX.X, ALU.add).then_inc(gates_ready, 1)
            dve.wait_ge(ranks, 1)
            dve.wait_ge(mask_ready, 2)
            step(dve.scalar_tensor_tensor(out=pos[:, :, 0:NE], in0=bank[5][:, 0:T * NE].rearrange("p (t n) -> p t n", t=T),
                                          scalar=-NOWHERE, in1=mask[:, :, :], op0=ALU.add, op1=ALU.mult))
            settle()
            step(dve.tensor_scalar(pos[:, :, 0:NE], pos[:, :, 0:NE], NOWHERE, None, ALU.add))
            settle()
            dve.tensor_reduce(pmax[:, :], pos[:, :, 0:NE], AX.XY, ALU.max).then_inc(pmax_ready, 1)

            def take(e):
                for t in range(T):
                    ins = dve.tensor_scalar(pick[:, t, :], slot[:, 0:CAP], pos[:, t, bass.ds(e, 1)], None, ALU.is_equal)
                ins.then_inc(picked, 1)

            dve.wait_ge(gates_ready, 2)
            take(0)
            dve.wait_ge(pmax_turned, 1)
            step(dve.tensor_reduce(pm1[:, :], bank[5][0:1, 0:P], AX.X, ALU.max))
            settle()
            dve.tensor_scalar(flag[:, :], pm1[:, :], float(CAP), None, ALU.is_ge).then_inc(flag_ready, 1)
            dve.engine_nop().then_inc(gu_read, 1)

            def gained():
                return dve.tensor_tensor(xe_t, bank[7][:, :].rearrange("p (k n) -> p k n", k=KD),
                                         vec[:, R_G2:R_G2 + KD].unsqueeze(2).broadcast_to([P, KD, CAP]), ALU.mult)

            def expert(e, n, g):
                dve.wait_ge(gathered, g + 1)
                take(e + 1)
                for t in range(T):
                    ins = dve.tensor_scalar(pickg[:, t, :], slot[:, :], pos[:, t, bass.ds(e, 1)],
                                            gate[:, t, bass.ds(e, 1)], ALU.is_equal, ALU.mult)
                ins.then_inc(pickg_ready, 1)
                dve.wait_ge(gu_used, KD * n + KD)
                dve.tensor_scalar(gate_c, bank[4][:, :], LIMIT, None, ALU.min).then_inc(gate_cut, 1)
                dve.tensor_scalar(up_c, bank[5][:, :], LIMIT, -LIMIT, ALU.min, ALU.max).then_inc(gu_read, 1)
                dve.wait_ge(gate_cut, n + 1)
                dve.wait_ge(gu_read, n + 2)
                dve.scalar_tensor_tensor(out=act, in0=up_c, scalar=1.0, in1=gate_c, op0=ALU.add, op1=ALU.mult).then_inc(act_half, 1)
                dve.wait_ge(act_half, n + 1)
                dve.wait_ge(sig_ready, n + 1)
                dve.tensor_tensor(act, act, sig_g, ALU.mult).then_inc(act_ready, 1)
                dve.wait_ge(gathered, g + 2)
                gained().then_inc(xe_ready, 1)

            dve.wait_ge(gathered, 1)
            gained().then_inc(xe_ready, 1)
            with dve.Fori(0, NE) as e:
                expert(e, e, e)
            more = overflow(dve)
            with dve.If(more > 0):
                with dve.Fori(1, ROUNDS) as r:
                    dve.wait_ge(pickg_ready, NE * r)
                    dve.wait_ge(picked, (NE + 1) * r)
                    dve.tensor_scalar(pos[:, :, :], pos[:, :, :], -float(CAP), None, ALU.add).then_inc(moved, 1)
                    dve.wait_ge(moved, r)
                    take(0)
                    dve.wait_ge(gathered, (NE + 1) * r + 1)
                    gained().then_inc(xe_ready, 1)
                    with dve.Fori(0, NE) as e:
                        expert(e, r * NE + e, r * (NE + 1) + e)
            for t in range(T):
                for c in range(2):
                    if t + c == 0:
                        dve.wait_ge(acc_final, 1)
                    xs = xres[:, t, c * BANK:(c + 1) * BANK]
                    dve.tensor_tensor(xs, bank[2 * t + c][:, :], xs, ALU.add).then_inc(x_final, 1)

        @block.tensor
        def _(pe):
            pe.wait_ge(consts, 1)
            pe.wait_ge(ld_vec, 16 * 9)
            pe.transpose(bank[0][:, 0:ROWS], vec_r[:, :], ident[0:ROWS, 0:ROWS]).then_inc(vec_turned, 1)
            for t in range(T):
                pe.wait_ge(x_norm, t + 1)
                for i in range(2):
                    for k in range(4):
                        c = 4 * i + k
                        mm = pe.transpose(bank[4 + 2 * t + i][:, k * P:(k + 1) * P], hn[:, t, c * P:(c + 1) * P], ident[:, :])
                    mm.then_inc(x_turned, 1)

            def project(dst, b, t, ks=range(KD)):
                for k in ks:
                    mm = pe.matmul(dst[:, :], ht[:, k, t * P:(t + 1) * P], win[:, b % WINS, k, :],
                                   start=(k == 0), stop=(k == KD - 1))
                return mm

            for b in range(2):
                pe.wait_ge(ld_win[b], 16)
                for t in range(T):
                    if b == 0:
                        pe.wait_ge(h_ready, 2 * t + 2)
                        if t == 0:
                            pe.wait_ge(vec_ready, 1)
                    project(bank[2 * b + t], b, t).then_inc(z_q, 1)
                pe.wait_ge(z_q, 2 * b + 2)
                pe.nop().then_inc(win_used, 1)
            pe.wait_ge(ld_win[2], 16)
            for i in range(2):
                for c in range(2):
                    m = 2 * i + c
                    for k in range(KD):
                        mm = pe.matmul(bank[6 + i][:, c * SEQ:(c + 1) * SEQ], win[:, 2, k, m * P:(m + 1) * P], ht[:, k, :],
                                       start=(k == 0), stop=(k == KD - 1))
                mm.then_inc(z_xm, 1)
            pe.wait_ge(z_xm, 2)
            pe.nop().then_inc(win_used, 1)
            pe.wait_ge(ld_wif, 16)
            for s in range(2):
                for k in range(KD):
                    mm = pe.matmul(bank[4][0:HM, s * SEQ:(s + 1) * SEQ], wif[:, k, s * HM:(s + 1) * HM], ht[:, k, :],
                                   start=(k == 0), stop=(k == KD - 1))
            mm.then_inc(z_if, 1)
            pe.wait_ge(ld_win[3], 16)
            for t in range(T):
                pe.wait_ge(qk_norm, t + 1)
                mm = project(bank[t], 3, t)
                mm.then_inc(z_v, 1)
            pe.wait_ge(z_v, 2)
            pe.nop().then_inc(win_used, 1)
            for s in range(2):
                for i in range(2):
                    if s == 0 and i == 0:
                        pe.wait_ge(qk_norm, 4)
                    if s == 1 and i == 0:
                        pe.wait_ge(f_neg, 1)
                    for j in range(2):
                        for t in range(T):
                            c = 2 * i + j
                            mm = pe.transpose(bank[2 + 2 * s + i][:, j * SEQ + t * P:j * SEQ + (t + 1) * P],
                                              qk_n[:, s, t, c * P:(c + 1) * P], ident[:, :])
                    mm.then_inc(qk_turned, 1)

            def score(h):
                if h == 0:
                    pe.wait_ge(qk_ready, 4)
                if h >= 2:
                    pe.wait_ge(s_max, h - 1)
                r = (h % 2) * DA
                for t in range(T):
                    lo, hi = (0, P) if t == 0 else (P, SW)
                    mm = pe.matmul(bank[4 + h % 2][:, lo:hi], qk_t[r:r + DA, 0, h // 2, t * P:(t + 1) * P],
                                   qk_t[r:r + DA, 1, h // 2, 0:(t + 1) * P], start=True, stop=True)
                mm.then_inc(scores, 1)

            def turn_p(h):
                pe.wait_ge(p_ready, 2 * h + 2)
                if h == 0:
                    pe.wait_ge(xm_read, 2)
                if h >= 2:
                    pe.wait_ge(pt_ready, h - 1)
                for i in range(3):
                    mm = pe.transpose(bank[6 + h % 2][:, i * P:(i + 1) * P], p_a[:, h % 2, i * P:(i + 1) * P], ident[:, :])
                mm.then_inc(p_turned, 1)

            def attend(h):
                pe.wait_ge(pt_ready, h + 1)
                if h == 0:
                    pe.wait_ge(v_read, 2)
                    pe.wait_ge(cols_ready, 1)
                r, j = (h % 2) * DA, h // 2
                if j >= 2:
                    pe.wait_ge(mix_a, j - 1)
                dst = bank[2 + j % 2][r:r + DA, (j // 2) * SEQ:(j // 2 + 1) * SEQ]
                pe.matmul(dst, v_a[:, 0, h * DA:(h + 1) * DA], pt_a[:, h % 2, 0:SEQ], start=True, stop=False)
                pe.matmul(dst[:, P:SEQ], v_a[:, 1, h * DA:(h + 1) * DA], pt_a[:, h % 2, SEQ:SW],
                          start=False, stop=True).then_inc(o_ready, 1)

            def fill(i):
                b, t, first = 4 + i // 4, (i // 2) % 2, i % 2 == 0
                if first:
                    if t == 0:
                        pe.wait_ge(ld_win[b], 16)
                    if b == 4:
                        pe.wait_ge(v_read, t + 1)
                    else:
                        pe.wait_ge(fill_read, t + 1)
                mm = project(bank[t], b, t, range(0, 4) if first else range(4, KD))
                if not first:
                    mm.then_inc(z_fill, 1)
                    if t == 1:
                        pe.wait_ge(z_fill, 2 * (b - 4) + 2)
                        pe.nop().then_inc(win_used, 1)

            for h in range(HA + 2):
                if h < HA:
                    score(h)
                    if h == 0:
                        pe.wait_ge(rows_ready, 1)
                        for s, rows in ((0, rows_i), (1, rows_l)):
                            for t in range(T):
                                at = (s * T + t) * HM
                                mm = pe.transpose(bank[2][:, at:at + HM], rows[:, t * P:(t + 1) * P], ident[0:HM, 0:HM])
                        mm.then_inc(cols_turned, 1)
                    fill(h)
                if 1 <= h <= HA:
                    turn_p(h - 1)
                if h >= 2:
                    attend(h - 2)
            pe.wait_ge(ld_wm, 32)
            pe.wait_ge(xc_ready, 1)
            pe.wait_ge(s_max, HA)
            pe.wait_ge(pt_ready, HA)
            for s, w in ((0, wmq), (1, wmk)):
                for h in range(HM):
                    mm = pe.matmul(bank[4 + 2 * s + h // 2][:, (h % 2) * SEQ:(h % 2 + 1) * SEQ], w[:, h, :], xc[:, h, :],
                                   start=True, stop=True)
                    if h % 2:
                        mm.then_inc(qkm, 1)

            def m_score(h):
                if h == 0:
                    pe.wait_ge(qkm_read, 4)
                    pe.wait_ge(consts, 8)
                    pe.wait_ge(rows_ready, 1)
                if h >= 2:
                    pe.wait_ge(m_g, h - 1)
                s_b, a_b = bank[4 + h % 2], bank[6 + h % 2]
                pe.matmul(a_b[:, 0:SEQ], sel[:, h, :], rows_a[:, :], start=True, stop=True)
                pe.matmul(s_b[:, 0:SEQ], km_t[:, h, 0:P], qm_t[:, h, :], start=True, stop=True)
                pe.matmul(s_b[:, SEQ:SW], km_t[:, h, P:SEQ], qm_t[:, h, P:SEQ], start=True, stop=True).then_inc(m_scores, 1)

            def m_sum(h):
                pe.wait_ge(m_g, h + 1)
                if h == 0:
                    pe.wait_ge(mix_a, 4)
                    pe.wait_ge(fill_read, 4)
                at = (h % 2) * SEQ
                g = g_m[:, h % 2, :]
                pe.matmul(bank[h // 2][:, at:at + DM + 1], g[:, 0:P], vm[:, 0, h, :], start=True, stop=True)
                dst = bank[2 + h // 2][:, at:at + DM + 1]
                pe.matmul(dst, g[:, P:SEQ], vm[:, 0, h, :], start=True, stop=False)
                pe.matmul(dst, g[:, SEQ:SW], vm[:, 1, h, :], start=False, stop=True).then_inc(m_num, 1)

            for h in range(HM + 1):
                if h < HM:
                    m_score(h)
                if h >= 1:
                    m_sum(h - 1)
            for h in range(HM):
                pe.wait_ge(m_out, 2 * h + 2)
                for t in range(T):
                    mm = pe.transpose(bank[4 + h][:, t * P:(t + 1) * P], om[:, t, h * DM:(h + 1) * DM], ident[:, :])
                mm.then_inc(m_turned, 1)
            pe.wait_ge(ld_wout, 16)
            pe.wait_ge(mix_a, 4)
            pe.wait_ge(mix_m, HM)
            for t in range(T):
                for c in range(2):
                    for k in range(KD):
                        mm = pe.matmul(bank[2 * t + c][:, :], mix_t[:, k, t * P:(t + 1) * P], wout[:, k, c * BANK:(c + 1) * BANK],
                                       start=(k == 0), stop=(k == KD - 1))
                    mm.then_inc(mixed, 1)
            for t in range(T):
                pe.wait_ge(h2_norm, t + 1)
                for i in range(2):
                    for k in range(4):
                        c = 4 * i + k
                        mm = pe.transpose(bank[4 + 2 * t + i][:, k * P:(k + 1) * P], hn[:, t, c * P:(c + 1) * P], ident[:, :])
                    mm.then_inc(h2_turned, 1)
            pe.wait_ge(ld_wr, 32)
            pe.wait_ge(h2_ready, 4)
            for t in range(T):
                for k in range(KD):
                    mm = pe.matmul(bank[4][:, t * NE:(t + 1) * NE], ht[:, k, t * P:(t + 1) * P], wr[:, k, :],
                                   start=(k == 0), stop=(k == KD - 1))
                mm.then_inc(logits, 1)
            pe.wait_ge(mask_ready, 1)
            pe.matmul(bank[5][:, 0:NE], before[:, :], mask[:, 0, :], start=True, stop=True)
            pe.wait_ge(mask_ready, 2)
            pe.matmul(bank[5][:, NE:2 * NE], ones[:, :], mask[:, 0, :], start=True, stop=False)
            pe.matmul(bank[5][:, NE:2 * NE], before[:, :], mask[:, 1, :], start=False, stop=True).then_inc(ranks, 1)
            pe.wait_ge(gates_ready, 2)
            for t in range(T):
                mm = pe.transpose(bank[6][0:NE, t * P:(t + 1) * P], gate[:, t, :], ident[:, :])
            mm.then_inc(gate_turned, 1)
            pe.wait_ge(pmax_ready, 1)
            pe.transpose(bank[5][0:1, 0:P], pmax[:, :], ident[:, :]).then_inc(pmax_turned, 1)

            def gather(g):
                pe.wait_ge(picked, g + 1)
                for k in range(KD):
                    for t in range(T):
                        mm = pe.matmul(bank[7][:, k * CAP:(k + 1) * CAP], hn[:, t, k * P:(k + 1) * P], pick[:, t, :],
                                       start=(t == 0), stop=(t == T - 1))
                mm.then_inc(gathered, 1)

            gather(0)
            pe.wait_ge(ld_bdn, 16)
            pe.wait_ge(bank6_read, 1)
            pe.wait_ge(x1_ready, 4)
            for t in range(T):
                for c in range(2):
                    mm = pe.matmul(bank[2 * t + c][:, :], gate_t[:, t * P:(t + 1) * P], bdn[:, c * BANK:(c + 1) * BANK],
                                   start=True, stop=False, skip_group_check=True)

            def expert(n, g, u, times):
                pe.wait_ge(xe_ready, g + 1)
                pe.wait_ge(gu_read, n + 1)
                pe.wait_ge(ld_brow[u], 16 * times + 16)
                for i in range(4):
                    h, c = i // 2, i % 2
                    mm = pe.matmul(bank[4 + h][c * CAP:(c + 1) * CAP, :], ones[32 * i:32 * i + 1, 0:CAP],
                                   brow[32 * i:32 * i + 1, u, :], start=True, stop=False, skip_group_check=True)
                mm.then_inc(brow_used, 1)
                for k in range(KD):
                    pe.wait_ge(ld_gu[u * KD + k], 16 * times + 16)
                    for h in range(2):
                        for c in range(2):
                            at = h * FF + c * BANK
                            mm = pe.matmul(bank[4 + h][c * CAP:(c + 1) * CAP, :], xe_t[:, k, :], gu[:, u, k, at:at + BANK],
                                           start=False, stop=(k == KD - 1), skip_group_check=True)
                    mm.then_inc(gu_used, 1)
                pe.wait_ge(pickg_ready, n + 1)
                pe.wait_ge(bank6_read, n + 1)
                for t in range(T):
                    mm = pe.transpose(bank[6][:, t * P:(t + 1) * P], pickg[:, t, :], ident[:, :])
                mm.then_inc(slots_turned, 1)
                gather(g + 1)
                pe.wait_ge(act_ready, n + 1)
                pe.wait_ge(slots_ready, n + 1)
                for k in range(4):
                    mm = pe.transpose(bank[6][:, k * P:(k + 1) * P], act[:, k * P:(k + 1) * P], ident[:, :])
                mm.then_inc(act_turned, 1)
                pe.wait_ge(act_t_ready, n + 1)
                for k in range(KD):
                    if k % 2 == 0:
                        pe.wait_ge(ld_d[k // 2], 16 * n + 16)
                    at = (k % 4) * P + (k // 4) * CAP
                    for c in range(2):
                        mm = pe.matmul(bank[6][c * CAP:(c + 1) * CAP, :], act_t[:, at:at + CAP], dn[:, k, c * BANK:(c + 1) * BANK],
                                       start=(k == 0), stop=(k == KD - 1), skip_group_check=True)
                    if k % 2:
                        mm.then_inc(d_used, 1)
                pe.wait_ge(bank6_read, n + 2)
                for t in range(T):
                    for c in range(2):
                        mm = pe.matmul(bank[2 * t + c][:, :], s_sb[c * CAP:(c + 1) * CAP, t * P:(t + 1) * P],
                                       y_sb[c * CAP:(c + 1) * CAP, :], start=False, stop=False, skip_group_check=True)
                mm.then_inc(y_spread, 1)

            with pe.Fori(0, NE // 2) as i:
                for u in range(2):
                    expert(2 * i + u, 2 * i + u, u, i)
            more = overflow(pe)
            with pe.If(more > 0):
                with pe.Fori(1, ROUNDS) as r:
                    gather(r * (NE + 1))
                    with pe.Fori(0, NE // 2) as i:
                        for u in range(2):
                            expert(r * NE + 2 * i + u, r * (NE + 1) + 2 * i + u, u, r * (NE // 2) + i)
            pe.wait_ge(y_spread, NE)
            pe.nop().then_inc(acc_final, 1)


_INS = ['x', 'norm1_g', 'w_in', 'q_norm_g', 'k_norm_g', 'conv_w', 'conv_b', 'w_mq', 'w_mk', 'b_igate', 'b_fgate',
        'mh_norm_g', 'w_out', 'norm2_g', 'w_router', 'b_router', 'w_gate_up', 'b_gate_up', 'w_down', 'b_down']


def kernel(**inputs):
    import concourse.bacc as _bacc
    from concourse.bass_utils import run_bass_kernel_spmd as _run

    nc = _bacc.Bacc("TRN2", target_bir_lowering=False, num_devices=1, dynamic_dma_scratch_size=1024)
    arrays, args = {}, []
    given = [(name, np.ascontiguousarray(inputs[name])) for name in _INS] + [("attn_bias", attention_bias())]
    for name, a in given:
        arrays[f"in_{name}"] = a
        args.append(nc.dram_tensor(f"in_{name}", a.shape, mybir.dt.from_np(a.dtype), kind="ExternalInput").ap())
    args.append(nc.dram_tensor("out", (1, SEQ, D), F32, kind="ExternalOutput").ap())
    layer_kernel(nc, *args)
    r = _run(nc, [arrays], core_ids=[0])
    return r.results[0]["out"]
```

```python
from contextlib import ExitStack

import numpy as np

import concourse.bass as bass
from concourse import mybir

F32 = mybir.dt.float32
BF16 = mybir.dt.bfloat16
I32 = mybir.dt.int32
U32 = mybir.dt.uint32
ALU = mybir.AluOpType
ACT = mybir.ActivationFunctionType
AX = mybir.AxisListType

P = 128
SEQ = 256
D = 1024
T = SEQ // P
KD = D // P
HALF = D // 2
BANK = 512
HA, DA = 8, 64
HM, DM = 4, 128
TAPS = 4
F_ROW = 32
NE, TOPK = 32, 4
FF = D
CAP = 64
ACC = (2, 3, 4, 5)
TURN = (0, 1, 6, 7)
ROUNDS = SEQ // CAP
LIMIT, ALPHA = 7.0, 1.702
EPS = 1e-6
MASKED = -1e30
NOWHERE = -1000.0
SW = P + SEQ
WINS = 4
R_G1, R_G2, R_MH, R_CB, R_CW, R_QG, R_KG, ROWS = 0, 8, 16, 20, 24, 40, 41, 42


def attention_bias():
    p = np.arange(P)[:, None]
    dist = np.concatenate([p - np.arange(P)[None], p + P - np.arange(SEQ)[None]], 1)
    count = np.zeros(dist.shape)
    for window, dil in ((128, 1), (512, 4), (2048, 16)):
        count += (dist >= 0) & (dist <= window) & (dist % dil == 0)
    slopes = 2.0 ** (-8.0 * np.arange(1, HA + 1) / HA)
    bias = np.where(count > 0, np.log(np.maximum(count, 1)), MASKED)[:, None, :] - slopes[None, :, None] * dist[:, None, :]
    return np.where(count[:, None, :] > 0, bias, MASKED).astype(np.float32)


def layer_kernel(nc, x, norm1_g, w_in, q_norm_g, k_norm_g, conv_w, conv_b, w_mq, w_mk, b_igate, b_fgate,
                 mh_norm_g, w_out, norm2_g, w_router, b_router, w_gate_up, b_gate_up, w_down, b_down,
                 attn_bias, out):
    with ExitStack() as ctx:
        def sb(name, shape, dt=F32):
            return ctx.enter_context(nc.sbuf_tensor(name, shape, dt))

        def sem(name):
            return ctx.enter_context(nc.semaphore(name))

        gu_ring = sb("gu_ring", [P, 2 * KD * 2 * FF])
        d_ring = sb("d_ring", [P, KD * D])
        gu = gu_ring[:, :].rearrange("p (u k n) -> p u k n", u=2, k=KD)
        dn = d_ring[:, :].rearrange("p (k n) -> p k n", k=KD)
        win = gu_ring[:, 0:WINS * KD * HALF].rearrange("p (b k n) -> p b k n", b=WINS, k=KD)
        wout = dn
        half = KD * 2 * FF
        place = [half]

        def in_second_half(words):
            at = place[0]
            place[0] += words
            assert place[0] <= 2 * half
            return gu_ring[:, at:at + words]

        bias_a = in_second_half(HA * SW).rearrange("p (h n) -> p h n", h=HA)
        qk_n = in_second_half(2 * T * HALF).rearrange("p (s t n) -> p s t n", s=2, t=T)
        qk_t = in_second_half(2 * 4 * SEQ).rearrange("p (s j n) -> p s j n", s=2, j=4)
        v_a = in_second_half(T * HALF).rearrange("p (t n) -> p t n", t=T)
        assert place[0] == half + 4 * 2 * FF
        PADW = SEQ + TAPS - 1
        xm = in_second_half(HM * PADW).rearrange("p (h n) -> p h n", h=HM)
        conv = in_second_half(HM * SEQ).rearrange("p (h n) -> p h n", h=HM)
        xc = in_second_half(HM * SEQ).rearrange("p (h n) -> p h n", h=HM)
        vm = in_second_half(T * HM * (DM + 1)).rearrange("p (t h n) -> p t h n", t=T, h=HM)
        qm_t = in_second_half(HM * SEQ).rearrange("p (h n) -> p h n", h=HM)
        km_t = in_second_half(HM * SEQ).rearrange("p (h n) -> p h n", h=HM)
        wmq = in_second_half(HM * DM).rearrange("p (h n) -> p h n", h=HM)
        wmk = in_second_half(HM * DM).rearrange("p (h n) -> p h n", h=HM)
        sig_c = km_t

        xres = sb("xres", [P, T, D])
        hn = sb("hn", [P, T, D])
        hn_flat = hn[:, :, :].rearrange("p t n -> p (t n)")
        e_m = hn_flat[:, 0:HM * SW].rearrange("p (h n) -> p h n", h=HM)
        parts = sb("parts", [P, T, 3, D], BF16)
        sel = hn_flat[0:HM, 4 * SW:4 * SW + HM * P].rearrange("p (h n) -> p h n", h=HM)
        ht = sb("ht", [P, KD, SEQ])
        ht_flat = ht[:, :, :].rearrange("p k n -> p (k n)")
        xe_t = ht_flat[:, 0:BANK].rearrange("p (k n) -> p k n", k=KD)
        act_t = ht_flat[:, BANK:2 * BANK]
        y_sb = ht_flat[:, 2 * BANK:3 * BANK]
        s_sb = ht_flat[:, 3 * BANK:4 * BANK].rearrange("p (b n) -> p b n", b=2)
        mix_t = sb("mix_t", [P, KD, SEQ])
        mix_flat = mix_t[:, :, :].rearrange("p k n -> p (k n)")
        rows_i, rows_f, rows_l, rows_b, ones_r = (mix_flat[0:HM, i * SEQ:(i + 1) * SEQ] for i in range(5))
        gate_c, sig_g, up_c, act = (mix_flat[:, i * BANK:(i + 1) * BANK] for i in range(4))
        attn_tmp = sb("attn_tmp", [P, 4 * SW])
        p_a = attn_tmp[:, 0:2 * SW].rearrange("p (b n) -> p b n", b=2)
        pt_a = attn_tmp[:, 2 * SW:4 * SW].rearrange("p (b n) -> p b n", b=2)
        sq = attn_tmp[:, 0:2 * HALF].rearrange("p (b n) -> p b n", b=2)
        sq_x = attn_tmp[:, 0:D]
        brow = attn_tmp[:, 0:2 * BANK].rearrange("p (u n) -> p u n", u=2)
        om = sb("om", [P, T, HALF])
        bdn = om[0:NE, :, :].rearrange("p t n -> p (t n)")
        eps = sb("eps", [P, 1])
        qkg = sb("qkg", [P, 2])
        rows_a = sb("rows_a", [HM, SEQ])
        ident = sb("ident", [P, P])
        ones = sb("ones", [P, P])
        before = sb("before", [P, P])
        slot = sb("slot", [P, 2 * CAP])
        slot_i = sb("slot_i", [P, 2 * CAP], I32)
        expert_no = slot[:, 0:NE]
        vec = sb("vec", [P, ROWS])
        bif = sb("bif", [HM, 2])
        early = parts[:, :, :, :].rearrange("p t i n -> p (t i n)").bitcast(F32)
        wif = early[:, 0:KD * (F_ROW + HM)].rearrange("p (k n) -> p k n", k=KD)
        vec_r = early[0:ROWS, KD * (F_ROW + HM):KD * (F_ROW + HM) + P]
        wr = sb("wr", [P, KD, NE])
        br = sb("br", [P, NE])
        ss1 = sb("ss1", [P, T])
        rs1 = sb("rs1", [P, T])
        ssqk = sb("ssqk", [P, 2, T, HA])
        rsqk = sb("rsqk", [P, 2, T, HA])
        mx = sb("mx", [P, HA, T])
        nmx = sb("nmx", [P, HA, T])
        den = sb("den", [P, HA, T])
        rden = sb("rden", [P, HA, T])
        acol = sb("acol", [P, 2, T, HM])
        em = sb("em", [P, T, HM])
        dm = sb("dm", [P, T, HM])
        rm = sb("rm", [P, T, HM])
        ssm = sb("ssm", [P, T, HM])
        rsm = sb("rsm", [P, T, HM])
        ss2h = sb("ss2h", [P, T, 2])
        ss2 = sb("ss2", [P, T])
        rs2 = sb("rs2", [P, T])
        lg = sb("lg", [P, T, NE])
        top_v = sb("top_v", [P, T, 8])
        top_i = sb("top_i", [P, T, 8], U32)
        top_f = sb("top_f", [P, T, TOPK])
        nv0 = sb("nv0", [P, T])
        gate4 = sb("gate4", [P, T, TOPK])
        gsum = sb("gsum", [P, T])
        eq, eqg = (mix_flat[:, i * T * TOPK * NE:(i + 1) * T * TOPK * NE].rearrange("p (t j e) -> p t j e", t=T, j=TOPK)
                   for i in range(2))
        mask = sb("mask", [P, T, NE])
        gate = sb("gate", [P, T, NE])
        gate_t = attn_tmp[0:NE, 2 * BANK:2 * BANK + SEQ]
        pos = sb("pos", [P, T, NE + 1])
        pmax = sb("pmax", [P, 1])
        pm1 = sb("pm1", [1, 1])
        flag = sb("flag", [1, 1], I32)
        pick = sb("pick", [P, T, CAP], BF16)
        pickg = attn_tmp[:, 2 * BANK + SEQ:3 * BANK].rearrange("p (t n) -> p t n", t=T)

        bank = [ctx.enter_context(nc.psum_tensor(f"bank{i}", [P, BANK], F32)) for i in range(8)]

        ld_x = [sem(f"ld_x{t}") for t in range(T)]
        ld_vec = sem("ld_vec")
        ld_small = sem("ld_small")
        ld_wif = sem("ld_wif")
        ld_wr = sem("ld_wr")
        ld_win = [sem(f"ld_win{b}") for b in range(6)]
        ld_bias_a = sem("ld_bias_a")
        ld_wm = sem("ld_wm")
        ld_wout = sem("ld_wout")
        ld_bdn = sem("ld_bdn")
        ld_gu = [sem(f"ld_gu{i}") for i in range(2 * KD)]
        ld_d = [sem(f"ld_d{i}") for i in range(4)]
        ld_brow = [sem(f"ld_brow{i}") for i in range(2)]
        pool_step = sem("pool_step")
        consts = sem("consts")
        dve_step = sem("dve_step")
        act_step = sem("act_step")
        x_ms = sem("x_ms")
        x_rs = sem("x_rs")
        x_norm = sem("x_norm")
        x_turned = sem("x_turned")
        h_ready = sem("h_ready")
        vec_turned = sem("vec_turned")
        vec_ready = sem("vec_ready")
        eps_ready = sem("eps_ready")
        win_used = sem("win_used")
        z_q = sem("z_q")
        z_xm = sem("z_xm")
        z_if = sem("z_if")
        z_v = sem("z_v")
        z_fill = sem("z_fill")
        fill_read = sem("fill_read")
        qk_sq = sem("qk_sq")
        qk_ms = sem("qk_ms")
        qk_rs = sem("qk_rs")
        qk_norm = sem("qk_norm")
        qk_turned = sem("qk_turned")
        qk_ready = sem("qk_ready")
        xm_read = sem("xm_read")
        conv_ready = sem("conv_ready")
        conv_sig = sem("conv_sig")
        xc_ready = sem("xc_ready")
        f_neg = sem("f_neg")
        f_log = sem("f_log")
        if_read = sem("if_read")
        rows_ready = sem("rows_ready")
        cols_turned = sem("cols_turned")
        cols_ready = sem("cols_ready")
        em_ready = sem("em_ready")
        v_read = sem("v_read")
        scores = sem("scores")
        s_max = sem("s_max")
        s_exp = sem("s_exp")
        p_ready = sem("p_ready")
        p_turned = sem("p_turned")
        pt_ready = sem("pt_ready")
        o_ready = sem("o_ready")
        mix_a = sem("mix_a")
        om_sig = sem("om_sig")
        qkm = sem("qkm")
        qkm_read = sem("qkm_read")
        m_scores = sem("m_scores")
        a_spread = sem("a_spread")
        wif_zero = sem("wif_zero")
        hi_ready = sem("hi_ready")
        mid_ready = sem("mid_ready")
        lo_ready = sem("lo_ready")
        rest_1 = sem("rest_1")
        rest_2 = sem("rest_2")
        m_arg1 = sem("m_arg1")
        m_arg = sem("m_arg")
        m_exp = sem("m_exp")
        m_sel = sem("m_sel")
        m_g = sem("m_g")
        m_num = sem("m_num")
        m_ss = sem("m_ss")
        den_read = sem("den_read")
        m_ms = sem("m_ms")
        m_rs = sem("m_rs")
        m_out = sem("m_out")
        m_turned = sem("m_turned")
        mix_m = sem("mix_m")
        mixed = sem("mixed")
        x1_ready = sem("x1_ready")
        x1_ss = sem("x1_ss")
        x1_rs = sem("x1_rs")
        ss2_sum = sem("ss2_sum")
        h2_norm = sem("h2_norm")
        h2_turned = sem("h2_turned")
        h2_ready = sem("h2_ready")
        logits = sem("logits")
        top_max = sem("top_max")
        top_ready = sem("top_ready")
        top_exp = sem("top_exp")
        mask_ready = sem("mask_ready")
        gates_ready = sem("gates_ready")
        ranks = sem("ranks")
        gate_turned = sem("gate_turned")
        bank6_read = sem("bank6_read")
        pmax_ready = sem("pmax_ready")
        pmax_turned = sem("pmax_turned")
        flag_ready = sem("flag_ready")
        picked = sem("picked")
        pickg_ready = sem("pickg_ready")
        gathered = sem("gathered")
        xe_ready = sem("xe_ready")
        gu_used = sem("gu_used")
        brow_used = sem("brow_used")
        gu_read = sem("gu_read")
        gate_cut = sem("gate_cut")
        sig_ready = sem("sig_ready")
        act_half = sem("act_half")
        moved = sem("moved")
        act_ready = sem("act_ready")
        slots_turned = sem("slots_turned")
        slots_ready = sem("slots_ready")
        act_turned = sem("act_turned")
        act_t_ready = sem("act_t_ready")
        d_used = sem("d_used")
        y_spread = sem("y_spread")
        acc_final = sem("acc_final")
        x_final = sem("x_final")
        stored = sem("stored")

        w_in0 = w_in[0].rearrange("(k p) n -> p k n", p=P)
        BLOCKS = [0, HALF, 3 * HALF, 2 * HALF, 4 * HALF, 5 * HALF]

        def overflow(eng):
            eng.wait_ge(flag_ready, 1)
            return eng.value_load(flag[0:1, 0:1], min_val=0, max_val=1)

        block = ctx.enter_context(nc.Block())

        @block.sync
        def _(sp):
            def load_gu(e, u, k):
                sp.dma_start(gu[:, u, k, :], w_gate_up[0, e, k * P:(k + 1) * P, :]).then_inc(ld_gu[u * KD + k], 16)

            def load_brow(e, u):
                sp.dma_start(brow[0:97:32, u, :], b_gate_up[0, e, :].rearrange("(i n) -> i n", n=BANK)).then_inc(ld_brow[u], 16)

            def load_d(e, j):
                sp.dma_start(dn[:, 2 * j:2 * j + 2, :],
                             w_down[0, e, 2 * j * P:2 * (j + 1) * P, :].rearrange("(c p) n -> p c n", p=P)).then_inc(ld_d[j], 16)

            def load_win(b):
                sp.dma_start(win[:, b % WINS, :, :], w_in0[:, :, BLOCKS[b]:BLOCKS[b] + HALF]).then_inc(ld_win[b], 16)

            sp.dma_start(vec_r[R_G1:R_G1 + KD, :], norm1_g[0].rearrange("(k n) -> k n", n=P)).then_inc(ld_vec, 16)
            for t in range(T):
                sp.dma_start(xres[:, t, :], x[0, t * P:(t + 1) * P, :]).then_inc(ld_x[t], 16)
            sp.dma_start(vec_r[R_G2:R_G2 + KD, :], norm2_g[0].rearrange("(k n) -> k n", n=P)).then_inc(ld_vec, 16)
            sp.dma_start(vec_r[R_MH:R_MH + HM, :], mh_norm_g[0]).then_inc(ld_vec, 16)
            for r, g in ((R_QG, q_norm_g), (R_KG, k_norm_g)):
                for i in range(2):
                    sp.dma_start(vec_r[r:r + 1, i * DA:(i + 1) * DA], g).then_inc(ld_vec, 16)
            load_win(0)
            load_win(1)
            load_win(2)
            sp.wait_ge(wif_zero, 1)
            for c, at in ((0, 0), (HM, F_ROW)):
                sp.dma_start(wif[:, :, at:at + HM], w_in0[:, :, 6 * HALF + c:6 * HALF + c + HM]).then_inc(ld_wif, 16)
            load_win(3)
            sp.dma_start(bias_a, attn_bias).then_inc(ld_bias_a, 16)
            sp.dma_start(wmq, w_mq[0].rearrange("h d e -> d h e")).then_inc(ld_wm, 16)
            sp.dma_start(wmk, w_mk[0].rearrange("h d e -> d h e")).then_inc(ld_wm, 16)
            sp.dma_start(wr[:, :, :], w_router[0].rearrange("(k p) n -> p k n", p=P)).then_inc(ld_wr, 16)
            sp.dma_start(br[:, :], b_router[0:1, :].broadcast_to([P, NE])).then_inc(ld_wr, 16)
            sp.dma_start(wout, w_out[0].rearrange("(k p) n -> p k n", p=P)).then_inc(ld_wout, 16)
            for b in (4, 5):
                sp.wait_ge(win_used, b - WINS + 1)
                load_win(b)
            for b, used in ((2, 3), (3, 4), (0, 5), (1, 6)):
                sp.wait_ge(win_used, used)
                load_gu(0, 0, 2 * b)
                load_gu(0, 0, 2 * b + 1)
            sp.wait_ge(mix_a, 4)
            for k in range(4):
                load_gu(1, 1, k)
            load_brow(0, 0)
            load_brow(1, 1)
            sp.wait_ge(m_num, HM)
            for k in range(4, KD):
                load_gu(1, 1, k)
            sp.wait_ge(mix_m, HM)
            sp.dma_start(bdn, b_down[0]).then_inc(ld_bdn, 16)
            sp.wait_ge(mixed, 4)
            for j in range(4):
                load_d(0, j)

            def weights(base):
                def next_gu(n, e, u):
                    sp.wait_ge(brow_used, n - 1)
                    load_brow(e, u)
                    for k in range(KD):
                        sp.wait_ge(gu_used, KD * (n - 2) + k + 1)
                        load_gu(e, u, k)

                def next_d(n, e):
                    for j in range(4):
                        sp.wait_ge(d_used, 4 * (n - 1) + j + 1)
                        load_d(e, j)

                with sp.Fori(0, NE // 2 - 1) as i:
                    for u in range(2):
                        e = 2 * i + 2 + u
                        next_gu(base + e, e, u)
                        next_d(base + e - 1, e - 1)
                next_d(base + NE - 1, NE - 1)

            weights(0)
            more = overflow(sp)
            with sp.If(more > 0):
                with sp.Fori(1, ROUNDS) as r:
                    base = r * NE
                    for u in range(2):
                        sp.wait_ge(brow_used, base + u - 1)
                        load_brow(u, u)
                        for k in range(KD):
                            sp.wait_ge(gu_used, KD * (base + u - 2) + k + 1)
                            load_gu(u, u, k)
                    for j in range(4):
                        sp.wait_ge(d_used, 4 * (base - 1) + j + 1)
                        load_d(0, j)
                    weights(base)
            for t in range(T):
                for c in range(2):
                    sp.wait_ge(x_final, 2 * t + c + 1)
                    sp.dma_start(out[0, t * P:(t + 1) * P, c * BANK:(c + 1) * BANK],
                                 xres[:, t, c * BANK:(c + 1) * BANK]).then_inc(stored, 16)
            sp.wait_ge(stored, 16 * 2 * T)

        @block.gpsimd
        def _(pool):
            pool.memset(wif, 0.0).then_inc(wif_zero, 1)
            pool.memset(ident[:, :], 0.0).then_inc(pool_step, 1)
            pool.memset(ones[:, :], 1.0).then_inc(pool_step, 1)
            pool.iota(slot_i[:, :].rearrange("p (d n) -> p d n", d=2), pattern=[[0, 2], [1, CAP]], base=0,
                      channel_multiplier=0).then_inc(pool_step, 1)
            pool.wait_ge(pool_step, 3)
            pool.affine_select(out=ident[:, :], in_=ident[:, :], compare_op=ALU.not_equal, fill=1.0, base=0,
                               pattern=[[-1, P]], channel_multiplier=1).then_inc(consts, 1)
            pool.affine_select(out=before[:, :], in_=ones[:, :], compare_op=ALU.is_gt, fill=0.0, base=0,
                               pattern=[[1, P]], channel_multiplier=-1).then_inc(consts, 1)
            pool.tensor_copy(slot[:, :], slot_i[:, :]).then_inc(consts, 1)
            pool.memset(xm[:, :, 0:TAPS - 1], 0.0).then_inc(consts, 1)
            pool.memset(vm[:, :, :, DM:DM + 1], 1.0).then_inc(consts, 1)
            pool.memset(ones_r, 1.0).then_inc(consts, 1)
            pool.memset(pos[:, :, NE:NE + 1], NOWHERE).then_inc(consts, 1)
            pool.wait_ge(x_turned, 4)
            pool.memset(sel, 0.0).then_inc(pool_step, 1)
            pool.wait_ge(pool_step, 4)
            pool.affine_select(out=sel, in_=sel, compare_op=ALU.not_equal, fill=1.0, base=0,
                               pattern=[[-1, HM], [0, P]], channel_multiplier=1).then_inc(consts, 1)
            for h in range(HM):
                pool.wait_ge(m_exp, h + 1)
                diag = e_m[:, h, :].rearrange("p (b n) -> p b n", b=3)[:, 0:3:2, :]
                pool.affine_select(out=diag, in_=diag, compare_op=ALU.is_ge, fill=0.0, base=0,
                                   pattern=[[0, 2], [1, P]], channel_multiplier=-1).then_inc(m_sel, 1)
            for t in range(T):
                pool.wait_ge(hi_ready, t + 1)
                pool.wait_ge(h2_turned, 2 * t + 2)
                pool.tensor_tensor(hn[:, t, :], hn[:, t, :], parts[:, t, 0, :], ALU.subtract).then_inc(rest_1, 1)
                pool.wait_ge(mid_ready, t + 1)
                pool.tensor_tensor(hn[:, t, :], hn[:, t, :], parts[:, t, 1, :], ALU.subtract).then_inc(rest_2, 1)

        @block.scalar
        def _(act_e):
            act = act_e
            act.dma_start(vec_r[R_CB:R_CB + HM, :], conv_b[0].rearrange("(k n) -> k n", n=P)).then_inc(ld_vec, 16)
            act.dma_start(vec_r[R_CW:R_CW + TAPS * HM, :], conv_w[0].rearrange("j (k n) -> (j k) n", n=P)).then_inc(ld_vec, 16)
            act.dma_start(bif[:, 0:1], b_igate[0].rearrange("(h o) -> h o", o=1)).then_inc(ld_small, 16)
            act.dma_start(bif[:, 1:2], b_fgate[0].rearrange("(h o) -> h o", o=1)).then_inc(ld_small, 16)
            act.preload_act_table_set("natural_log_exp_and_others")

            for t in range(T):
                act.wait_ge(ld_x[t], 16)
                if t:
                    act.wait_ge(x_ms, t)
                act.activation(sq_x, xres[:, t, :], ACT.Square, accum_out=ss1[:, t:t + 1]).then_inc(x_ms, 1)
                act.wait_ge(x_ms, t + 1)
                act.wait_ge(eps_ready, 1)
                act.activation(rs1[:, t:t + 1], ss1[:, t:t + 1], ACT.Ln, scale=1.0 / D, bias=eps[:, 0:1]).then_inc(act_step, 1)
                act.wait_ge(act_step, t + 1)
                act.activation(rs1[:, t:t + 1], rs1[:, t:t + 1], ACT.Exp, scale=-0.5).then_inc(x_rs, 1)
            for s in range(2):
                for t in range(T):
                    n = 2 * s + t
                    act.wait_ge(z_q, n + 1)
                    if n == 0:
                        act.wait_ge(x_ms, T)
                    if n >= 2:
                        act.wait_ge(qk_ms, n - 1)
                    act.activation(sq[:, t, :], bank[n][:, :], ACT.Square).then_inc(qk_sq, 1)
            for s in range(2):
                act.wait_ge(qk_ms, 2 * s + 2)
                act.activation(rsqk[:, s], ssqk[:, s], ACT.Ln, scale=1.0 / DA, bias=eps[:, 0:1]).then_inc(act_step, 1)
                act.wait_ge(act_step, 3 + s)
                act.activation(rsqk[:, s], rsqk[:, s], ACT.Exp, scale=-0.5).then_inc(qk_rs, 1)
            for i in range(2):
                act.wait_ge(z_xm, i + 1)
                if i == 0:
                    act.wait_ge(consts, 7)
                act.activation(xm[:, 2 * i:2 * i + 2, TAPS - 1:PADW], bank[6 + i][:, :].rearrange("p (h n) -> p h n", h=2),
                               ACT.Copy).then_inc(xm_read, 1)
            act.wait_ge(f_neg, 1)
            act.activation(rows_l, rows_l, ACT.Exp).then_inc(act_step, 1)
            act.wait_ge(act_step, 5)
            act.activation(rows_l, rows_l, ACT.Ln, bias=1.0).then_inc(f_log, 1)
            act.wait_ge(conv_ready, HM)
            act.activation(sig_c, conv, ACT.Sigmoid).then_inc(conv_sig, 1)
            act.preload_act_table_set("natural_log_exp_and_others")
            for n in range(4):
                act.wait_ge(qk_turned, n + 1)
                s, i = n // 2, n % 2
                act.activation(qk_t[:, s, 2 * i:2 * i + 2, :], bank[2 + n][:, :].rearrange("p (j n) -> p j n", j=2),
                               ACT.Copy, scale=qkg[:, s:s + 1]).then_inc(qk_ready, 1)
            act.wait_ge(z_v, 2)
            for t in range(T):
                act.activation(v_a[:, t, :], bank[t][:, :], ACT.Copy).then_inc(v_read, 1)

            def turned_p(h):
                act.wait_ge(p_turned, h + 1)
                if h >= 2:
                    act.wait_ge(o_ready, h - 1)
                act.activation(pt_a[:, h % 2, :], bank[4 + h % 2][:, 0:SW], ACT.Copy).then_inc(pt_ready, 1)

            def mixed_a(j):
                act.wait_ge(o_ready, 2 * j + 2)
                if j == 0:
                    act.wait_ge(cols_turned, 1)
                act.activation(mix_t[:, j, :], bank[2 + j % 2][:, (j // 2) * SEQ:(j // 2 + 1) * SEQ], ACT.Copy).then_inc(mix_a, 1)

            for h in range(HA + 2):
                if h < HA:
                    act.wait_ge(s_max, h + 1)
                    for t in range(T):
                        lo, hi = (0, P) if t == 0 else (P, SW)
                        act.activation(p_a[:, h % 2, lo:hi], p_a[:, h % 2, lo:hi], ACT.Exp, bias=nmx[:, h, t:t + 1],
                                       accum_out=den[:, h, t:t + 1]).then_inc(s_exp, 1)
                if 1 <= h <= HA:
                    turned_p(h - 1)
                if h in (3, 5, 7, 9):
                    mixed_a((h - 3) // 2)
                if h >= 2 and h % 2 == 0 and h <= 8:
                    n = h // 2 - 1
                    act.wait_ge(z_fill, n + 1)
                    if n < 2:
                        act.activation(vm[:, n, :, 0:DM], bank[n][:, :].rearrange("p (h n) -> p h n", h=HM),
                                       ACT.Copy).then_inc(fill_read, 1)
                    else:
                        act.activation(om[:, n - 2, :], bank[n - 2][:, :], ACT.Copy).then_inc(fill_read, 1)
                if h == 1:
                    act.wait_ge(cols_ready, 1)
                    act.activation(em[:, :, :], acol[:, 1], ACT.Exp).then_inc(em_ready, 1)
                if h == 2:
                    for m in range(HM):
                        act.wait_ge(m_arg, m + 1)
                        act.activation(e_m[:, m, :], e_m[:, m, :], ACT.Exp, scale=-1.0).then_inc(m_exp, 1)
                if h in (3, 4):
                    dst = (qm_t, km_t)[h - 3]
                    for i in range(2):
                        act.wait_ge(qkm, 2 * (h - 3) + i + 1)
                        act.activation(dst[:, 2 * i:2 * i + 2, :], bank[6 + i][:, :].rearrange("p (h n) -> p h n", h=2),
                                       ACT.Copy).then_inc(qkm_read, 1)
            for h in range(HM):
                act.wait_ge(den_read, T * HM)
                for t in range(T):
                    src = bank[6 * t + h // 2][:, (h % 2) * SEQ:(h % 2) * SEQ + DM]
                    if h + t:
                        act.wait_ge(m_ss, 2 * h + t)
                    act.activation(attn_tmp[:, 2 * BANK:2 * BANK + DM], src, ACT.Square, accum_out=ssm[:, t, h:h + 1]).then_inc(m_ss, 1)
            act.wait_ge(m_ms, 1)
            act.activation(rsm[:, :, :], ssm[:, :, :], ACT.Ln, scale=1.0 / DM, bias=eps[:, 0:1]).then_inc(act_step, 1)
            act.wait_ge(act_step, 6)
            act.activation(rsm[:, :, :], rsm[:, :, :], ACT.Exp, scale=-0.5).then_inc(m_rs, 1)
            act.wait_ge(fill_read, 4)
            act.activation(om[:, :, :], om[:, :, :], ACT.Sigmoid).then_inc(om_sig, 1)
            act.preload_act_table_set("natural_log_exp_and_others")
            for h in range(HM):
                act.wait_ge(m_turned, h + 1)
                act.activation(mix_t[:, 4 + h, :], bank[TURN[h]][:, 0:SEQ], ACT.Copy,
                               scale=vec[:, R_MH + h:R_MH + h + 1]).then_inc(mix_m, 1)
            def part(i, t):
                if i == 0:
                    act.wait_ge(h2_norm, t + 1)
                else:
                    act.wait_ge((rest_1, rest_2)[i - 1], t + 1)
                act.activation(parts[:, t, i, :], hn[:, t, :], ACT.Copy).then_inc((hi_ready, mid_ready, lo_ready)[i], 1)

            for t in range(T):
                for c in range(2):
                    act.wait_ge(x1_ready, 2 * t + c + 1)
                    if t + c == 0:
                        act.wait_ge(mix_m, HM)
                    if t:
                        act.wait_ge(x1_ss, c + 1)
                    act.activation(bank[6 + c][:, :], xres[:, t, c * BANK:(c + 1) * BANK], ACT.Square,
                                   accum_out=ss2h[:, t, c:c + 1]).then_inc(x1_ss, 1)
                act.wait_ge(ss2_sum, t + 1)
                act.activation(rs2[:, t:t + 1], ss2[:, t:t + 1], ACT.Ln, scale=1.0 / D, bias=eps[:, 0:1]).then_inc(act_step, 1)
                act.wait_ge(act_step, 7 + t)
                act.activation(rs2[:, t:t + 1], rs2[:, t:t + 1], ACT.Exp, scale=-0.5).then_inc(x1_rs, 1)
                if t == 0:
                    part(0, 0)
            part(0, 1)
            part(1, 0)
            part(2, 0)
            for t in range(T):
                act.wait_ge(top_ready, 1)
                act.activation(gate4[:, t, :], top_v[:, t, 0:TOPK], ACT.Exp, bias=nv0[:, t:t + 1],
                               accum_out=gsum[:, t:t + 1]).then_inc(top_exp, 1)
            part(1, 1)
            part(2, 1)
            act.wait_ge(gate_turned, 1)
            act.activation(gate_t, bank[6][0:NE, 0:SEQ], ACT.Copy).then_inc(bank6_read, 1)

            def expert(n, u):
                act.wait_ge(slots_turned, n + 1)
                act.activation(s_sb[:, u, :], bank[6][:, 0:SEQ], ACT.Copy).then_inc(slots_ready, 1)
                act.wait_ge(gate_cut, n + 1)
                act.activation(sig_g, gate_c, ACT.Sigmoid, scale=ALPHA).then_inc(sig_ready, 1)
                act.wait_ge(act_turned, n + 1)
                act.activation(act_t, bank[6][:, :], ACT.Copy).then_inc(act_t_ready, 1)
                act.wait_ge(d_used, 4 * n + 4)
                act.wait_ge(y_spread, n + 1)
                act.activation(y_sb, bank[6][:, :], ACT.Copy).then_inc(bank6_read, 1)

            with act.Fori(0, NE // 2) as i:
                for u in range(2):
                    expert(2 * i + u, u)
            more = overflow(act)
            with act.If(more > 0):
                with act.Fori(NE // 2, ROUNDS * NE // 2) as i:
                    for u in range(2):
                        expert(2 * i + u, u)

        @block.vector
        def _(dve):
            steps = [0]

            def step(ins):
                steps[0] += 1
                ins.then_inc(dve_step, 1)

            def settle():
                dve.wait_ge(dve_step, steps[0])

            dve.memset(eps[:, :], EPS).then_inc(eps_ready, 1)
            for t in range(T):
                dve.wait_ge(x_rs, t + 1)
                dve.tensor_scalar(hn[:, t, :], xres[:, t, :], rs1[:, t:t + 1], None, ALU.mult).then_inc(x_norm, 1)
            dve.wait_ge(vec_turned, 1)
            step(dve.tensor_copy(vec[:, :], bank[0][:, 0:ROWS]))
            settle()
            step(dve.tensor_scalar(qkg[:, 0:1], vec[:, R_QG:R_QG + 1], float(DA) ** -0.5, None, ALU.mult))
            dve.tensor_copy(qkg[:, 1:2], vec[:, R_KG:R_KG + 1]).then_inc(vec_ready, 1)
            for t in range(T):
                for i in range(2):
                    dve.wait_ge(x_turned, 2 * t + i + 1)
                    dve.tensor_tensor(ht[:, 4 * i:4 * i + 4, t * P:(t + 1) * P],
                                      bank[4 + 2 * t + i][:, :].rearrange("p (k n) -> p k n", k=4),
                                      vec[:, R_G1 + 4 * i:R_G1 + 4 * i + 4].unsqueeze(2).broadcast_to([P, 4, P]),
                                      ALU.mult).then_inc(h_ready, 1)
            for s in range(2):
                for t in range(T):
                    dve.wait_ge(qk_sq, 2 * s + t + 1)
                    dve.tensor_reduce(ssqk[:, s, t, :], sq[:, t, :].rearrange("p (h n) -> p h n", h=HA), AX.X,
                                      ALU.add).then_inc(qk_ms, 1)
                if s == 0:
                    continue
                for s2 in range(2):
                    dve.wait_ge(qk_rs, s2 + 1)
                    for t in range(T):
                        dve.tensor_tensor(qk_n[:, s2, t, :].rearrange("p (h n) -> p h n", h=HA),
                                          bank[2 * s2 + t][:, :].rearrange("p (h n) -> p h n", h=HA),
                                          rsqk[:, s2, t, :].unsqueeze(2).broadcast_to([P, HA, DA]),
                                          ALU.mult).then_inc(qk_norm, 1)
            dve.wait_ge(z_if, 1)
            dve.wait_ge(ld_small, 32)
            dve.wait_ge(consts, 7)
            step(dve.tensor_copy(rows_f, bank[4][F_ROW:F_ROW + HM, 0:SEQ]))
            settle()
            step(dve.tensor_scalar(rows_f, rows_f, bif[:, 1:2], None, ALU.add))
            step(dve.tensor_scalar(rows_i, bank[4][0:HM, 0:SEQ], bif[:, 0:1], None, ALU.add))
            settle()
            dve.scalar_tensor_tensor(out=rows_l, in0=rows_f, scalar=-1.0, in1=rows_f, op0=ALU.mult, op1=ALU.min).then_inc(f_neg, 1)
            dve.wait_ge(xm_read, 2)
            for j in range(TAPS):
                for h in range(HM):
                    tap = vec[:, R_CW + j * HM + h:R_CW + j * HM + h + 1]
                    if j == 0:
                        step(dve.tensor_scalar(conv[:, h, :], xm[:, h, 0:SEQ], tap, vec[:, R_CB + h:R_CB + h + 1],
                                               ALU.mult, ALU.add))
                    else:
                        ins = dve.scalar_tensor_tensor(out=conv[:, h, :], in0=xm[:, h, j:j + SEQ], scalar=tap,
                                                       in1=conv[:, h, :], op0=ALU.mult, op1=ALU.add)
                        if j < TAPS - 1:
                            step(ins)
                        else:
                            ins.then_inc(conv_ready, 1)
                if j < TAPS - 1:
                    settle()
            dve.wait_ge(f_log, 1)
            step(dve.scalar_tensor_tensor(out=rows_f, in0=rows_f, scalar=0.0, in1=rows_l, op0=ALU.min, op1=ALU.subtract))
            settle()
            step(dve.tensor_tensor_scan(rows_b, ones_r, rows_f, 0.0, ALU.mult, ALU.add))
            settle()
            step(dve.tensor_tensor(rows_i, rows_i, rows_b, ALU.subtract))
            settle()
            step(dve.tensor_tensor_scan(rows_a[:, :], ones_r, rows_i, 0.0, ALU.mult, ALU.max))
            settle()
            dve.scalar_tensor_tensor(out=rows_l, in0=rows_b, scalar=-1.0, in1=rows_a[:, :], op0=ALU.mult,
                                     op1=ALU.subtract).then_inc(rows_ready, 1)

            def softmax(h):
                dve.wait_ge(scores, h + 1)
                if h == 0:
                    dve.wait_ge(ld_bias_a, 16)
                if h >= 2:
                    dve.wait_ge(p_turned, h - 1)
                for t in range(T):
                    lo, hi = (0, P) if t == 0 else (P, SW)
                    step(dve.tensor_tensor_reduce(out=p_a[:, h % 2, lo:hi], in0=bank[4 + h % 2][:, lo:hi],
                                                  in1=bias_a[:, h, lo:hi], scale=1.0, scalar=MASKED, op0=ALU.add,
                                                  op1=ALU.max, accum_out=mx[:, h, t:t + 1]))
                settle()
                dve.tensor_scalar(nmx[:, h, :], mx[:, h, :], -1.0, None, ALU.mult).then_inc(s_max, 1)

            def normalise(h):
                dve.wait_ge(s_exp, 2 * h + 2)
                step(dve.reciprocal(rden[:, h, :], den[:, h, :]))
                settle()
                for t in range(T):
                    lo, hi = (0, P) if t == 0 else (P, SW)
                    dve.tensor_scalar(p_a[:, h % 2, lo:hi], p_a[:, h % 2, lo:hi], rden[:, h, t:t + 1], None,
                                      ALU.mult).then_inc(p_ready, 1)

            def decay(h):
                a_bc = bank[6 + h // 2][:, (h % 2) * SEQ:(h % 2 + 1) * SEQ]
                dve.tensor_scalar(e_m[:, h, 0:SEQ], a_bc, acol[:, 0, 0, h:h + 1], 0.0, ALU.subtract, ALU.max)\
                    .then_inc(m_arg1, 1)
                dve.wait_ge(m_arg1, h + 1)
                dve.tensor_scalar(e_m[:, h, SEQ:SW], a_bc[:, P:SEQ], acol[:, 0, 1, h:h + 1], 0.0,
                                  ALU.subtract, ALU.max).then_inc(m_arg, 1)

            def weighed(h):
                dve.wait_ge(m_scores, h + 1)
                dve.wait_ge(m_sel, h + 1)
                dve.scalar_tensor_tensor(out=e_m[:, h, :], in0=bank[6 + h % 2][:, 0:SW], scalar=float(DM) ** -0.5,
                                         in1=e_m[:, h, :], op0=ALU.mult, op1=ALU.mult).then_inc(m_g, 1)

            for h in range(HA + 1):
                if h < HA:
                    softmax(h)
                if h == 0:
                    dve.wait_ge(cols_turned, 1)
                    dve.tensor_copy(acol[:, :, :, :], bank[2][:, 0:2 * T * HM].rearrange("p (s t h) -> p s t h", s=2, t=T)).then_inc(cols_ready, 1)
                    dve.wait_ge(cols_ready, 1)
                    dve.wait_ge(conv_sig, 1)
                    dve.tensor_tensor(xc, conv, sig_c, ALU.mult).then_inc(xc_ready, 1)
                if h >= 1:
                    normalise(h - 1)
                if h == 1:
                    dve.wait_ge(a_spread, 1)
                    for m in range(HM):
                        decay(m)
                if h >= 5:
                    weighed(h - 5)
            for h in range(HM):
                dve.wait_ge(m_num, HM)
                for t in range(T):
                    at = (h % 2) * SEQ + DM
                    dve.tensor_copy(dm[:, t, h:h + 1], bank[6 * t + h // 2][:, at:at + 1]).then_inc(den_read, 1)
            dve.wait_ge(den_read, T * HM)
            step(dve.scalar_tensor_tensor(out=dm[:, :, :], in0=dm[:, :, :], scalar=-1.0, in1=dm[:, :, :], op0=ALU.mult, op1=ALU.max))
            settle()
            dve.wait_ge(em_ready, 1)
            step(dve.tensor_tensor(dm[:, :, :], dm[:, :, :], em[:, :, :], ALU.max))
            settle()
            step(dve.reciprocal(rm[:, :, :], dm[:, :, :]))
            settle()
            step(dve.tensor_tensor(dm[:, :, :], rm[:, :, :], rm[:, :, :], ALU.mult))
            settle()
            dve.wait_ge(m_ss, T * HM)
            dve.tensor_tensor(ssm[:, :, :], ssm[:, :, :], dm[:, :, :], ALU.mult).then_inc(m_ms, 1)
            dve.wait_ge(m_rs, 1)
            step(dve.tensor_tensor(rm[:, :, :], rm[:, :, :], rsm[:, :, :], ALU.mult))
            settle()
            dve.wait_ge(om_sig, 1)
            for h in range(HM):
                for t in range(T):
                    o = om[:, t, h * DM:(h + 1) * DM]
                    dve.scalar_tensor_tensor(out=o, in0=bank[6 * t + h // 2][:, (h % 2) * SEQ:(h % 2) * SEQ + DM],
                                             scalar=rm[:, t, h:h + 1], in1=o, op0=ALU.mult, op1=ALU.mult).then_inc(m_out, 1)
            def add_x(t, c):
                dve.wait_ge(mixed, 2 * t + c + 1)
                xs = xres[:, t, c * BANK:(c + 1) * BANK]
                dve.tensor_tensor(xs, bank[ACC[2 * t + c]][:, :], xs, ALU.add).then_inc(x1_ready, 1)

            def norm_x(t):
                dve.wait_ge(x1_ss, 2 * t + 2)
                dve.tensor_tensor(ss2[:, t:t + 1], ss2h[:, t, 0:1], ss2h[:, t, 1:2], ALU.add).then_inc(ss2_sum, 1)
                dve.wait_ge(x1_rs, t + 1)
                dve.tensor_scalar(hn[:, t, :], xres[:, t, :], rs2[:, t:t + 1], None, ALU.mult).then_inc(h2_norm, 1)

            def gain_x(t):
                for i in range(2):
                    dve.wait_ge(h2_turned, 2 * t + i + 1)
                    dve.tensor_tensor(ht[:, 4 * i:4 * i + 4, t * P:(t + 1) * P],
                                      bank[6 * t + i][:, :].rearrange("p (k n) -> p k n", k=4),
                                      vec[:, R_G2 + 4 * i:R_G2 + 4 * i + 4].unsqueeze(2).broadcast_to([P, 4, P]),
                                      ALU.mult).then_inc(h2_ready, 1)

            add_x(0, 0)
            add_x(0, 1)
            norm_x(0)
            add_x(1, 0)
            gain_x(0)
            add_x(1, 1)
            norm_x(1)
            gain_x(1)
            dve.wait_ge(ld_wr, 32)
            for t in range(T):
                dve.wait_ge(logits, t + 1)
                step(dve.tensor_tensor(lg[:, t, :], bank[ACC[t]][:, 0:NE], br[:, :], ALU.add))
            for t in range(T):
                dve.wait_ge(dve_step, steps[0] - 1 + t)
                dve.max(top_v[:, t, :], lg[:, t, :]).then_inc(top_max, 1)
            dve.wait_ge(top_max, 1)
            step(dve.max_index(top_i[:, 0, :], top_v[:, 0, :], lg[:, 0, :]))
            dve.wait_ge(top_max, 2)
            step(dve.max_index(top_i[:, 1, :], top_v[:, 1, :], lg[:, 1, :]))
            dve.tensor_scalar(nv0[:, :], top_v[:, :, 0], -1.0, None, ALU.mult).then_inc(top_ready, 1)
            settle()
            step(dve.tensor_copy(top_f[:, :, :], top_i[:, :, 0:TOPK]))
            settle()
            step(dve.tensor_tensor(eq, expert_no.unsqueeze(1).unsqueeze(1).broadcast_to([P, T, TOPK, NE]),
                                   top_f[:, :, :].unsqueeze(3).broadcast_to([P, T, TOPK, NE]), ALU.is_equal))
            settle()
            dve.tensor_reduce(mask[:, :, :], eq.rearrange("p t j e -> p t e j"), AX.X, ALU.add).then_inc(mask_ready, 1)
            dve.wait_ge(top_exp, T)
            step(dve.reciprocal(gsum[:, :], gsum[:, :]))
            settle()
            step(dve.tensor_tensor(gate4[:, :, :], gate4[:, :, :], gsum[:, :].unsqueeze(2).broadcast_to([P, T, TOPK]), ALU.mult))
            settle()
            step(dve.tensor_tensor(eqg, eq, gate4[:, :, :].unsqueeze(3).broadcast_to([P, T, TOPK, NE]), ALU.mult))
            settle()
            dve.tensor_reduce(gate[:, :, :], eqg.rearrange("p t j e -> p t e j"), AX.X, ALU.add).then_inc(gates_ready, 1)
            dve.wait_ge(ranks, 1)
            dve.wait_ge(mask_ready, 1)
            step(dve.scalar_tensor_tensor(out=pos[:, :, 0:NE], in0=bank[0][:, 0:T * NE].rearrange("p (t n) -> p t n", t=T),
                                          scalar=-NOWHERE, in1=mask[:, :, :], op0=ALU.add, op1=ALU.mult))
            settle()
            step(dve.tensor_scalar(pos[:, :, 0:NE], pos[:, :, 0:NE], NOWHERE, None, ALU.add))
            settle()
            dve.tensor_reduce(pmax[:, :], pos[:, :, 0:NE], AX.XY, ALU.max).then_inc(pmax_ready, 1)

            def take(e):
                for t in range(T):
                    ins = dve.tensor_scalar(pick[:, t, :], slot[:, 0:CAP], pos[:, t, bass.ds(e, 1)], None, ALU.is_equal)
                ins.then_inc(picked, 1)

            dve.wait_ge(gates_ready, 1)
            take(0)
            dve.wait_ge(pmax_turned, 1)
            step(dve.tensor_reduce(pm1[:, :], bank[0][0:1, 0:P], AX.X, ALU.max))
            settle()
            dve.tensor_scalar(flag[:, :], pm1[:, :], float(CAP), None, ALU.is_ge).then_inc(flag_ready, 1)
            dve.engine_nop().then_inc(gu_read, 1)

            def gained():
                return dve.tensor_tensor(xe_t, bank[7][:, :].rearrange("p (k n) -> p k n", k=KD),
                                         vec[:, R_G2:R_G2 + KD].unsqueeze(2).broadcast_to([P, KD, CAP]), ALU.mult)

            def expert(e, n, g):
                dve.wait_ge(gathered, g + 1)
                take(e + 1)
                for t in range(T):
                    ins = dve.tensor_scalar(pickg[:, t, :], slot[:, :], pos[:, t, bass.ds(e, 1)],
                                            gate[:, t, bass.ds(e, 1)], ALU.is_equal, ALU.mult)
                ins.then_inc(pickg_ready, 1)
                dve.wait_ge(gu_used, KD * n + KD)
                dve.tensor_scalar(gate_c, bank[0][:, :], LIMIT, None, ALU.min).then_inc(gate_cut, 1)
                dve.tensor_scalar(up_c, bank[1][:, :], LIMIT, -LIMIT, ALU.min, ALU.max).then_inc(gu_read, 1)
                dve.wait_ge(gate_cut, n + 1)
                dve.wait_ge(gu_read, n + 2)
                dve.scalar_tensor_tensor(out=act, in0=up_c, scalar=1.0, in1=gate_c, op0=ALU.add, op1=ALU.mult).then_inc(act_half, 1)
                dve.wait_ge(act_half, n + 1)
                dve.wait_ge(sig_ready, n + 1)
                dve.tensor_tensor(act, act, sig_g, ALU.mult).then_inc(act_ready, 1)
                dve.wait_ge(gathered, g + 2)
                gained().then_inc(xe_ready, 1)

            dve.wait_ge(gathered, 1)
            gained().then_inc(xe_ready, 1)
            with dve.Fori(0, NE) as e:
                expert(e, e, e)
            more = overflow(dve)
            with dve.If(more > 0):
                with dve.Fori(1, ROUNDS) as r:
                    dve.wait_ge(pickg_ready, NE * r)
                    dve.wait_ge(picked, (NE + 1) * r)
                    dve.tensor_scalar(pos[:, :, :], pos[:, :, :], -float(CAP), None, ALU.add).then_inc(moved, 1)
                    dve.wait_ge(moved, r)
                    take(0)
                    dve.wait_ge(gathered, (NE + 1) * r + 1)
                    gained().then_inc(xe_ready, 1)
                    with dve.Fori(0, NE) as e:
                        expert(e, r * NE + e, r * (NE + 1) + e)
            for t in range(T):
                for c in range(2):
                    if t + c == 0:
                        dve.wait_ge(acc_final, 1)
                    xs = xres[:, t, c * BANK:(c + 1) * BANK]
                    dve.tensor_tensor(xs, bank[ACC[2 * t + c]][:, :], xs, ALU.add).then_inc(x_final, 1)

        @block.tensor
        def _(pe):
            pe.wait_ge(consts, 1)
            for t in range(T):
                pe.wait_ge(x_norm, t + 1)
                for i in range(2):
                    for k in range(4):
                        c = 4 * i + k
                        mm = pe.transpose(bank[4 + 2 * t + i][:, k * P:(k + 1) * P], hn[:, t, c * P:(c + 1) * P], ident[:, :])
                    mm.then_inc(x_turned, 1)
                if t == 0:
                    pe.wait_ge(ld_vec, 16 * 9)
                    pe.transpose(bank[0][:, 0:ROWS], vec_r, ident[0:ROWS, 0:ROWS]).then_inc(vec_turned, 1)

            def project(dst, b, t, ks=range(KD)):
                for k in ks:
                    mm = pe.matmul(dst[:, :], ht[:, k, t * P:(t + 1) * P], win[:, b % WINS, k, :],
                                   start=(k == 0), stop=(k == KD - 1))
                return mm

            for b in range(2):
                pe.wait_ge(ld_win[b], 16)
                for t in range(T):
                    if b == 0:
                        pe.wait_ge(h_ready, 2 * t + 2)
                        if t == 0:
                            pe.wait_ge(vec_ready, 1)
                    project(bank[2 * b + t], b, t).then_inc(z_q, 1)
                pe.wait_ge(z_q, 2 * b + 2)
                pe.nop().then_inc(win_used, 1)
            pe.wait_ge(ld_win[2], 16)
            for i in range(2):
                for c in range(2):
                    m = 2 * i + c
                    for k in range(KD):
                        mm = pe.matmul(bank[6 + i][:, c * SEQ:(c + 1) * SEQ], win[:, 2, k, m * P:(m + 1) * P], ht[:, k, :],
                                       start=(k == 0), stop=(k == KD - 1))
                mm.then_inc(z_xm, 1)
            pe.wait_ge(z_xm, 2)
            pe.nop().then_inc(win_used, 1)
            pe.wait_ge(ld_wif, 32)
            for k in range(KD):
                mm = pe.matmul(bank[4][0:F_ROW + HM, 0:SEQ], wif[:, k, :], ht[:, k, :], start=(k == 0), stop=(k == KD - 1))
            mm.then_inc(z_if, 1)
            pe.wait_ge(ld_win[3], 16)
            for t in range(T):
                pe.wait_ge(qk_norm, t + 1)
                mm = project(bank[t], 3, t)
                mm.then_inc(z_v, 1)
            pe.wait_ge(z_v, 2)
            pe.nop().then_inc(win_used, 1)
            for s in range(2):
                for i in range(2):
                    if s == 0 and i == 0:
                        pe.wait_ge(qk_norm, 4)
                    if s == 1 and i == 0:
                        pe.wait_ge(f_neg, 1)
                    for j in range(2):
                        for t in range(T):
                            c = 2 * i + j
                            mm = pe.transpose(bank[2 + 2 * s + i][:, j * SEQ + t * P:j * SEQ + (t + 1) * P],
                                              qk_n[:, s, t, c * P:(c + 1) * P], ident[:, :])
                    mm.then_inc(qk_turned, 1)

            def score(h):
                if h == 0:
                    pe.wait_ge(qk_ready, 4)
                if h >= 2:
                    pe.wait_ge(pt_ready, h - 1)
                r = (h % 2) * DA
                for t in range(T):
                    lo, hi = (0, P) if t == 0 else (P, SW)
                    mm = pe.matmul(bank[4 + h % 2][:, lo:hi], qk_t[r:r + DA, 0, h // 2, t * P:(t + 1) * P],
                                   qk_t[r:r + DA, 1, h // 2, 0:(t + 1) * P], start=True, stop=True)
                mm.then_inc(scores, 1)

            def turn_p(h):
                pe.wait_ge(p_ready, 2 * h + 2)
                for i in range(3):
                    mm = pe.transpose(bank[4 + h % 2][:, i * P:(i + 1) * P], p_a[:, h % 2, i * P:(i + 1) * P], ident[:, :])
                mm.then_inc(p_turned, 1)

            def attend(h):
                pe.wait_ge(pt_ready, h + 1)
                if h == 0:
                    pe.wait_ge(v_read, 2)
                    pe.wait_ge(cols_ready, 1)
                r, j = (h % 2) * DA, h // 2
                if j >= 2:
                    pe.wait_ge(mix_a, j - 1)
                dst = bank[2 + j % 2][r:r + DA, (j // 2) * SEQ:(j // 2 + 1) * SEQ]
                pe.matmul(dst, v_a[:, 0, h * DA:(h + 1) * DA], pt_a[:, h % 2, 0:SEQ], start=True, stop=False)
                pe.matmul(dst[:, P:SEQ], v_a[:, 1, h * DA:(h + 1) * DA], pt_a[:, h % 2, SEQ:SW],
                          start=False, stop=True).then_inc(o_ready, 1)

            def fill(i):
                b, t, first = 4 + i // 4, (i // 2) % 2, i % 2 == 0
                if first:
                    if t == 0:
                        pe.wait_ge(ld_win[b], 16)
                    if b == 4:
                        pe.wait_ge(v_read, t + 1)
                    else:
                        pe.wait_ge(fill_read, t + 1)
                mm = project(bank[t], b, t, range(0, 4) if first else range(4, KD))
                if not first:
                    mm.then_inc(z_fill, 1)
                    if t == 1:
                        pe.wait_ge(z_fill, 2 * (b - 4) + 2)
                        pe.nop().then_inc(win_used, 1)

            def m_score(h):
                if h == 0:
                    pe.wait_ge(qkm_read, 4)
                if h >= 2:
                    pe.wait_ge(m_g, h - 1)
                s_b = bank[6 + h % 2]
                pe.matmul(s_b[:, 0:SEQ], km_t[:, h, 0:P], qm_t[:, h, :], start=True, stop=True)
                pe.matmul(s_b[:, SEQ:SW], km_t[:, h, P:SEQ], qm_t[:, h, P:SEQ], start=True, stop=True).then_inc(m_scores, 1)

            def m_sum(h):
                if h == 0:
                    pe.wait_ge(m_g, HM)
                    pe.wait_ge(fill_read, 4)
                at = (h % 2) * SEQ
                g = e_m[:, h, :]
                pe.matmul(bank[h // 2][:, at:at + DM + 1], g[:, 0:P], vm[:, 0, h, :], start=True, stop=True)
                dst = bank[6 + h // 2][:, at:at + DM + 1]
                pe.matmul(dst, g[:, P:SEQ], vm[:, 0, h, :], start=True, stop=False)
                pe.matmul(dst, g[:, SEQ:SW], vm[:, 1, h, :], start=False, stop=True).then_inc(m_num, 1)

            for h in range(HA + 2):
                if h < HA:
                    score(h)
                    if h == 0:
                        pe.wait_ge(rows_ready, 1)
                        for s, rows in ((0, rows_i), (1, rows_l)):
                            for t in range(T):
                                at = (s * T + t) * HM
                                mm = pe.transpose(bank[2][:, at:at + HM], rows[:, t * P:(t + 1) * P], ident[0:HM, 0:HM])
                        mm.then_inc(cols_turned, 1)
                    fill(h)
                if h == 0:
                    pe.wait_ge(consts, 8)
                    pe.wait_ge(xm_read, 2)
                    for m in range(HM):
                        mm = pe.matmul(bank[6 + m // 2][:, (m % 2) * SEQ:(m % 2 + 1) * SEQ], sel[:, m, :], rows_a[:, :],
                                       start=True, stop=True)
                    mm.then_inc(a_spread, 1)
                if 1 <= h <= HA:
                    turn_p(h - 1)
                if h >= 2:
                    attend(h - 2)
                if h in (2, 3):
                    if h == 2:
                        pe.wait_ge(ld_wm, 32)
                        pe.wait_ge(xc_ready, 1)
                        pe.wait_ge(m_arg, HM)
                    else:
                        pe.wait_ge(qkm_read, 2)
                    for m in range(HM):
                        mm = pe.matmul(bank[6 + m // 2][:, (m % 2) * SEQ:(m % 2 + 1) * SEQ], (wmq, wmk)[h - 2][:, m, :],
                                       xc[:, m, :], start=True, stop=True)
                        if m % 2:
                            mm.then_inc(qkm, 1)
                if 4 <= h < HA:
                    m_score(h - 4)
            for h in range(HM):
                m_sum(h)
            def out_half(t, c, ks):
                for k in ks:
                    mm = pe.matmul(bank[ACC[2 * t + c]][:, :], mix_t[:, k, t * P:(t + 1) * P], wout[:, k, c * BANK:(c + 1) * BANK],
                                   start=(k == 0), stop=(k == KD - 1))
                return mm

            pe.wait_ge(ld_wout, 16)
            pe.wait_ge(mix_a, 4)
            pe.wait_ge(pt_ready, HA)
            for t in range(T):
                for c in range(2):
                    out_half(t, c, range(4))
            pe.wait_ge(m_out, T * HM)
            for h in range(HM):
                for t in range(T):
                    mm = pe.transpose(bank[TURN[h]][:, t * P:(t + 1) * P], om[:, t, h * DM:(h + 1) * DM], ident[:, :])
                mm.then_inc(m_turned, 1)

            def turn_x(t):
                pe.wait_ge(h2_norm, t + 1)
                for i in range(2):
                    for k in range(4):
                        c = 4 * i + k
                        mm = pe.transpose(bank[6 * t + i][:, k * P:(k + 1) * P], hn[:, t, c * P:(c + 1) * P], ident[:, :])
                    mm.then_inc(h2_turned, 1)

            def route(t):
                pe.wait_ge(ld_wr, 32)
                pe.wait_ge(h2_ready, 2 * t + 2)
                pe.wait_ge(x1_ready, 2)
                for k in range(KD):
                    mm = pe.matmul(bank[ACC[t]][:, 0:NE], ht[:, k, t * P:(t + 1) * P], wr[:, k, :],
                                   start=(k == 0), stop=(k == KD - 1))
                mm.then_inc(logits, 1)

            pe.wait_ge(mix_m, HM)
            out_half(0, 0, range(4, KD)).then_inc(mixed, 1)
            out_half(0, 1, range(4, KD)).then_inc(mixed, 1)
            out_half(1, 0, range(4, KD)).then_inc(mixed, 1)
            turn_x(0)
            out_half(1, 1, range(4, KD)).then_inc(mixed, 1)
            route(0)
            turn_x(1)
            route(1)
            pe.wait_ge(mask_ready, 1)
            pe.matmul(bank[0][:, 0:NE], before[:, :], mask[:, 0, :], start=True, stop=True)
            pe.matmul(bank[0][:, NE:2 * NE], ones[:, :], mask[:, 0, :], start=True, stop=False)
            pe.matmul(bank[0][:, NE:2 * NE], before[:, :], mask[:, 1, :], start=False, stop=True).then_inc(ranks, 1)
            pe.wait_ge(gates_ready, 1)
            for t in range(T):
                mm = pe.transpose(bank[6][0:NE, t * P:(t + 1) * P], gate[:, t, :], ident[:, :])
            mm.then_inc(gate_turned, 1)
            pe.wait_ge(pmax_ready, 1)
            pe.transpose(bank[0][0:1, 0:P], pmax[:, :], ident[:, :]).then_inc(pmax_turned, 1)

            def gather(g):
                pe.wait_ge(picked, g + 1)
                for k in range(KD):
                    for t in range(T):
                        for i in range(3):
                            mm = pe.matmul(bank[7][:, k * CAP:(k + 1) * CAP], parts[:, t, i, k * P:(k + 1) * P], pick[:, t, :],
                                           start=(t + i == 0), stop=(t == T - 1 and i == 2))
                mm.then_inc(gathered, 1)

            pe.wait_ge(lo_ready, 2)
            gather(0)
            def start_sum():
                pe.wait_ge(ld_bdn, 16)
                pe.wait_ge(bank6_read, 1)
                pe.wait_ge(x1_ready, 4)
                pe.wait_ge(top_max, T)
                for t in range(T):
                    for c in range(2):
                        mm = pe.matmul(bank[ACC[2 * t + c]][:, :], gate_t[:, t * P:(t + 1) * P], bdn[:, c * BANK:(c + 1) * BANK],
                                       start=True, stop=False, skip_group_check=True)
                mm.then_inc(y_spread, 1)

            def spread(n, u, t):
                pe.wait_ge(bank6_read, n + 2)
                for c in range(2):
                    mm = pe.matmul(bank[ACC[2 * t + c]][:, :], s_sb[c * CAP:(c + 1) * CAP, u, t * P:(t + 1) * P],
                                   y_sb[c * CAP:(c + 1) * CAP, :], start=False, stop=False, skip_group_check=True)
                if t == T - 1:
                    mm.then_inc(y_spread, 1)

            def expert(n, g, u, times, first=False):
                pe.wait_ge(xe_ready, g + 1)
                pe.wait_ge(gu_read, n + 1)
                pe.wait_ge(ld_brow[u], 16 * times + 16)
                for i in range(4):
                    h, c = i // 2, i % 2
                    mm = pe.matmul(bank[h][c * CAP:(c + 1) * CAP, :], ones[32 * i:32 * i + 1, 0:CAP],
                                   brow[32 * i:32 * i + 1, u, :], start=True, stop=False, skip_group_check=True)
                mm.then_inc(brow_used, 1)
                for k in range(KD):
                    pe.wait_ge(ld_gu[u * KD + k], 16 * times + 16)
                    for h in range(2):
                        for c in range(2):
                            at = h * FF + c * BANK
                            mm = pe.matmul(bank[h][c * CAP:(c + 1) * CAP, :], xe_t[:, k, :], gu[:, u, k, at:at + BANK],
                                           start=False, stop=(k == KD - 1), skip_group_check=True)
                    mm.then_inc(gu_used, 1)
                pe.wait_ge(pickg_ready, n + 1)
                pe.wait_ge(bank6_read, n + 1)
                for t in range(T):
                    mm = pe.transpose(bank[6][:, t * P:(t + 1) * P], pickg[:, t, :], ident[:, :])
                mm.then_inc(slots_turned, 1)
                gather(g + 1)
                if not first:
                    spread(n - 1, 1 - u, 0)
                pe.wait_ge(act_ready, n + 1)
                pe.wait_ge(slots_ready, n + 1)
                for k in range(4):
                    mm = pe.transpose(bank[6][:, k * P:(k + 1) * P], act[:, k * P:(k + 1) * P], ident[:, :])
                mm.then_inc(act_turned, 1)
                if not first:
                    spread(n - 1, 1 - u, 1)
                pe.wait_ge(act_t_ready, n + 1)
                for k in range(KD):
                    if k % 2 == 0:
                        pe.wait_ge(ld_d[k // 2], 16 * n + 16)
                    at = (k % 4) * P + (k // 4) * CAP
                    for c in range(2):
                        mm = pe.matmul(bank[6][c * CAP:(c + 1) * CAP, :], act_t[:, at:at + CAP], dn[:, k, c * BANK:(c + 1) * BANK],
                                       start=(k == 0), stop=(k == KD - 1), skip_group_check=True)
                    if k % 2:
                        mm.then_inc(d_used, 1)

            def experts(r):
                n, g, times = r * NE, r * (NE + 1), r * (NE // 2)
                expert(n, g, 0, times, first=True)
                with pe.Fori(0, NE // 2 - 1) as i:
                    expert(n + 2 * i + 1, g + 2 * i + 1, 1, times + i)
                    expert(n + 2 * i + 2, g + 2 * i + 2, 0, times + i + 1)
                expert(n + NE - 1, g + NE - 1, 1, times + NE // 2 - 1)
                for t in range(T):
                    spread(n + NE - 1, 1, t)

            start_sum()
            experts(0)
            pe.wait_ge(y_spread, NE + 1)
            more = overflow(pe)
            with pe.If(more > 0):
                with pe.Fori(1, ROUNDS) as r:
                    gather(r * (NE + 1))
                    experts(r)
                pe.wait_ge(y_spread, ROUNDS * NE + 1)
            pe.nop().then_inc(acc_final, 1)


_INS = ['x', 'norm1_g', 'w_in', 'q_norm_g', 'k_norm_g', 'conv_w', 'conv_b', 'w_mq', 'w_mk', 'b_igate', 'b_fgate',
        'mh_norm_g', 'w_out', 'norm2_g', 'w_router', 'b_router', 'w_gate_up', 'b_gate_up', 'w_down', 'b_down']


def kernel(**inputs):
    import concourse.bacc as _bacc
    from concourse.bass_utils import run_bass_kernel_spmd as _run

    nc = _bacc.Bacc("TRN2", target_bir_lowering=False, num_devices=1, dynamic_dma_scratch_size=1024)
    arrays, args = {}, []
    given = [(name, np.ascontiguousarray(inputs[name])) for name in _INS] + [("attn_bias", attention_bias())]
    for name, a in given:
        arrays[f"in_{name}"] = a
        args.append(nc.dram_tensor(f"in_{name}", a.shape, mybir.dt.from_np(a.dtype), kind="ExternalInput").ap())
    args.append(nc.dram_tensor("out", (1, SEQ, D), F32, kind="ExternalOutput").ap())
    layer_kernel(nc, *args)
    r = _run(nc, [arrays], core_ids=[0])
    return r.results[0]["out"]
```

```python
from contextlib import ExitStack

import numpy as np

import concourse.bass as bass
from concourse import mybir

F32 = mybir.dt.float32
BF16 = mybir.dt.bfloat16
I32 = mybir.dt.int32
U32 = mybir.dt.uint32
ALU = mybir.AluOpType
ACT = mybir.ActivationFunctionType
AX = mybir.AxisListType

P = 128
SEQ = 256
D = 1024
T = SEQ // P
KD = D // P
HALF = D // 2
BANK = 512
HA, DA = 8, 64
HM, DM = 4, 128
TAPS = 4
NE, TOPK = 32, 4
FF = D
CAP = 64
LAST = 4
ACC = (2, 3, 4, 5)
TURN = (0, 1, 6, 7)
ROUNDS = SEQ // CAP
LIMIT, ALPHA = 7.0, 1.702
EPS = 1e-6
MASKED = -1e30
NOWHERE = -1000.0
SW = P + SEQ
WINS = 4
WARM = (12, 2, 12, 2)
R_G1, R_G2, R_MH, R_CB, R_CW, R_QG, R_KG, ROWS = 0, 8, 16, 20, 24, 40, 41, 42


def attention_bias():
    p = np.arange(P)[:, None]
    dist = np.concatenate([p - np.arange(P)[None], p + P - np.arange(SEQ)[None]], 1)
    count = np.zeros(dist.shape)
    for window, dil in ((128, 1), (512, 4), (2048, 16)):
        count += (dist >= 0) & (dist <= window) & (dist % dil == 0)
    slopes = 2.0 ** (-8.0 * np.arange(1, HA + 1) / HA)
    bias = np.where(count > 0, np.log(np.maximum(count, 1)), MASKED)[:, None, :] - slopes[None, :, None] * dist[:, None, :]
    return np.where(count[:, None, :] > 0, bias, MASKED).astype(np.float32)


def layer_kernel(nc, x, norm1_g, w_in, q_norm_g, k_norm_g, conv_w, conv_b, w_mq, w_mk, b_igate, b_fgate,
                 mh_norm_g, w_out, norm2_g, w_router, b_router, w_gate_up, b_gate_up, w_down, b_down,
                 attn_bias, out):
    with ExitStack() as ctx:
        def sb(name, shape, dt=F32):
            return ctx.enter_context(nc.sbuf_tensor(name, shape, dt))

        def sem(name):
            return ctx.enter_context(nc.semaphore(name))

        gu_ring = sb("gu_ring", [P, 2 * KD * 2 * FF])
        d_ring = sb("d_ring", [P, KD * D])
        gu = gu_ring[:, :].rearrange("p (u k n) -> p u k n", u=2, k=KD)
        dn = d_ring[:, :].rearrange("p (k n) -> p k n", k=KD)
        win = gu_ring[:, 0:WINS * KD * HALF].rearrange("p (b k n) -> p b k n", b=WINS, k=KD)
        wout = dn
        half = KD * 2 * FF
        place = [half]

        def in_second_half(words):
            at = place[0]
            place[0] += words
            assert place[0] <= 2 * half
            return gu_ring[:, at:at + words]

        bias_a = in_second_half(HA * SW).rearrange("p (h n) -> p h n", h=HA)
        qk_n = in_second_half(2 * T * HALF).rearrange("p (s t n) -> p s t n", s=2, t=T)
        qk_t = in_second_half(2 * 4 * SEQ).rearrange("p (s j n) -> p s j n", s=2, j=4)
        v_a = in_second_half(T * HALF).rearrange("p (t n) -> p t n", t=T)
        assert place[0] == half + 4 * 2 * FF
        PADW = SEQ + TAPS - 1
        xm = in_second_half(HM * PADW).rearrange("p (h n) -> p h n", h=HM)
        conv = in_second_half(HM * SEQ).rearrange("p (h n) -> p h n", h=HM)
        xc = in_second_half(HM * SEQ).rearrange("p (h n) -> p h n", h=HM)
        vm = in_second_half(T * HM * (DM + 1)).rearrange("p (t h n) -> p t h n", t=T, h=HM)
        qm_t = in_second_half(HM * SEQ).rearrange("p (h n) -> p h n", h=HM)
        km_t = in_second_half(HM * SEQ).rearrange("p (h n) -> p h n", h=HM)
        wmq = in_second_half(HM * DM).rearrange("p (h n) -> p h n", h=HM)
        wmk = in_second_half(HM * DM).rearrange("p (h n) -> p h n", h=HM)
        sig_c = km_t

        xres = sb("xres", [P, T, D])
        hn = sb("hn", [P, T, D])
        hn_flat = hn[:, :, :].rearrange("p t n -> p (t n)")
        e_m = hn_flat[:, 0:HM * SW].rearrange("p (h n) -> p h n", h=HM)
        parts = sb("parts", [P, T, 3, D], BF16)
        sel = hn_flat[0:HM, 4 * SW:4 * SW + HM * P].rearrange("p (h n) -> p h n", h=HM)
        ht = sb("ht", [P, KD, SEQ])
        ht_flat = ht[:, :, :].rearrange("p k n -> p (k n)")
        xe_t = ht_flat[:, 0:BANK].rearrange("p (k n) -> p k n", k=KD)
        act_t = ht_flat[:, BANK:2 * BANK]
        y_sb = ht_flat[:, 2 * BANK:3 * BANK]
        s_sb = ht_flat[:, 3 * BANK:4 * BANK].rearrange("p (b n) -> p b n", b=2)
        mix_t = sb("mix_t", [P, KD, SEQ])
        mix_flat = mix_t[:, :, :].rearrange("p k n -> p (k n)")
        rows_i, rows_f, rows_l, rows_b, ones_r = (mix_flat[0:HM, i * SEQ:(i + 1) * SEQ] for i in range(5))
        gate_c, sig_g, up_c, act = (mix_flat[:, i * BANK:(i + 1) * BANK] for i in range(4))
        attn_tmp = sb("attn_tmp", [P, 4 * SW])
        p_a = attn_tmp[:, 0:2 * SW].rearrange("p (b n) -> p b n", b=2)
        pt_a = attn_tmp[:, 2 * SW:4 * SW].rearrange("p (b n) -> p b n", b=2)
        sq = attn_tmp[:, 0:2 * HALF].rearrange("p (b n) -> p b n", b=2)
        sq_x = attn_tmp[:, 0:D]
        brow = attn_tmp[:, 0:2 * BANK].rearrange("p (u n) -> p u n", u=2)
        om = sb("om", [P, T, HALF])
        bdn = om[0:NE, :, :].rearrange("p t n -> p (t n)")
        eps = sb("eps", [P, 1])
        qkg = sb("qkg", [P, 2])
        rows_a = sb("rows_a", [HM, SEQ])
        ident = sb("ident", [P, P])
        ones = sb("ones", [P, P])
        before = sb("before", [P, P])
        slot = sb("slot", [P, 2 * CAP])
        slot_i = sb("slot_i", [P, 2 * CAP], I32)
        expert_no = slot[:, 0:NE]
        vec = sb("vec", [P, ROWS])
        bif = sb("bif", [HM, 2])
        early = parts[:, :, :, :].rearrange("p t i n -> p (t i n)").bitcast(F32)
        wif = early[:, 0:KD * 2 * HM].rearrange("p (k n) -> p k n", k=KD)
        vec_r = early[0:ROWS, KD * 2 * HM:KD * 2 * HM + P]
        if_c = early[:, P + KD * 2 * HM:P + (KD + T) * 2 * HM].rearrange("p (t s h) -> p t s h", t=T, s=2)
        wr = sb("wr", [P, KD, NE])
        br = sb("br", [P, NE])
        ss1 = sb("ss1", [P, T])
        rs1 = sb("rs1", [P, T])
        ssqk = sb("ssqk", [P, 2, T, HA])
        rsqk = sb("rsqk", [P, 2, T, HA])
        mx = sb("mx", [P, HA, T])
        nmx = sb("nmx", [P, HA, T])
        den = sb("den", [P, HA, T])
        rden = sb("rden", [P, HA, T])
        acol = sb("acol", [P, 2, T, HM])
        em = sb("em", [P, T, HM])
        dm = sb("dm", [P, T, HM])
        rm = sb("rm", [P, T, HM])
        ssm = sb("ssm", [P, T, HM])
        rsm = sb("rsm", [P, T, HM])
        ss2h = sb("ss2h", [P, T, 2])
        ss2 = sb("ss2", [P, T])
        rs2 = sb("rs2", [P, T])
        lg = sb("lg", [P, T, NE])
        top_v = sb("top_v", [P, T, 8])
        top_i = sb("top_i", [P, T, 8], U32)
        top_f = sb("top_f", [P, T, TOPK])
        nv0 = sb("nv0", [P, T])
        gate4 = sb("gate4", [P, T, TOPK])
        gsum = sb("gsum", [P, T])
        eq, eqg = (mix_flat[:, i * T * TOPK * NE:(i + 1) * T * TOPK * NE].rearrange("p (t j e) -> p t j e", t=T, j=TOPK)
                   for i in range(2))
        mask = sb("mask", [P, T, NE])
        gate = sb("gate", [P, T, NE])
        gate_t = attn_tmp[0:NE, 2 * BANK:2 * BANK + SEQ]
        pos = sb("pos", [P, T, NE])
        pmax = sb("pmax", [P, 1])
        pm1 = sb("pm1", [1, 1])
        flag = sb("flag", [1, 1], I32)
        pick = sb("pick", [P, T, CAP], BF16)
        pickg = attn_tmp[:, 2 * BANK + SEQ:3 * BANK].rearrange("p (t n) -> p t n", t=T)

        bank = [ctx.enter_context(nc.psum_tensor(f"bank{i}", [P, BANK], F32)) for i in range(8)]

        ld_x = [sem(f"ld_x{t}") for t in range(T)]
        ld_g1 = sem("ld_g1")
        ld_vec = sem("ld_vec")
        ld_small = sem("ld_small")
        ld_wif = sem("ld_wif")
        ld_wr = sem("ld_wr")
        ld_win = [sem(f"ld_win{b}") for b in range(6)]
        ld_win0b = sem("ld_win0b")
        ld_bias_a = sem("ld_bias_a")
        ld_wm = sem("ld_wm")
        ld_wout = sem("ld_wout")
        ld_bdn = sem("ld_bdn")
        ld_gu = [sem(f"ld_gu{i}") for i in range(2 * KD)]
        ld_d = [sem(f"ld_d{i}") for i in range(4)]
        ld_brow = [sem(f"ld_brow{i}") for i in range(2)]
        pool_step = sem("pool_step")
        consts = sem("consts")
        dve_step = sem("dve_step")
        act_step = sem("act_step")
        x_ms = sem("x_ms")
        x_rs = sem("x_rs")
        x_norm = sem("x_norm")
        x_turned = sem("x_turned")
        h_ready = sem("h_ready")
        g1_turned = sem("g1_turned")
        g1_ready = sem("g1_ready")
        vec_turned = sem("vec_turned")
        vec_ready = sem("vec_ready")
        eps_ready = sem("eps_ready")
        z_q = sem("z_q")
        z_xm = sem("z_xm")
        z_if = sem("z_if")
        z_v = sem("z_v")
        z_fill = sem("z_fill")
        fill_read = sem("fill_read")
        qk_sq = sem("qk_sq")
        qk_ms = sem("qk_ms")
        qk_rs = sem("qk_rs")
        qk_norm = sem("qk_norm")
        qk_turned = sem("qk_turned")
        qk_ready = sem("qk_ready")
        xm_read = sem("xm_read")
        conv_ready = sem("conv_ready")
        conv_sig = sem("conv_sig")
        xc_ready = sem("xc_ready")
        f_neg = sem("f_neg")
        f_log = sem("f_log")
        rows_ready = sem("rows_ready")
        cols_turned = sem("cols_turned")
        cols_ready = sem("cols_ready")
        em_ready = sem("em_ready")
        v_read = sem("v_read")
        scores = sem("scores")
        s_max = sem("s_max")
        s_exp = sem("s_exp")
        p_ready = sem("p_ready")
        p_turned = sem("p_turned")
        pt_ready = sem("pt_ready")
        o_ready = sem("o_ready")
        mix_a = sem("mix_a")
        om_sig = sem("om_sig")
        qkm = sem("qkm")
        qkm_read = sem("qkm_read")
        m_scores = sem("m_scores")
        a_spread = sem("a_spread")
        if_copied = sem("if_copied")
        if_turned = sem("if_turned")
        hi_ready = sem("hi_ready")
        mid_ready = sem("mid_ready")
        lo_ready = sem("lo_ready")
        rest_1 = sem("rest_1")
        rest_half = sem("rest_half")
        lo_half = sem("lo_half")
        m_arg1 = sem("m_arg1")
        m_arg = sem("m_arg")
        m_exp = sem("m_exp")
        m_sel = sem("m_sel")
        m_g = sem("m_g")
        m_num = sem("m_num")
        m_ss = sem("m_ss")
        den_read = sem("den_read")
        m_ms = sem("m_ms")
        m_rs = sem("m_rs")
        m_out = sem("m_out")
        m_turned = sem("m_turned")
        mix_m = sem("mix_m")
        mixed = sem("mixed")
        x1_ready = sem("x1_ready")
        x1_ss = sem("x1_ss")
        x1_rs = sem("x1_rs")
        ss2_sum = sem("ss2_sum")
        h2_norm = sem("h2_norm")
        wr_ready = sem("wr_ready")
        turned_x0 = sem("turned_x0")
        turned_x1 = sem("turned_x1")
        h2_turned = sem("h2_turned")
        logits = sem("logits")
        top_max = sem("top_max")
        top_ready = sem("top_ready")
        top_exp = sem("top_exp")
        mask_ready = sem("mask_ready")
        gates_ready = sem("gates_ready")
        ranks = sem("ranks")
        gate_turned = sem("gate_turned")
        bank6_read = sem("bank6_read")
        pmax_ready = sem("pmax_ready")
        pmax_turned = sem("pmax_turned")
        flag_ready = sem("flag_ready")
        picked = sem("picked")
        pickg_ready = sem("pickg_ready")
        gathered = sem("gathered")
        xe_ready = sem("xe_ready")
        gu_used = sem("gu_used")
        brow_used = sem("brow_used")
        gu_read = sem("gu_read")
        gate_cut = sem("gate_cut")
        sig_ready = sem("sig_ready")
        act_half = sem("act_half")
        moved = sem("moved")
        act_ready = sem("act_ready")
        slots_turned = sem("slots_turned")
        slots_ready = sem("slots_ready")
        act_turned = sem("act_turned")
        act_t_ready = sem("act_t_ready")
        d_used = sem("d_used")
        y_spread = sem("y_spread")
        acc_final = sem("acc_final")
        x_final = sem("x_final")
        stored = sem("stored")

        w_in0 = w_in[0].rearrange("(k p) n -> p k n", p=P)
        BLOCKS = [0, HALF, 3 * HALF, 2 * HALF, 4 * HALF, 5 * HALF]

        def overflow(eng):
            eng.wait_ge(flag_ready, 1)
            return eng.value_load(flag[0:1, 0:1], min_val=0, max_val=1)

        block = ctx.enter_context(nc.Block())

        @block.sync
        def _(sp):
            def load_gu(e, u, k):
                sp.dma_start(gu[:, u, k, :], w_gate_up[0, e, k * P:(k + 1) * P, :]).then_inc(ld_gu[u * KD + k], 16)

            def load_brow(e, u):
                sp.dma_start(brow[0:97:32, u, :], b_gate_up[0, e, :].rearrange("(i n) -> i n", n=BANK)).then_inc(ld_brow[u], 16)

            def load_d(e, j):
                sp.dma_start(dn[:, 2 * j:2 * j + 2, :],
                             w_down[0, e, 2 * j * P:2 * (j + 1) * P, :].rearrange("(c p) n -> p c n", p=P)).then_inc(ld_d[j], 16)

            def load_win(b):
                sp.dma_start(win[:, b % WINS, :, :], w_in0[:, :, BLOCKS[b]:BLOCKS[b] + HALF]).then_inc(ld_win[b], 16)

            for t in range(T):
                sp.dma_start(xres[:, t, :], x[0, t * P:(t + 1) * P, :]).then_inc(ld_x[t], 16)
            for k, loaded in ((0, ld_win[0]), (4, ld_win0b)):
                sp.dma_start(win[:, 0, k:k + 4, :], w_in0[:, k:k + 4, 0:HALF]).then_inc(loaded, 16)
            sp.dma_start(wif, w_in0[:, :, 6 * HALF:6 * HALF + 2 * HM]).then_inc(ld_wif, 16)
            load_win(1)
            sp.dma_start(bif[:, 0:1], b_igate[0].rearrange("(h o) -> h o", o=1)).then_inc(ld_small, 16)
            sp.dma_start(bif[:, 1:2], b_fgate[0].rearrange("(h o) -> h o", o=1)).then_inc(ld_small, 16)
            sp.dma_start(vec_r[R_CB:R_CB + HM, :], conv_b[0].rearrange("(k n) -> k n", n=P)).then_inc(ld_vec, 16)
            sp.dma_start(vec_r[R_CW:R_CW + TAPS * HM, :], conv_w[0].rearrange("j (k n) -> (j k) n", n=P)).then_inc(ld_vec, 16)
            sp.dma_start(vec_r[R_G2:R_G2 + KD, :], norm2_g[0].rearrange("(k n) -> k n", n=P)).then_inc(ld_vec, 16)
            sp.dma_start(vec_r[R_MH:R_MH + HM, :], mh_norm_g[0]).then_inc(ld_vec, 16)
            for r, g in ((R_QG, q_norm_g), (R_KG, k_norm_g)):
                for i in range(2):
                    sp.dma_start(vec_r[r:r + 1, i * DA:(i + 1) * DA], g).then_inc(ld_vec, 16)
            load_win(2)
            load_win(3)
            sp.dma_start(bias_a, attn_bias).then_inc(ld_bias_a, 16)
            sp.dma_start(wmq, w_mq[0].rearrange("h d e -> d h e")).then_inc(ld_wm, 16)
            sp.dma_start(wmk, w_mk[0].rearrange("h d e -> d h e")).then_inc(ld_wm, 16)
            sp.dma_start(wr[:, :, :], w_router[0].rearrange("(k p) n -> p k n", p=P)).then_inc(ld_wr, 16)
            sp.dma_start(br[:, :], b_router[0:1, :].broadcast_to([P, NE])).then_inc(ld_wr, 16)
            sp.dma_start(wout, w_out[0].rearrange("(k p) n -> p k n", p=P)).then_inc(ld_wout, 16)
            for b in (4, 5):
                sp.wait_ge(z_q, 2 * (b - WINS) + 2)
                load_win(b)
            for b, used, n in ((2, z_xm, 2), (3, z_v, 2), (0, z_fill, 2), (1, z_fill, 4)):
                sp.wait_ge(used, n)
                load_gu(0, 0, 2 * b)
                load_gu(0, 0, 2 * b + 1)
            sp.wait_ge(mix_a, 4)
            for k in range(4):
                load_gu(1, 1, k)
            load_brow(0, 0)
            load_brow(1, 1)
            sp.wait_ge(m_num, HM)
            for k in range(4, KD):
                load_gu(1, 1, k)
            sp.wait_ge(mix_m, HM)
            sp.dma_start(bdn, b_down[0]).then_inc(ld_bdn, 16)
            sp.wait_ge(mixed, 4)
            for j in range(4):
                load_d(0, j)

            def weights(base):
                def next_gu(n, e, u):
                    sp.wait_ge(brow_used, n - 1)
                    load_brow(e, u)
                    for k in range(KD):
                        sp.wait_ge(gu_used, KD * (n - 2) + k + 1)
                        load_gu(e, u, k)

                def next_d(n, e):
                    for j in range(4):
                        sp.wait_ge(d_used, 4 * (n - 1) + j + 1)
                        load_d(e, j)

                with sp.Fori(0, (NE - LAST) // 2 - 1) as i:
                    for u in range(2):
                        e = 2 * i + 2 + u
                        next_gu(base + e, e, u)
                        next_d(base + e - 1, e - 1)
                first = NE - LAST
                next_gu(base + first, first, 0)
                next_d(base + first - 1, first - 1)
                next_d(base + first, first)
                for e in range(first + 1, NE):
                    next_gu(base + e, e, e % 2)
                    next_d(base + e, e)

            weights(0)
            more = overflow(sp)
            with sp.If(more > 0):
                with sp.Fori(1, ROUNDS) as r:
                    base = r * NE
                    for u in range(2):
                        sp.wait_ge(brow_used, base + u - 1)
                        load_brow(u, u)
                        for k in range(KD):
                            sp.wait_ge(gu_used, KD * (base + u - 2) + k + 1)
                            load_gu(u, u, k)
                    for j in range(4):
                        sp.wait_ge(d_used, 4 * (base - 1) + j + 1)
                        load_d(0, j)
                    weights(base)
            for t in range(T):
                for c in range(2):
                    sp.wait_ge(x_final, 2 * t + c + 1)
                    sp.dma_start(out[0, t * P:(t + 1) * P, c * BANK:(c + 1) * BANK],
                                 xres[:, t, c * BANK:(c + 1) * BANK]).then_inc(stored, 16)
            sp.wait_ge(stored, 16 * 2 * T)

        @block.gpsimd
        def _(pool):
            pool.memset(ident[:, :], 0.0).then_inc(pool_step, 1)
            pool.memset(ones[:, :], 1.0).then_inc(pool_step, 1)
            pool.iota(slot_i[:, :].rearrange("p (d n) -> p d n", d=2), pattern=[[0, 2], [1, CAP]], base=0,
                      channel_multiplier=0).then_inc(pool_step, 1)
            pool.wait_ge(pool_step, 3)
            pool.affine_select(out=ident[:, :], in_=ident[:, :], compare_op=ALU.not_equal, fill=1.0, base=0,
                               pattern=[[-1, P]], channel_multiplier=1).then_inc(consts, 1)
            pool.affine_select(out=before[:, :], in_=ones[:, :], compare_op=ALU.is_gt, fill=0.0, base=0,
                               pattern=[[1, P]], channel_multiplier=-1).then_inc(consts, 1)
            pool.tensor_copy(slot[:, :], slot_i[:, :]).then_inc(consts, 1)
            pool.memset(xm[:, :, 0:TAPS - 1], 0.0).then_inc(consts, 1)
            pool.memset(vm[:, :, :, DM:DM + 1], 1.0).then_inc(consts, 1)
            pool.memset(ones_r, 1.0).then_inc(consts, 1)
            pool.wait_ge(x_turned, 4)
            pool.memset(sel, 0.0).then_inc(pool_step, 1)
            pool.wait_ge(pool_step, 4)
            pool.affine_select(out=sel, in_=sel, compare_op=ALU.not_equal, fill=1.0, base=0,
                               pattern=[[-1, HM], [0, P]], channel_multiplier=1).then_inc(consts, 1)
            for h in range(HM):
                pool.wait_ge(m_exp, h + 1)
                diag = e_m[:, h, :].rearrange("p (b n) -> p b n", b=3)[:, 0:3:2, :]
                pool.affine_select(out=diag, in_=diag, compare_op=ALU.is_ge, fill=0.0, base=0,
                                   pattern=[[0, 2], [1, P]], channel_multiplier=-1).then_inc(m_sel, 1)
            for t, n in ((0, D), (1, HALF)):
                pool.wait_ge(hi_ready, t + 1)
                pool.wait_ge(h2_norm, t + 1)
                pool.tensor_tensor(hn[:, t, 0:n], hn[:, t, 0:n], parts[:, t, 0, 0:n], ALU.subtract).then_inc(rest_1, 1)
                pool.wait_ge(mid_ready, t + 1)
                pool.tensor_tensor(parts[:, t, 2, 0:n], hn[:, t, 0:n], parts[:, t, 1, 0:n], ALU.subtract).then_inc(lo_ready, 1)

        @block.scalar
        def _(act_e):
            act = act_e
            act.dma_start(vec_r[R_G1:R_G1 + KD, :], norm1_g[0].rearrange("(k n) -> k n", n=P)).then_inc(ld_g1, 16)
            act.preload_act_table_set("natural_log_exp_and_others")

            for t in range(T):
                act.wait_ge(ld_x[t], 16)
                if t:
                    act.wait_ge(x_ms, t)
                act.activation(sq_x, xres[:, t, :], ACT.Square, accum_out=ss1[:, t:t + 1]).then_inc(x_ms, 1)
                act.wait_ge(x_ms, t + 1)
                act.wait_ge(eps_ready, 1)
                act.activation(rs1[:, t:t + 1], ss1[:, t:t + 1], ACT.Ln, scale=1.0 / D, bias=eps[:, 0:1]).then_inc(act_step, 1)
                act.wait_ge(act_step, t + 1)
                act.activation(rs1[:, t:t + 1], rs1[:, t:t + 1], ACT.Exp, scale=-0.5).then_inc(x_rs, 1)
            for s in range(2):
                for t in range(T):
                    n = 2 * s + t
                    act.wait_ge(z_q, n + 1)
                    if n == 0:
                        act.wait_ge(x_ms, T)
                    if n >= 2:
                        act.wait_ge(qk_ms, n - 1)
                    act.activation(sq[:, t, :], bank[n][:, :], ACT.Square).then_inc(qk_sq, 1)
            for s in range(2):
                act.wait_ge(qk_ms, 2 * s + 2)
                act.activation(rsqk[:, s], ssqk[:, s], ACT.Ln, scale=1.0 / DA, bias=eps[:, 0:1]).then_inc(act_step, 1)
                act.wait_ge(act_step, 3 + s)
                act.activation(rsqk[:, s], rsqk[:, s], ACT.Exp, scale=-0.5).then_inc(qk_rs, 1)
            for i in range(2):
                act.wait_ge(z_xm, i + 1)
                if i == 0:
                    act.wait_ge(consts, 6)
                act.activation(xm[:, 2 * i:2 * i + 2, TAPS - 1:PADW], bank[6 + i][:, :].rearrange("p (h n) -> p h n", h=2),
                               ACT.Copy).then_inc(xm_read, 1)
            act.wait_ge(f_neg, 1)
            act.activation(rows_l, rows_l, ACT.Exp).then_inc(act_step, 1)
            act.wait_ge(act_step, 5)
            act.activation(rows_l, rows_l, ACT.Ln, bias=1.0).then_inc(f_log, 1)
            act.wait_ge(conv_ready, HM)
            act.activation(sig_c, conv, ACT.Sigmoid).then_inc(conv_sig, 1)
            act.preload_act_table_set("natural_log_exp_and_others")
            act.wait_ge(vec_ready, 1)
            for n in range(4):
                act.wait_ge(qk_turned, n + 1)
                s, i = n // 2, n % 2
                act.activation(qk_t[:, s, 2 * i:2 * i + 2, :], bank[2 + n][:, :].rearrange("p (j n) -> p j n", j=2),
                               ACT.Copy, scale=qkg[:, s:s + 1]).then_inc(qk_ready, 1)
            for t in range(T):
                act.wait_ge(z_v, t + 1)
                act.activation(v_a[:, t, :], bank[t][:, :], ACT.Copy).then_inc(v_read, 1)

            def turned_p(h):
                act.wait_ge(p_turned, h + 1)
                if h >= 2:
                    act.wait_ge(o_ready, h - 1)
                act.activation(pt_a[:, h % 2, :], bank[4 + h % 2][:, 0:SW], ACT.Copy).then_inc(pt_ready, 1)

            def mixed_a(j):
                act.wait_ge(o_ready, 2 * j + 2)
                if j == 0:
                    act.wait_ge(cols_turned, 1)
                act.activation(mix_t[:, j, :], bank[2 + j % 2][:, (j // 2) * SEQ:(j // 2 + 1) * SEQ], ACT.Copy).then_inc(mix_a, 1)

            for h in range(HA + 2):
                if h < HA:
                    act.wait_ge(s_max, h + 1)
                    for t in range(T):
                        lo, hi = (0, P) if t == 0 else (P, SW)
                        act.activation(p_a[:, h % 2, lo:hi], p_a[:, h % 2, lo:hi], ACT.Exp, bias=nmx[:, h, t:t + 1],
                                       accum_out=den[:, h, t:t + 1]).then_inc(s_exp, 1)
                if 1 <= h <= HA:
                    turned_p(h - 1)
                if h in (3, 5, 7, 9):
                    mixed_a((h - 3) // 2)
                if h >= 2 and h % 2 == 0 and h <= 8:
                    n = h // 2 - 1
                    act.wait_ge(z_fill, n + 1)
                    if n < 2:
                        act.activation(vm[:, n, :, 0:DM], bank[n][:, :].rearrange("p (h n) -> p h n", h=HM),
                                       ACT.Copy).then_inc(fill_read, 1)
                    else:
                        act.activation(om[:, n - 2, :], bank[n - 2][:, :], ACT.Copy).then_inc(fill_read, 1)
                if h == 1:
                    act.wait_ge(cols_ready, 1)
                    act.activation(em[:, :, :], acol[:, 1], ACT.Exp).then_inc(em_ready, 1)
                if h == 2:
                    for m in range(HM):
                        act.wait_ge(m_arg, m + 1)
                        act.activation(e_m[:, m, :], e_m[:, m, :], ACT.Exp, scale=-1.0).then_inc(m_exp, 1)
                if h in (3, 4):
                    dst = (qm_t, km_t)[h - 3]
                    for i in range(2):
                        act.wait_ge(qkm, 2 * (h - 3) + i + 1)
                        act.activation(dst[:, 2 * i:2 * i + 2, :], bank[6 + i][:, :].rearrange("p (h n) -> p h n", h=2),
                                       ACT.Copy).then_inc(qkm_read, 1)
            for h in range(HM):
                act.wait_ge(den_read, T * HM)
                for t in range(T):
                    src = bank[6 * t + h // 2][:, (h % 2) * SEQ:(h % 2) * SEQ + DM]
                    if h + t:
                        act.wait_ge(m_ss, 2 * h + t)
                    act.activation(attn_tmp[:, 2 * BANK:2 * BANK + DM], src, ACT.Square, accum_out=ssm[:, t, h:h + 1]).then_inc(m_ss, 1)
            act.wait_ge(m_ms, 1)
            act.activation(rsm[:, :, :], ssm[:, :, :], ACT.Ln, scale=1.0 / DM, bias=eps[:, 0:1]).then_inc(act_step, 1)
            act.wait_ge(act_step, 6)
            act.activation(rsm[:, :, :], rsm[:, :, :], ACT.Exp, scale=-0.5).then_inc(m_rs, 1)
            act.wait_ge(fill_read, 4)
            act.activation(om[:, :, :], om[:, :, :], ACT.Sigmoid).then_inc(om_sig, 1)
            act.preload_act_table_set("natural_log_exp_and_others")
            for h in range(HM):
                act.wait_ge(m_turned, h + 1)
                act.activation(mix_t[:, 4 + h, :], bank[TURN[h]][:, 0:SEQ], ACT.Copy,
                               scale=vec[:, R_MH + h:R_MH + h + 1]).then_inc(mix_m, 1)
            def square_x(t, c):
                act.wait_ge(x1_ready, 2 * t + c + 1)
                act.activation(hn[:, t, c * BANK:(c + 1) * BANK], xres[:, t, c * BANK:(c + 1) * BANK], ACT.Square,
                               accum_out=ss2h[:, t, c:c + 1]).then_inc(x1_ss, 1)

            def rms_x(t):
                act.wait_ge(ss2_sum, t + 1)
                act.activation(rs2[:, t:t + 1], ss2[:, t:t + 1], ACT.Ln, scale=1.0 / D, bias=eps[:, 0:1]).then_inc(act_step, 1)
                act.wait_ge(act_step, 7 + t)
                act.activation(rs2[:, t:t + 1], rs2[:, t:t + 1], ACT.Exp, scale=-0.5).then_inc(x1_rs, 1)

            def high_part(t):
                act.wait_ge(x1_rs, t + 1)
                act.activation(parts[:, t, 0, :], xres[:, t, :], ACT.Copy, scale=rs2[:, t:t + 1]).then_inc(hi_ready, 1)

            def mid_part(t):
                act.wait_ge(rest_1, t + 1)
                if t == 1:
                    act.wait_ge(rest_half, 1)
                act.activation(parts[:, t, 1, :], hn[:, t, :], ACT.Copy).then_inc(mid_ready, 1)

            square_x(0, 0)
            square_x(0, 1)
            rms_x(0)
            for i in range(2):
                act.wait_ge(h2_turned, i + 1)
                act.activation(ht[:, 4 * i:4 * i + 4, 0:P], bank[i][:, :].rearrange("p (k n) -> p k n", k=4),
                               ACT.Copy).then_inc(turned_x0, 1)
            high_part(0)
            square_x(1, 0)
            square_x(1, 1)
            mid_part(0)
            rms_x(1)
            high_part(1)
            for t in range(T):
                act.wait_ge(top_ready, 1)
                act.activation(gate4[:, t, :], top_v[:, t, 0:TOPK], ACT.Exp, bias=nv0[:, t:t + 1],
                               accum_out=gsum[:, t:t + 1]).then_inc(top_exp, 1)
            mid_part(1)
            act.wait_ge(gate_turned, 1)
            act.activation(gate_t, bank[6][0:NE, 0:SEQ], ACT.Copy).then_inc(bank6_read, 1)

            def expert(n, u):
                act.wait_ge(slots_turned, n + 1)
                act.activation(s_sb[:, u, :], bank[6][:, 0:SEQ], ACT.Copy).then_inc(slots_ready, 1)
                act.wait_ge(gate_cut, n + 1)
                act.activation(sig_g, gate_c, ACT.Sigmoid, scale=ALPHA).then_inc(sig_ready, 1)
                act.wait_ge(act_turned, n + 1)
                act.activation(act_t, bank[6][:, :], ACT.Copy).then_inc(act_t_ready, 1)
                act.wait_ge(d_used, 4 * n + 4)
                act.wait_ge(y_spread, n + 1)
                act.activation(y_sb, bank[6][:, :], ACT.Copy).then_inc(bank6_read, 1)

            with act.Fori(0, NE // 2) as i:
                for u in range(2):
                    expert(2 * i + u, u)
            more = overflow(act)
            with act.If(more > 0):
                with act.Fori(NE // 2, ROUNDS * NE // 2) as i:
                    for u in range(2):
                        expert(2 * i + u, u)

        @block.vector
        def _(dve):
            steps = [0]

            def step(ins):
                steps[0] += 1
                ins.then_inc(dve_step, 1)

            def settle():
                dve.wait_ge(dve_step, steps[0])

            dve.memset(eps[:, :], EPS).then_inc(eps_ready, 1)
            for t in range(T):
                dve.wait_ge(x_rs, t + 1)
                dve.tensor_scalar(hn[:, t, :], xres[:, t, :], rs1[:, t:t + 1], None, ALU.mult).then_inc(x_norm, 1)
            dve.wait_ge(g1_turned, 1)
            dve.tensor_copy(vec[:, R_G1:R_G1 + KD], bank[0][:, 0:KD]).then_inc(g1_ready, 1)
            dve.wait_ge(g1_ready, 1)
            for t in range(T):
                for i in range(2):
                    dve.wait_ge(x_turned, 2 * t + i + 1)
                    dve.tensor_tensor(ht[:, 4 * i:4 * i + 4, t * P:(t + 1) * P],
                                      bank[4 + 2 * t + i][:, :].rearrange("p (k n) -> p k n", k=4),
                                      vec[:, R_G1 + 4 * i:R_G1 + 4 * i + 4].unsqueeze(2).broadcast_to([P, 4, P]),
                                      ALU.mult).then_inc(h_ready, 1)
            for s in range(2):
                for t in range(T):
                    dve.wait_ge(qk_sq, 2 * s + t + 1)
                    dve.tensor_reduce(ssqk[:, s, t, :], sq[:, t, :].rearrange("p (h n) -> p h n", h=HA), AX.X,
                                      ALU.add).then_inc(qk_ms, 1)
                if s == 0:
                    continue
                for s2 in range(2):
                    dve.wait_ge(qk_rs, s2 + 1)
                    for t in range(T):
                        dve.tensor_tensor(qk_n[:, s2, t, :].rearrange("p (h n) -> p h n", h=HA),
                                          bank[2 * s2 + t][:, :].rearrange("p (h n) -> p h n", h=HA),
                                          rsqk[:, s2, t, :].unsqueeze(2).broadcast_to([P, HA, DA]),
                                          ALU.mult).then_inc(qk_norm, 1)
            dve.wait_ge(z_if, T)
            dve.tensor_copy(if_c, bank[4][:, 0:T * 2 * HM].rearrange("p (t s h) -> p t s h", t=T, s=2)).then_inc(if_copied, 1)
            dve.wait_ge(vec_turned, 1)
            step(dve.tensor_copy(vec[:, KD:ROWS], bank[5][:, KD:ROWS]))
            settle()
            step(dve.tensor_scalar(qkg[:, 0:1], vec[:, R_QG:R_QG + 1], float(DA) ** -0.5, None, ALU.mult))
            dve.tensor_copy(qkg[:, 1:2], vec[:, R_KG:R_KG + 1]).then_inc(vec_ready, 1)
            dve.wait_ge(if_turned, 1)
            dve.wait_ge(ld_small, 16 * 2)
            dve.wait_ge(consts, 6)
            step(dve.tensor_scalar(rows_f, bank[4][0:HM, SEQ:2 * SEQ], bif[:, 1:2], None, ALU.add))
            step(dve.tensor_scalar(rows_i, bank[4][0:HM, 0:SEQ], bif[:, 0:1], None, ALU.add))
            settle()
            dve.scalar_tensor_tensor(out=rows_l, in0=rows_f, scalar=-1.0, in1=rows_f, op0=ALU.mult, op1=ALU.min).then_inc(f_neg, 1)
            dve.wait_ge(xm_read, 2)
            for j in range(TAPS):
                for h in range(HM):
                    tap = vec[:, R_CW + j * HM + h:R_CW + j * HM + h + 1]
                    if j == 0:
                        step(dve.tensor_scalar(conv[:, h, :], xm[:, h, 0:SEQ], tap, vec[:, R_CB + h:R_CB + h + 1],
                                               ALU.mult, ALU.add))
                    else:
                        ins = dve.scalar_tensor_tensor(out=conv[:, h, :], in0=xm[:, h, j:j + SEQ], scalar=tap,
                                                       in1=conv[:, h, :], op0=ALU.mult, op1=ALU.add)
                        if j < TAPS - 1:
                            step(ins)
                        else:
                            ins.then_inc(conv_ready, 1)
                if j < TAPS - 1:
                    settle()
            dve.wait_ge(f_log, 1)
            step(dve.scalar_tensor_tensor(out=rows_f, in0=rows_f, scalar=0.0, in1=rows_l, op0=ALU.min, op1=ALU.subtract))
            settle()
            step(dve.tensor_tensor_scan(rows_b, ones_r, rows_f, 0.0, ALU.mult, ALU.add))
            settle()
            step(dve.tensor_tensor(rows_i, rows_i, rows_b, ALU.subtract))
            settle()
            step(dve.tensor_tensor_scan(rows_a[:, :], ones_r, rows_i, 0.0, ALU.mult, ALU.max))
            settle()
            dve.scalar_tensor_tensor(out=rows_l, in0=rows_b, scalar=-1.0, in1=rows_a[:, :], op0=ALU.mult,
                                     op1=ALU.subtract).then_inc(rows_ready, 1)

            def softmax(h):
                dve.wait_ge(scores, h + 1)
                if h == 0:
                    dve.wait_ge(ld_bias_a, 16)
                if h >= 2:
                    dve.wait_ge(p_turned, h - 1)
                for t in range(T):
                    lo, hi = (0, P) if t == 0 else (P, SW)
                    step(dve.tensor_tensor_reduce(out=p_a[:, h % 2, lo:hi], in0=bank[4 + h % 2][:, lo:hi],
                                                  in1=bias_a[:, h, lo:hi], scale=1.0, scalar=MASKED, op0=ALU.add,
                                                  op1=ALU.max, accum_out=mx[:, h, t:t + 1]))
                settle()
                dve.tensor_scalar(nmx[:, h, :], mx[:, h, :], -1.0, None, ALU.mult).then_inc(s_max, 1)

            def normalise(h):
                dve.wait_ge(s_exp, 2 * h + 2)
                step(dve.reciprocal(rden[:, h, :], den[:, h, :]))
                settle()
                for t in range(T):
                    lo, hi = (0, P) if t == 0 else (P, SW)
                    dve.tensor_scalar(p_a[:, h % 2, lo:hi], p_a[:, h % 2, lo:hi], rden[:, h, t:t + 1], None,
                                      ALU.mult).then_inc(p_ready, 1)

            def decay(h):
                a_bc = bank[6 + h // 2][:, (h % 2) * SEQ:(h % 2 + 1) * SEQ]
                dve.tensor_scalar(e_m[:, h, 0:SEQ], a_bc, acol[:, 0, 0, h:h + 1], 0.0, ALU.subtract, ALU.max)\
                    .then_inc(m_arg1, 1)
                dve.wait_ge(m_arg1, h + 1)
                dve.tensor_scalar(e_m[:, h, SEQ:SW], a_bc[:, P:SEQ], acol[:, 0, 1, h:h + 1], 0.0,
                                  ALU.subtract, ALU.max).then_inc(m_arg, 1)

            def weighed(h):
                dve.wait_ge(m_scores, h + 1)
                dve.wait_ge(m_sel, h + 1)
                dve.scalar_tensor_tensor(out=e_m[:, h, :], in0=bank[6 + h % 2][:, 0:SW], scalar=float(DM) ** -0.5,
                                         in1=e_m[:, h, :], op0=ALU.mult, op1=ALU.mult).then_inc(m_g, 1)

            for h in range(HA + 1):
                if h < HA:
                    softmax(h)
                if h == 0:
                    dve.wait_ge(cols_turned, 1)
                    dve.tensor_copy(acol[:, :, :, :], bank[2][:, 0:2 * T * HM].rearrange("p (s t h) -> p s t h", s=2, t=T)).then_inc(cols_ready, 1)
                    dve.wait_ge(cols_ready, 1)
                    dve.wait_ge(conv_sig, 1)
                    dve.tensor_tensor(xc, conv, sig_c, ALU.mult).then_inc(xc_ready, 1)
                if h >= 1:
                    normalise(h - 1)
                if h == 1:
                    dve.wait_ge(a_spread, 1)
                    for m in range(HM):
                        decay(m)
                if h >= 5:
                    weighed(h - 5)
            for h in range(HM):
                dve.wait_ge(m_num, HM)
                for t in range(T):
                    at = (h % 2) * SEQ + DM
                    dve.tensor_copy(dm[:, t, h:h + 1], bank[6 * t + h // 2][:, at:at + 1]).then_inc(den_read, 1)
            dve.wait_ge(den_read, T * HM)
            step(dve.scalar_tensor_tensor(out=dm[:, :, :], in0=dm[:, :, :], scalar=-1.0, in1=dm[:, :, :], op0=ALU.mult, op1=ALU.max))
            settle()
            dve.wait_ge(em_ready, 1)
            step(dve.tensor_tensor(dm[:, :, :], dm[:, :, :], em[:, :, :], ALU.max))
            settle()
            step(dve.reciprocal(rm[:, :, :], dm[:, :, :]))
            settle()
            step(dve.tensor_tensor(dm[:, :, :], rm[:, :, :], rm[:, :, :], ALU.mult))
            settle()
            dve.wait_ge(m_ss, T * HM)
            dve.tensor_tensor(ssm[:, :, :], ssm[:, :, :], dm[:, :, :], ALU.mult).then_inc(m_ms, 1)
            dve.wait_ge(m_rs, 1)
            step(dve.tensor_tensor(rm[:, :, :], rm[:, :, :], rsm[:, :, :], ALU.mult))
            settle()
            dve.wait_ge(om_sig, 1)
            for h in range(HM):
                for t in range(T):
                    o = om[:, t, h * DM:(h + 1) * DM]
                    dve.scalar_tensor_tensor(out=o, in0=bank[6 * t + h // 2][:, (h % 2) * SEQ:(h % 2) * SEQ + DM],
                                             scalar=rm[:, t, h:h + 1], in1=o, op0=ALU.mult, op1=ALU.mult).then_inc(m_out, 1)
            def add_x(t, c):
                dve.wait_ge(mixed, 2 * t + c + 1)
                xs = xres[:, t, c * BANK:(c + 1) * BANK]
                dve.tensor_tensor(xs, bank[ACC[2 * t + c]][:, :], xs, ALU.add).then_inc(x1_ready, 1)

            def sum_x(t):
                dve.wait_ge(x1_ss, 2 * t + 2)
                dve.tensor_tensor(ss2[:, t:t + 1], ss2h[:, t, 0:1], ss2h[:, t, 1:2], ALU.add).then_inc(ss2_sum, 1)

            def norm_x(t):
                dve.wait_ge(x1_rs, t + 1)
                dve.tensor_scalar(hn[:, t, :], xres[:, t, :], rs2[:, t:t + 1], None, ALU.mult).then_inc(h2_norm, 1)

            def turned_1(i):
                dve.wait_ge(h2_turned, 3 + i)
                dve.tensor_copy(ht[:, 4 * i:4 * i + 4, P:SEQ], bank[6 + i][:, :].rearrange("p (k n) -> p k n", k=4))\
                    .then_inc(turned_x1, 1)

            dve.wait_ge(ld_wr, 32)
            dve.tensor_tensor(wr[:, :, :], wr[:, :, :], vec[:, R_G2:R_G2 + KD].unsqueeze(2).broadcast_to([P, KD, NE]),
                              ALU.mult).then_inc(wr_ready, 1)
            add_x(0, 0)
            add_x(0, 1)
            sum_x(0)
            norm_x(0)
            add_x(1, 0)
            turned_1(0)
            add_x(1, 1)
            sum_x(1)
            turned_1(1)
            for t in range(T):
                dve.wait_ge(logits, t + 1)
                dve.wait_ge(x1_rs, t + 1)
                step(dve.scalar_tensor_tensor(out=lg[:, t, :], in0=bank[ACC[t]][:, 0:NE], scalar=rs2[:, t:t + 1],
                                              in1=br[:, :], op0=ALU.mult, op1=ALU.add))
                if t == 0:
                    norm_x(1)
            for t in range(T):
                dve.wait_ge(dve_step, steps[0] - 1 + t)
                dve.max(top_v[:, t, :], lg[:, t, :]).then_inc(top_max, 1)
            dve.wait_ge(top_max, 1)
            step(dve.max_index(top_i[:, 0, :], top_v[:, 0, :], lg[:, 0, :]))
            dve.wait_ge(top_max, 2)
            step(dve.max_index(top_i[:, 1, :], top_v[:, 1, :], lg[:, 1, :]))
            dve.tensor_scalar(nv0[:, :], top_v[:, :, 0], -1.0, None, ALU.mult).then_inc(top_ready, 1)
            dve.wait_ge(hi_ready, T)
            dve.wait_ge(h2_norm, T)
            dve.tensor_tensor(hn[:, 1, HALF:D], hn[:, 1, HALF:D], parts[:, 1, 0, HALF:D], ALU.subtract).then_inc(rest_half, 1)
            settle()
            step(dve.tensor_copy(top_f[:, :, :], top_i[:, :, 0:TOPK]))
            settle()
            step(dve.tensor_tensor(eq, expert_no.unsqueeze(1).unsqueeze(1).broadcast_to([P, T, TOPK, NE]),
                                   top_f[:, :, :].unsqueeze(3).broadcast_to([P, T, TOPK, NE]), ALU.is_equal))
            settle()
            dve.tensor_reduce(mask[:, :, :], eq.rearrange("p t j e -> p t e j"), AX.X, ALU.add).then_inc(mask_ready, 1)
            dve.wait_ge(top_exp, T)
            step(dve.reciprocal(gsum[:, :], gsum[:, :]))
            settle()
            step(dve.tensor_tensor(gate4[:, :, :], gate4[:, :, :], gsum[:, :].unsqueeze(2).broadcast_to([P, T, TOPK]), ALU.mult))
            settle()
            step(dve.tensor_tensor(eqg, eq, gate4[:, :, :].unsqueeze(3).broadcast_to([P, T, TOPK, NE]), ALU.mult))
            settle()
            dve.tensor_reduce(gate[:, :, :], eqg.rearrange("p t j e -> p t e j"), AX.X, ALU.add).then_inc(gates_ready, 1)
            dve.wait_ge(mid_ready, T)
            dve.wait_ge(rest_half, 1)
            dve.tensor_tensor(parts[:, 1, 2, HALF:D], hn[:, 1, HALF:D], parts[:, 1, 1, HALF:D], ALU.subtract).then_inc(lo_half, 1)
            dve.wait_ge(ranks, 1)
            dve.wait_ge(mask_ready, 1)
            step(dve.scalar_tensor_tensor(out=pos[:, :, :], in0=bank[0][:, 0:T * NE].rearrange("p (t n) -> p t n", t=T),
                                          scalar=-NOWHERE, in1=mask[:, :, :], op0=ALU.add, op1=ALU.mult))
            settle()
            step(dve.tensor_scalar(pos[:, :, :], pos[:, :, :], NOWHERE, None, ALU.add))
            settle()

            def take(e):
                for t in range(T):
                    ins = dve.tensor_scalar(pick[:, t, :], slot[:, 0:CAP], pos[:, t, bass.ds(e, 1)], None, ALU.is_equal)
                ins.then_inc(picked, 1)

            take(0)
            dve.tensor_reduce(pmax[:, :], pos[:, :, :], AX.XY, ALU.max).then_inc(pmax_ready, 1)
            dve.wait_ge(gates_ready, 1)
            dve.wait_ge(pmax_turned, 1)
            step(dve.tensor_reduce(pm1[:, :], bank[0][0:1, 0:P], AX.X, ALU.max))
            settle()
            dve.tensor_scalar(flag[:, :], pm1[:, :], float(CAP), None, ALU.is_ge).then_inc(flag_ready, 1)
            dve.engine_nop().then_inc(gu_read, 1)

            def gained():
                return dve.tensor_tensor(xe_t, bank[7][:, :].rearrange("p (k n) -> p k n", k=KD),
                                         vec[:, R_G2:R_G2 + KD].unsqueeze(2).broadcast_to([P, KD, CAP]), ALU.mult)

            def expert(e, n, last=False):
                dve.wait_ge(gathered, n + 1)
                if not last:
                    take(e + 1)
                for t in range(T):
                    ins = dve.tensor_scalar(pickg[:, t, :], slot[:, :], pos[:, t, bass.ds(e, 1)],
                                            gate[:, t, bass.ds(e, 1)], ALU.is_equal, ALU.mult)
                ins.then_inc(pickg_ready, 1)
                dve.wait_ge(gu_used, KD * n + KD)
                dve.tensor_scalar(gate_c, bank[0][:, :], LIMIT, None, ALU.min).then_inc(gate_cut, 1)
                dve.tensor_scalar(up_c, bank[1][:, :], LIMIT, -LIMIT, ALU.min, ALU.max).then_inc(gu_read, 1)
                dve.wait_ge(gate_cut, n + 1)
                dve.wait_ge(gu_read, n + 2)
                dve.scalar_tensor_tensor(out=act, in0=up_c, scalar=1.0, in1=gate_c, op0=ALU.add, op1=ALU.mult).then_inc(act_half, 1)
                dve.wait_ge(act_half, n + 1)
                dve.wait_ge(sig_ready, n + 1)
                dve.tensor_tensor(act, act, sig_g, ALU.mult).then_inc(act_ready, 1)
                if not last:
                    dve.wait_ge(gathered, n + 2)
                    gained().then_inc(xe_ready, 1)

            def experts(base):
                dve.wait_ge(gathered, base + 1)
                gained().then_inc(xe_ready, 1)
                with dve.Fori(0, NE - 1) as e:
                    expert(e, base + e)
                expert(NE - 1, base + NE - 1, last=True)

            experts(0)
            more = overflow(dve)
            with dve.If(more > 0):
                with dve.Fori(1, ROUNDS) as r:
                    base = r * NE
                    dve.wait_ge(pickg_ready, base)
                    dve.wait_ge(picked, base)
                    dve.tensor_scalar(pos[:, :, :], pos[:, :, :], -float(CAP), None, ALU.add).then_inc(moved, 1)
                    dve.wait_ge(moved, r)
                    take(0)
                    experts(base)
            for t in range(T):
                for c in range(2):
                    dve.wait_ge(acc_final, 2 * t + c + 1)
                    xs = xres[:, t, c * BANK:(c + 1) * BANK]
                    dve.tensor_tensor(xs, bank[ACC[2 * t + c]][:, :], xs, ALU.add).then_inc(x_final, 1)

        @block.tensor
        def _(pe):
            def keep_warm(n):
                for _ in range(n):
                    pe.matmul(bank[1][:, 0:P], ones[:, :], ident[:, :], start=True, stop=True)

            pe.wait_ge(consts, 1)
            keep_warm(WARM[0])
            for t in range(T):
                pe.wait_ge(x_norm, t + 1)
                for i in range(2):
                    for k in range(4):
                        c = 4 * i + k
                        mm = pe.transpose(bank[4 + 2 * t + i][:, k * P:(k + 1) * P], hn[:, t, c * P:(c + 1) * P], ident[:, :])
                    mm.then_inc(x_turned, 1)
                if t == 0:
                    pe.wait_ge(ld_g1, 16)
                    pe.transpose(bank[0][:, 0:KD], vec_r[R_G1:R_G1 + KD, :], ident[0:KD, 0:KD]).then_inc(g1_turned, 1)

            keep_warm(WARM[1])

            def project(dst, b, t, ks=range(KD)):
                for k in ks:
                    mm = pe.matmul(dst[:, :], ht[:, k, t * P:(t + 1) * P], win[:, b % WINS, k, :],
                                   start=(k == 0), stop=(k == KD - 1))
                return mm

            pe.wait_ge(ld_win[0], 16)
            for t in range(T):
                pe.wait_ge(h_ready, 2 * t + 2)
                if t == 0:
                    pe.wait_ge(g1_ready, 1)
                project(bank[t], 0, t, range(4))
                if t == 0:
                    pe.wait_ge(ld_win0b, 16)
                project(bank[t], 0, t, range(4, KD)).then_inc(z_q, 1)
            pe.wait_ge(ld_win[1], 16)
            pe.wait_ge(ld_wif, 16)
            for t in range(T):
                for k in range(KD):
                    h_t = ht[:, k, t * P:(t + 1) * P]
                    gates = pe.matmul(bank[4][:, t * 2 * HM:(t + 1) * 2 * HM], h_t, wif[:, k, :],
                                      start=(k == 0), stop=(k == KD - 1))
                    mm = pe.matmul(bank[2 + t][:, :], h_t, win[:, 1, k, :], start=(k == 0), stop=(k == KD - 1))
                gates.then_inc(z_if, 1)
                mm.then_inc(z_q, 1)
            pe.wait_ge(ld_vec, 16 * 8)
            pe.transpose(bank[5][:, 0:ROWS], vec_r, ident[0:ROWS, 0:ROWS]).then_inc(vec_turned, 1)
            pe.wait_ge(ld_win[2], 16)
            for i in range(2):
                for c in range(2):
                    m = 2 * i + c
                    for k in range(KD):
                        mm = pe.matmul(bank[6 + i][:, c * SEQ:(c + 1) * SEQ], win[:, 2, k, m * P:(m + 1) * P], ht[:, k, :],
                                       start=(k == 0), stop=(k == KD - 1))
                mm.then_inc(z_xm, 1)
            pe.wait_ge(if_copied, 1)
            for s in range(2):
                for t in range(T):
                    at = s * SEQ + t * P
                    mm = pe.transpose(bank[4][0:HM, at:at + P], if_c[:, t, s, :], ident[:, :])
            mm.then_inc(if_turned, 1)
            def turn_qk(s):
                if s == 0:
                    pe.wait_ge(qk_norm, 4)
                else:
                    pe.wait_ge(f_neg, 1)
                for i in range(2):
                    for j in range(2):
                        for t in range(T):
                            c = 2 * i + j
                            mm = pe.transpose(bank[2 + 2 * s + i][:, j * SEQ + t * P:j * SEQ + (t + 1) * P],
                                              qk_n[:, s, t, c * P:(c + 1) * P], ident[:, :])
                    mm.then_inc(qk_turned, 1)

            pe.wait_ge(ld_win[3], 16)
            for t in range(T):
                turn_qk(t)
                project(bank[t], 3, t).then_inc(z_v, 1)

            def score(h):
                if h == 0:
                    pe.wait_ge(qk_ready, 4)
                if h >= 2:
                    pe.wait_ge(pt_ready, h - 1)
                r = (h % 2) * DA
                for t in range(T):
                    lo, hi = (0, P) if t == 0 else (P, SW)
                    mm = pe.matmul(bank[4 + h % 2][:, lo:hi], qk_t[r:r + DA, 0, h // 2, t * P:(t + 1) * P],
                                   qk_t[r:r + DA, 1, h // 2, 0:(t + 1) * P], start=True, stop=True)
                mm.then_inc(scores, 1)

            def turn_p(h):
                pe.wait_ge(p_ready, 2 * h + 2)
                for i in range(3):
                    mm = pe.transpose(bank[4 + h % 2][:, i * P:(i + 1) * P], p_a[:, h % 2, i * P:(i + 1) * P], ident[:, :])
                mm.then_inc(p_turned, 1)

            def attend(j):
                pe.wait_ge(pt_ready, 2 * j + 2)
                if j == 0:
                    pe.wait_ge(v_read, 2)
                    pe.wait_ge(cols_ready, 1)
                if j >= 2:
                    pe.wait_ge(mix_a, j - 1)
                dst = bank[2 + j % 2][:, (j // 2) * SEQ:(j // 2 + 1) * SEQ]
                for r in range(2):
                    at = (2 * j + r) * DA
                    pe.matmul(dst[r * DA:(r + 1) * DA, :], v_a[:, 0, at:at + DA], pt_a[:, r, 0:SEQ], start=True, stop=False,
                              skip_group_check=True)
                for r in range(2):
                    at = (2 * j + r) * DA
                    pe.matmul(dst[r * DA:(r + 1) * DA, P:SEQ], v_a[:, 1, at:at + DA], pt_a[:, r, SEQ:SW],
                              start=False, stop=True, skip_group_check=True).then_inc(o_ready, 1)

            def fill(i):
                b, t, q = 4 + i // 8, (i // 4) % 2, i % 4
                if q == 0:
                    if t == 0:
                        pe.wait_ge(ld_win[b], 16)
                    if b == 4:
                        pe.wait_ge(v_read, t + 1)
                    else:
                        pe.wait_ge(fill_read, t + 1)
                mm = project(bank[t], b, t, range(2 * q, 2 * q + 2))
                if q == 3:
                    mm.then_inc(z_fill, 1)

            def m_score(h):
                if h == 0:
                    pe.wait_ge(qkm_read, 4)
                if h >= 2:
                    pe.wait_ge(m_g, h - 1)
                s_b = bank[6 + h % 2]
                pe.matmul(s_b[:, 0:SEQ], km_t[:, h, 0:P], qm_t[:, h, :], start=True, stop=True)
                pe.matmul(s_b[:, SEQ:SW], km_t[:, h, P:SEQ], qm_t[:, h, P:SEQ], start=True, stop=True).then_inc(m_scores, 1)

            def m_sum(h):
                if h == 0:
                    pe.wait_ge(m_g, HM)
                    pe.wait_ge(fill_read, 4)
                at = (h % 2) * SEQ
                g = e_m[:, h, :]
                pe.matmul(bank[h // 2][:, at:at + DM + 1], g[:, 0:P], vm[:, 0, h, :], start=True, stop=True)
                dst = bank[6 + h // 2][:, at:at + DM + 1]
                pe.matmul(dst, g[:, P:SEQ], vm[:, 0, h, :], start=True, stop=False)
                pe.matmul(dst, g[:, SEQ:SW], vm[:, 1, h, :], start=False, stop=True).then_inc(m_num, 1)

            for h in range(HA + 2):
                if h < HA:
                    if h:
                        fill(2 * h)
                    score(h)
                    if h == 0:
                        pe.wait_ge(rows_ready, 1)
                        for s, rows in ((0, rows_i), (1, rows_l)):
                            for t in range(T):
                                at = (s * T + t) * HM
                                mm = pe.transpose(bank[2][:, at:at + HM], rows[:, t * P:(t + 1) * P], ident[0:HM, 0:HM])
                        mm.then_inc(cols_turned, 1)
                        fill(0)
                    fill(2 * h + 1)
                if h == 0:
                    pe.wait_ge(consts, 7)
                    pe.wait_ge(xm_read, 2)
                    for m in range(HM):
                        mm = pe.matmul(bank[6 + m // 2][:, (m % 2) * SEQ:(m % 2 + 1) * SEQ], sel[:, m, :], rows_a[:, :],
                                       start=True, stop=True)
                    mm.then_inc(a_spread, 1)
                if h in (3, 4):
                    if h == 3:
                        pe.wait_ge(ld_wm, 32)
                        pe.wait_ge(xc_ready, 1)
                        pe.wait_ge(m_arg, HM)
                    else:
                        pe.wait_ge(qkm_read, 2)
                    for m in range(HM):
                        mm = pe.matmul(bank[6 + m // 2][:, (m % 2) * SEQ:(m % 2 + 1) * SEQ], (wmq, wmk)[h - 3][:, m, :],
                                       xc[:, m, :], start=True, stop=True)
                        if m % 2:
                            mm.then_inc(qkm, 1)
                if h == 5:
                    m_score(0)
                    m_score(1)
                if h >= 3 and h % 2:
                    attend((h - 3) // 2)
                if 1 <= h <= HA:
                    turn_p(h - 1)
                if h in (6, 7):
                    m_score(h - 4)
            for h in range(HM):
                m_sum(h)
            def out_half(t, c, ks):
                for k in ks:
                    mm = pe.matmul(bank[ACC[2 * t + c]][:, :], mix_t[:, k, t * P:(t + 1) * P], wout[:, k, c * BANK:(c + 1) * BANK],
                                   start=(k == 0), stop=(k == KD - 1))
                return mm

            pe.wait_ge(ld_wout, 16)
            pe.wait_ge(mix_a, 4)
            pe.wait_ge(pt_ready, HA)
            for t in range(T):
                for c in range(2):
                    out_half(t, c, range(4))
            pe.wait_ge(m_out, T * HM)
            for h in range(HM):
                for t in range(T):
                    mm = pe.transpose(bank[TURN[h]][:, t * P:(t + 1) * P], om[:, t, h * DM:(h + 1) * DM], ident[:, :])
                mm.then_inc(m_turned, 1)

            def turn_x(t, i):
                pe.wait_ge(x1_ready, 2 * t + i + 1)
                for k in range(4):
                    c = 4 * i + k
                    mm = pe.transpose(bank[6 * t + i][:, k * P:(k + 1) * P], xres[:, t, c * P:(c + 1) * P], ident[:, :])
                mm.then_inc(h2_turned, 1)

            def route(t, half):
                if t and not half:
                    pe.wait_ge(wr_ready, 1)
                    pe.wait_ge(x1_ready, 2)
                pe.wait_ge((turned_x0, turned_x1)[t], half + 1)
                for k in range(4 * half, 4 * half + 4):
                    mm = pe.matmul(bank[ACC[t]][:, 0:NE], ht[:, k, t * P:(t + 1) * P], wr[:, k, :],
                                   start=(k == 0), stop=(k == KD - 1))
                if half:
                    mm.then_inc(logits, 1)

            pe.wait_ge(mix_m, HM)
            out_half(0, 0, range(4, KD)).then_inc(mixed, 1)
            out_half(0, 1, range(4, KD)).then_inc(mixed, 1)
            turn_x(0, 0)
            out_half(1, 0, range(4, KD)).then_inc(mixed, 1)
            turn_x(0, 1)
            out_half(1, 1, range(4, 6))
            turn_x(1, 0)
            out_half(1, 1, range(6, KD)).then_inc(mixed, 1)
            route(1, 0)
            turn_x(1, 1)
            route(0, 0)
            route(0, 1)
            route(1, 1)
            keep_warm(WARM[2])
            pe.wait_ge(mask_ready, 1)
            pe.matmul(bank[0][:, 0:NE], before[:, :], mask[:, 0, :], start=True, stop=True)
            pe.matmul(bank[0][:, NE:2 * NE], ones[:, :], mask[:, 0, :], start=True, stop=False)
            pe.matmul(bank[0][:, NE:2 * NE], before[:, :], mask[:, 1, :], start=False, stop=True).then_inc(ranks, 1)
            keep_warm(WARM[3])
            pe.wait_ge(gates_ready, 1)
            for t in range(T):
                mm = pe.transpose(bank[6][0:NE, t * P:(t + 1) * P], gate[:, t, :], ident[:, :])
            mm.then_inc(gate_turned, 1)
            pe.wait_ge(pmax_ready, 1)
            pe.transpose(bank[0][0:1, 0:P], pmax[:, :], ident[:, :]).then_inc(pmax_turned, 1)

            def gather(n):
                pe.wait_ge(picked, n + 1)
                for k in range(KD):
                    for t in range(T):
                        for i in range(3):
                            mm = pe.matmul(bank[7][:, k * CAP:(k + 1) * CAP], parts[:, t, i, k * P:(k + 1) * P], pick[:, t, :],
                                           start=(t + i == 0), stop=(t == T - 1 and i == 2))
                mm.then_inc(gathered, 1)

            pe.wait_ge(lo_ready, 2)
            pe.wait_ge(lo_half, 1)
            gather(0)
            def start_sum(t):
                if t == 0:
                    pe.wait_ge(ld_bdn, 16)
                    pe.wait_ge(bank6_read, 1)
                    pe.wait_ge(x1_ready, 4)
                    pe.wait_ge(top_max, T)
                for c in range(2):
                    mm = pe.matmul(bank[ACC[2 * t + c]][:, :], gate_t[:, t * P:(t + 1) * P], bdn[:, c * BANK:(c + 1) * BANK],
                                   start=True, stop=False, skip_group_check=True)
                if t == T - 1:
                    mm.then_inc(y_spread, 1)

            def spread(n, u, t, done=None):
                pe.wait_ge(bank6_read, n + 2)
                for c in range(2):
                    if done and c:
                        mm.then_inc(done, 1)
                    mm = pe.matmul(bank[ACC[2 * t + c]][:, :], s_sb[c * CAP:(c + 1) * CAP, u, t * P:(t + 1) * P],
                                   y_sb[c * CAP:(c + 1) * CAP, :], start=False, stop=False, skip_group_check=True)
                if done:
                    mm.then_inc(done, 1)
                elif t == T - 1:
                    mm.then_inc(y_spread, 1)

            def expert(n, u, times, meanwhile=None, last=False):
                pe.wait_ge(gu_read, n + 1)
                pe.wait_ge(ld_brow[u], 16 * times + 16)
                for i in range(4):
                    h, c = i // 2, i % 2
                    mm = pe.matmul(bank[h][c * CAP:(c + 1) * CAP, :], ones[32 * i:32 * i + 1, 0:CAP],
                                   brow[32 * i:32 * i + 1, u, :], start=True, stop=False, skip_group_check=True)
                mm.then_inc(brow_used, 1)
                pe.wait_ge(xe_ready, n + 1)
                for k in range(KD):
                    pe.wait_ge(ld_gu[u * KD + k], 16 * times + 16)
                    for h in range(2):
                        for c in range(2):
                            at = h * FF + c * BANK
                            mm = pe.matmul(bank[h][c * CAP:(c + 1) * CAP, :], xe_t[:, k, :], gu[:, u, k, at:at + BANK],
                                           start=False, stop=(k == KD - 1), skip_group_check=True)
                    mm.then_inc(gu_used, 1)
                pe.wait_ge(pickg_ready, n + 1)
                pe.wait_ge(bank6_read, n + 1)
                for t in range(T):
                    mm = pe.transpose(bank[6][:, t * P:(t + 1) * P], pickg[:, t, :], ident[:, :])
                mm.then_inc(slots_turned, 1)
                if not last:
                    gather(n + 1)
                if meanwhile:
                    meanwhile(0)
                else:
                    spread(n - 1, 1 - u, 0)
                pe.wait_ge(act_ready, n + 1)
                pe.wait_ge(slots_ready, n + 1)
                for k in range(4):
                    mm = pe.transpose(bank[6][:, k * P:(k + 1) * P], act[:, k * P:(k + 1) * P], ident[:, :])
                mm.then_inc(act_turned, 1)
                if meanwhile:
                    meanwhile(1)
                else:
                    spread(n - 1, 1 - u, 1)
                pe.wait_ge(act_t_ready, n + 1)
                for k in range(KD):
                    if k % 2 == 0:
                        pe.wait_ge(ld_d[k // 2], 16 * n + 16)
                    at = (k % 4) * P + (k // 4) * CAP
                    for c in range(2):
                        mm = pe.matmul(bank[6][c * CAP:(c + 1) * CAP, :], act_t[:, at:at + CAP], dn[:, k, c * BANK:(c + 1) * BANK],
                                       start=(k == 0), stop=(k == KD - 1), skip_group_check=True)
                    if k % 2:
                        mm.then_inc(d_used, 1)

            def experts(r, meanwhile=None):
                n, times = r * NE, r * (NE // 2)
                expert(n, 0, times, meanwhile)
                with pe.Fori(0, NE // 2 - 1) as i:
                    expert(n + 2 * i + 1, 1, times + i)
                    expert(n + 2 * i + 2, 0, times + i + 1)
                expert(n + NE - 1, 1, times + NE // 2 - 1, last=True)

            experts(0, start_sum)
            more = overflow(pe)
            with pe.If(more > 0):
                with pe.Fori(1, ROUNDS) as r:
                    gather(r * NE)
                    experts(r)
                pe.wait_ge(bank6_read, ROUNDS * NE + 1)
            for t in range(T):
                spread(NE - 1, 1, t, acc_final)


_INS = ['x', 'norm1_g', 'w_in', 'q_norm_g', 'k_norm_g', 'conv_w', 'conv_b', 'w_mq', 'w_mk', 'b_igate', 'b_fgate',
        'mh_norm_g', 'w_out', 'norm2_g', 'w_router', 'b_router', 'w_gate_up', 'b_gate_up', 'w_down', 'b_down']


def kernel(**inputs):
    import concourse.bacc as _bacc
    from concourse.bass_utils import run_bass_kernel_spmd as _run

    nc = _bacc.Bacc("TRN2", target_bir_lowering=False, num_devices=1, dynamic_dma_scratch_size=1024)
    arrays, args = {}, []
    given = [(name, np.ascontiguousarray(inputs[name])) for name in _INS] + [("attn_bias", attention_bias())]
    for name, a in given:
        arrays[f"in_{name}"] = a
        args.append(nc.dram_tensor(f"in_{name}", a.shape, mybir.dt.from_np(a.dtype), kind="ExternalInput").ap())
    args.append(nc.dram_tensor("out", (1, SEQ, D), F32, kind="ExternalOutput").ap())
    layer_kernel(nc, *args)
    r = _run(nc, [arrays], core_ids=[0])
    return r.results[0]["out"]
```
